# Optimizing a Trainium2 kernel written in Bass

```python
import math
import jax, jax.numpy as jnp
from jax import lax
import numpy as np

D_MODEL = 2048
BATCH = 1
SEQ = 256
DEPTH = 2

CHUNK = 64
Q_BLOCK = 128
N_A = DEPTH // 2
N_B = DEPTH - N_A
RWKV_HEAD = 64
RWKV_HEADS = D_MODEL // RWKV_HEAD
DECAY_LORA = max(32, int(round(1.8 * D_MODEL ** 0.5 / 32)) * 32)
AAA_LORA = max(32, int(round(1.8 * D_MODEL ** 0.5 / 32)) * 32)
GN_EPS = 64e-5
DIFF_HEADS = D_MODEL // 256
DIFF_HEAD_DIM = D_MODEL // DIFF_HEADS // 2
SUBLN_EPS = 1e-5
DEEPNORM_ALPHA = (2.0 * DEPTH) ** 0.25
DEEPNORM_BETA = (8.0 * DEPTH) ** -0.25
LN_EPS = 1e-5


def _layernorm(x, g, b):
    xf = x.astype(jnp.float32)
    mu = jnp.mean(xf, -1, keepdims=True)
    xc = xf - mu
    var = jnp.mean(xc * xc, -1, keepdims=True)
    return (xc * lax.rsqrt(var + LN_EPS) * g + b).astype(x.dtype)

def _wkv7_scan(r, w, k, v, kk, a):
    B, T, H, N = r.shape

    def step(S, inp):
        r_t, w_t, k_t, v_t, kk_t, a_t = inp
        sa = jnp.einsum('bhvk,bhk->bhv', S, kk_t)
        S = (S * w_t[:, :, None, :]
             - sa[..., None] * (kk_t * a_t)[:, :, None, :]
             + v_t[..., None] * k_t[:, :, None, :])
        y = jnp.einsum('bhvk,bhk->bhv', S, r_t)
        return S, y

    xs = tuple(jnp.moveaxis(t.astype(jnp.float32), 1, 0) for t in (r, w, k, v, kk, a))
    S0 = jnp.zeros((B, H, N, N), jnp.float32)
    _, ys = lax.scan(step, S0, xs)
    return jnp.moveaxis(ys, 0, 1)

def _rwkv7_mixer(x, mu_proj, mu_lora, w_in, w0, w1, w2, a0, a1, a2,
                 k_k, k_a, r_k, gn_g, gn_b, w_out):
    B, T, C = x.shape
    H, N = RWKV_HEADS, RWKV_HEAD
    xx = jnp.pad(x, ((0, 0), (1, 0), (0, 0)))[:, :-1] - x
    xs = x[None] + xx[None] * mu_proj[:, None, None, :]
    proj = jnp.einsum('sbtd,sde->sbte', xs, w_in)
    r, k, v, g = proj[0], proj[1], proj[2], proj[3]
    xw = x + xx * mu_lora[0]
    xa = x + xx * mu_lora[1]
    w_log = -jax.nn.softplus(-(w0 + jnp.tanh(xw @ w1) @ w2)) - 0.5
    decay = jnp.exp(-jnp.exp(w_log.astype(jnp.float32)))
    a = jax.nn.sigmoid(a0 + (xa @ a1) @ a2)
    kk = (k * k_k).reshape(B, T, H, N).astype(jnp.float32)
    kk = kk / jnp.maximum(jnp.sqrt(jnp.sum(kk * kk, -1, keepdims=True)), 1e-12)
    k = k * (1.0 + (a - 1.0) * k_a)
    rh = r.reshape(B, T, H, N)
    kh = k.reshape(B, T, H, N)
    vh = v.reshape(B, T, H, N)
    y = _wkv7_scan(rh, decay.reshape(B, T, H, N), kh, vh, kk, a.reshape(B, T, H, N))
    mu = jnp.mean(y, -1, keepdims=True)
    yc = y - mu
    var = jnp.mean(yc * yc, -1, keepdims=True)
    y = (yc * lax.rsqrt(var + GN_EPS)).reshape(B, T, C) * gn_g + gn_b
    bonus = jnp.sum(rh.astype(jnp.float32) * kh.astype(jnp.float32) * r_k, -1, keepdims=True) * vh.astype(jnp.float32)
    y = (y + bonus.reshape(B, T, C)).astype(x.dtype)
    return (y * jax.nn.silu(g)) @ w_out

def _diff_attention(q, k, v, lam):
    B, H2, T, dh = q.shape
    H = H2 // 2
    slopes = jnp.repeat(2.0 ** (-(8.0 / H) * jnp.arange(1, H + 1, dtype=jnp.float32)), 2)
    scale = dh ** -0.5
    outs = []
    for i in range(T // Q_BLOCK):
        q0, q1 = i * Q_BLOCK, (i + 1) * Q_BLOCK
        qb = q[:, :, q0:q1]
        kb = k[:, :, :q1]
        vb = v[:, :, :q1]
        s = jnp.einsum('bmqd,bmkd->bmqk', qb, kb).astype(jnp.float32) * scale
        tq = jnp.arange(q0, q1)
        tk = jnp.arange(q1)
        dist = jnp.abs(tq[:, None] - tk[None, :]).astype(jnp.float32)
        allowed = (tk[None, :] // CHUNK) <= (tq[:, None] // CHUNK)
        s = jnp.where(allowed, s - slopes[:, None, None] * dist, -jnp.inf)
        p = jax.nn.softmax(s, axis=-1).reshape(B, H, 2, Q_BLOCK, q1)
        attn = p[:, :, 0] - lam * p[:, :, 1]
        outs.append(jnp.einsum('bhqk,bhkd->bhqd', attn.astype(vb.dtype), vb))
    return jnp.concatenate(outs, axis=2)

def _diff_mixer(x, k_sh, v_sh, w_qg, lam_p, subln_g, w_out, layer):
    B, T, C = x.shape
    H, dh = DIFF_HEADS, DIFF_HEAD_DIM
    qg = x @ w_qg
    q = qg[..., :C].reshape(B, T, 2 * H, dh).transpose(0, 2, 1, 3)
    g = qg[..., C:]
    lam_init = 0.8 - 0.6 * math.exp(-0.3 * layer)
    lam_f = lam_p.astype(jnp.float32)
    lam = (jnp.exp(jnp.sum(lam_f[0] * lam_f[1])) - jnp.exp(jnp.sum(lam_f[2] * lam_f[3])) + lam_init)
    o = _diff_attention(q, k_sh, v_sh, lam).astype(jnp.float32)
    o = o * lax.rsqrt(jnp.mean(o * o, -1, keepdims=True) + SUBLN_EPS) * subln_g * (1.0 - lam_init)
    o = o.transpose(0, 2, 1, 3).reshape(B, T, C).astype(x.dtype)
    return (o * jax.nn.silu(g)) @ w_out

def first_inputs(seed: int = 0) -> dict:
    key = jax.random.key(seed)
    ks = jax.random.split(key, 32)
    C, H, N, dh = D_MODEL, RWKV_HEADS, RWKV_HEAD, DIFF_HEAD_DIM
    f32 = jnp.float32
    nrm = lambda k, shape, s: jax.random.normal(k, shape, f32) * s
    return {
        "x": jax.random.normal(ks[0], (BATCH, SEQ, C), f32),
        "a_mu_proj": jax.random.uniform(ks[1], (N_A, 4, C), f32),
        "a_mu_lora": jax.random.uniform(ks[2], (N_A, 2, C), f32),
        "a_w_in": nrm(ks[3], (N_A, 4, C, C), C ** -0.5),
        "a_w0": jax.random.uniform(ks[4], (N_A, C), f32, -6.0, 0.0),
        "a_w1": nrm(ks[5], (N_A, C, DECAY_LORA), C ** -0.5),
        "a_w2": nrm(ks[6], (N_A, DECAY_LORA, C), 0.1 * DECAY_LORA ** -0.5),
        "a_a0": nrm(ks[7], (N_A, C), 0.5),
        "a_a1": nrm(ks[8], (N_A, C, AAA_LORA), C ** -0.5),
        "a_a2": nrm(ks[9], (N_A, AAA_LORA, C), 0.3 * AAA_LORA ** -0.5),
        "a_k_k": 0.85 + nrm(ks[10], (N_A, C), 0.05),
        "a_k_a": 1.0 + nrm(ks[11], (N_A, C), 0.05),
        "a_r_k": -0.04 + nrm(ks[12], (N_A, H, N), 0.1),
        "a_gn_g": 1.0 + nrm(ks[13], (N_A, C), 0.05),
        "a_gn_b": nrm(ks[14], (N_A, C), 0.01),
        "a_w_out": nrm(ks[15], (N_A, C, C), C ** -0.5 * DEEPNORM_BETA),
        "w_k_shared": nrm(ks[16], (C, C), C ** -0.5),
        "w_v_shared": nrm(ks[17], (C, C), C ** -0.5),
        "b_w_qg": nrm(ks[18], (N_B, C, 2 * C), C ** -0.5),
        "b_lambda": nrm(ks[19], (N_B, 4, dh), 0.1),
        "b_subln_g": 1.0 + nrm(ks[20], (N_B, 2 * dh), 0.05),
        "b_w_out": nrm(ks[21], (N_B, C, C), C ** -0.5 * DEEPNORM_BETA),
        "ln_g": 1.0 + nrm(ks[22], (DEPTH, C), 0.05),
        "ln_b": nrm(ks[23], (DEPTH, C), 0.01),
    }

def first_block(x, a_mu_proj, a_mu_lora, a_w_in, a_w0, a_w1, a_w2, a_a0, a_a1, a_a2,
              a_k_k, a_k_a, a_r_k, a_gn_g, a_gn_b, a_w_out, w_k_shared, w_v_shared,
              b_w_qg, b_lambda, b_subln_g, b_w_out, ln_g, ln_b):
    B, T, C = x.shape
    k_sh = None
    v_sh = None
    for layer in range(DEPTH):
        if layer < N_A:
            i = layer
            y = _rwkv7_mixer(x, a_mu_proj[i], a_mu_lora[i], a_w_in[i], a_w0[i], a_w1[i], a_w2[i],
                             a_a0[i], a_a1[i], a_a2[i], a_k_k[i], a_k_a[i], a_r_k[i],
                             a_gn_g[i], a_gn_b[i], a_w_out[i])
        else:
            j = layer - N_A
            y = _diff_mixer(x, k_sh, v_sh, b_w_qg[j], b_lambda[j], b_subln_g[j], b_w_out[j], layer)
        x = _layernorm(DEEPNORM_ALPHA * x + y, ln_g[layer], ln_b[layer])
        if layer == N_A - 1:
            k_sh = (x @ w_k_shared).reshape(B, T, 2 * DIFF_HEADS, DIFF_HEAD_DIM).transpose(0, 2, 1, 3)
            v_sh = (x @ w_v_shared).reshape(B, T, DIFF_HEADS, 2 * DIFF_HEAD_DIM).transpose(0, 2, 1, 3)
    return x


DEPTH_2 = 1

N_META = 16
POOL_WIDTH = D_MODEL // 2
POOL_WINDOWS = (2, 4, 8, 16)
N_POOL_GROUPS = len(POOL_WINDOWS)
POOL_GROUP_DIM = POOL_WIDTH // N_POOL_GROUPS
CONV_WIDTH = D_MODEL // 2
CONV_KERNEL = 31
D_FF = 4 * D_MODEL
IN_COLS = POOL_WIDTH + 2 * CONV_WIDTH + 2 * D_MODEL
RMS_EPS = 1e-6


def rms_norm(x, g):
    xf = x.astype(jnp.float32)
    y = xf * lax.rsqrt(jnp.mean(xf * xf, axis=-1, keepdims=True) + RMS_EPS)
    return (y * g.astype(jnp.float32)).astype(x.dtype)

def layer_norm(x, g, b):
    xf = x.astype(jnp.float32)
    mu = jnp.mean(xf, axis=-1, keepdims=True)
    var = jnp.mean(jnp.square(xf - mu), axis=-1, keepdims=True)
    y = (xf - mu) * lax.rsqrt(var + LN_EPS)
    return (y * g.astype(jnp.float32) + b.astype(jnp.float32)).astype(x.dtype)

def causal_multiscale_pool(z, w_grp, scale):
    B, L, _ = z.shape
    zf = z.astype(jnp.float32).reshape(B, L, N_POOL_GROUPS, POOL_GROUP_DIM)
    cs = jnp.cumsum(zf, axis=1)
    pos = jnp.arange(L)
    means = []
    for g, w in enumerate(POOL_WINDOWS):
        csg = cs[:, :, g]
        lag = jnp.pad(csg[:, : L - w], ((0, 0), (w, 0), (0, 0)))
        cnt = jnp.minimum(pos + 1, w).astype(jnp.float32)[None, :, None]
        means.append((csg - lag) / cnt)
    pooled = jnp.stack(means, axis=2)
    d = (pooled - zf).astype(z.dtype)
    y = jnp.einsum('blgc,gcd->blgd', d, w_grp).reshape(B, L, POOL_WIDTH)
    return y * scale

def conformer_conv(v, gate, w_dw, b_dw, ln_g, ln_b):
    a = v * jax.nn.sigmoid(gate)
    c = lax.conv_general_dilated(
        a, w_dw[:, None, :], window_strides=(1,),
        padding=[(CONV_KERNEL - 1, 0)],
        dimension_numbers=('NWC', 'WIO', 'NWC'),
        feature_group_count=CONV_WIDTH) + b_dw
    return jax.nn.silu(layer_norm(c, ln_g, ln_b))

def second_inputs(seed: int = 0) -> dict:
    key = jax.random.key(seed)
    ks = jax.random.split(key, 24)
    f32 = jnp.float32
    n = lambda k, shape, s: jax.random.normal(k, shape, f32) * s
    gain = lambda k, shape: 1.0 + 0.05 * jax.random.normal(k, shape, f32)
    return {
        "x": jax.random.normal(ks[0], (BATCH, SEQ, D_MODEL), f32),
        "meta": n(ks[1], (N_META, D_MODEL), 1.0),
        "g_pre_mix": gain(ks[2], (DEPTH_2, D_MODEL)),
        "w_in": n(ks[3], (DEPTH_2, D_MODEL, IN_COLS), D_MODEL ** -0.5),
        "w_pool_grp": n(ks[4], (DEPTH_2, N_POOL_GROUPS, POOL_GROUP_DIM, POOL_GROUP_DIM), POOL_GROUP_DIM ** -0.5),
        "pool_scale": gain(ks[5], (DEPTH_2, POOL_WIDTH)),
        "w_pool_out": n(ks[6], (DEPTH_2, POOL_WIDTH, D_MODEL), POOL_WIDTH ** -0.5),
        "w_dw": n(ks[7], (DEPTH_2, CONV_KERNEL, CONV_WIDTH), CONV_KERNEL ** -0.5),
        "b_dw": n(ks[8], (DEPTH_2, CONV_WIDTH), 0.02),
        "conv_ln_g": gain(ks[9], (DEPTH_2, CONV_WIDTH)),
        "conv_ln_b": n(ks[10], (DEPTH_2, CONV_WIDTH), 0.02),
        "w_conv_out": n(ks[11], (DEPTH_2, CONV_WIDTH, D_MODEL), CONV_WIDTH ** -0.5),
        "w_o": n(ks[12], (DEPTH_2, D_MODEL, D_MODEL), D_MODEL ** -0.5),
        "g_post_mix": gain(ks[13], (DEPTH_2, D_MODEL)),
        "g_pre_mlp": gain(ks[14], (DEPTH_2, D_MODEL)),
        "w_up": n(ks[15], (DEPTH_2, D_MODEL, D_FF), D_MODEL ** -0.5),
        "w_down": n(ks[16], (DEPTH_2, D_FF, D_MODEL), D_FF ** -0.5),
        "g_post_mlp": gain(ks[17], (DEPTH_2, D_MODEL)),
    }

def second_block(x, meta, g_pre_mix, w_in, w_pool_grp, pool_scale, w_pool_out,
              w_dw, b_dw, conv_ln_g, conv_ln_b, w_conv_out, w_o, g_post_mix,
              g_pre_mlp, w_up, w_down, g_post_mlp):
    B = x.shape[0]
    meta_b = jnp.broadcast_to(meta[None].astype(x.dtype), (B, N_META, D_MODEL))
    h = jnp.concatenate([meta_b, x], axis=1)
    splits = np.cumsum([POOL_WIDTH, CONV_WIDTH, CONV_WIDTH, D_MODEL]).tolist()
    for l in range(DEPTH_2):
        u = rms_norm(h, g_pre_mix[l])
        proj = u @ w_in[l]
        z_pool, v_conv, g_conv, gate_a, gate_b = jnp.split(proj, splits, axis=-1)
        y_a = causal_multiscale_pool(z_pool, w_pool_grp[l], pool_scale[l]) @ w_pool_out[l]
        y_b = conformer_conv(v_conv, g_conv, w_dw[l], b_dw[l],
                             conv_ln_g[l], conv_ln_b[l]) @ w_conv_out[l]
        m = jax.nn.sigmoid(gate_a) * y_a + jax.nn.sigmoid(gate_b) * y_b
        h = h + rms_norm(m @ w_o[l], g_post_mix[l])
        u = rms_norm(h, g_pre_mlp[l])
        f = jnp.square(jax.nn.relu(u @ w_up[l])) @ w_down[l]
        h = h + rms_norm(f, g_post_mlp[l])
    return h[:, N_META:]


def setup_inputs(seed=0):
    out = dict(first_inputs(seed))
    for name, value in second_inputs(seed + 1).items():
        if name != "x":
            out[name + "_2"] = value
    return out


def reference(
    x, a_mu_proj, a_mu_lora, a_w_in, a_w0, a_w1, a_w2, a_a0, a_a1, a_a2, a_k_k, a_k_a, a_r_k,
    a_gn_g, a_gn_b, a_w_out, w_k_shared, w_v_shared, b_w_qg, b_lambda, b_subln_g, b_w_out, ln_g,
    ln_b, meta_2, g_pre_mix_2, w_in_2, w_pool_grp_2, pool_scale_2, w_pool_out_2, w_dw_2, b_dw_2,
    conv_ln_g_2, conv_ln_b_2, w_conv_out_2, w_o_2, g_post_mix_2, g_pre_mlp_2, w_up_2, w_down_2,
    g_post_mlp_2,
):
    x = first_block(
        x, a_mu_proj, a_mu_lora, a_w_in, a_w0, a_w1, a_w2, a_a0, a_a1, a_a2, a_k_k, a_k_a,
        a_r_k, a_gn_g, a_gn_b, a_w_out, w_k_shared, w_v_shared, b_w_qg, b_lambda, b_subln_g,
        b_w_out, ln_g, ln_b,
    )
    return second_block(
        x, meta_2, g_pre_mix_2, w_in_2, w_pool_grp_2, pool_scale_2, w_pool_out_2, w_dw_2,
        b_dw_2, conv_ln_g_2, conv_ln_b_2, w_conv_out_2, w_o_2, g_post_mix_2, g_pre_mlp_2,
        w_up_2, w_down_2, g_post_mlp_2,
    )


_drawn_inputs = setup_inputs


def setup_inputs(seed=0):
    import zlib

    import numpy as np

    out = dict(_drawn_inputs(seed))
    spreads = {}
    factors = {'a_mu_lora': 5.28,
     'a_w1': 8.0,
     'a_w2': 8.0,
     'a_k_k': 7.893,
     'a_k_a': 5.662,
     'a_gn_g': 5.921,
     'a_gn_b': 22.965,
     'b_lambda': 8.0,
     'b_subln_g': 7.82,
     'ln_b': 3.906,
     'b_dw_2': 3.358,
     'conv_ln_b_2': 6.52}
    for name, (base, spread) in spreads.items():
        noise = np.random.default_rng([zlib.crc32(name.encode()), seed]).standard_normal(out[name].shape)
        drawn = base * np.exp(spread * noise) if base else spread * noise
        out[name] = __import__('jax').numpy.asarray(drawn.astype(out[name].dtype))
    for name, factor in factors.items():
        out[name] = (out[name] * factor).astype(out[name].dtype)
    return out
```

```python
from contextlib import ExitStack, contextmanager

import numpy as np

import concourse.bass as bass
from concourse import mybir

F32 = mybir.dt.float32
F32R = mybir.dt.float32r
ALU = mybir.AluOpType
ACT = mybir.ActivationFunctionType
AX = mybir.AxisListType

P = 128
T = 256
C = 2048
KT = C // P
HEADS, N = 32, 64
CH = 64
LORA = 96
META = 16
TM = T + META
FF = 4 * C
RING = 4
SLABS = 8
GW = 512
DECAY = float(np.exp(-0.5))
ALPHA = (2.0 * 2) ** 0.25
GN_EPS, LN_EPS, SUBLN_EPS, RMS_EPS = 64e-5, 1e-5, 1e-5, 1e-6
DH = 128
AH = 8
LAM_INIT = 0.8 - 0.6 * float(np.exp(-0.3))
TAPS = 31
PER = 3
WINDOWS = (2, 4, 8, 16)

CONST = {}


def constants():
    p = np.arange(P)
    s, t = (p % CH)[:, None], np.arange(CH)[None, :]
    parts = {"ident": np.eye(P), "ident64": (s == t) * 1.0}
    parts["heads"] = (p[:, None] // N == p[None, :] // N) * 1.0
    parts["sel2"] = (p[:, None] // N == np.arange(2)[None, :]) * 1.0
    parts["causal"] = np.concatenate([(s < t), (s <= t)], 1) * 1.0
    for lv in range(6):
        m = 1 << lv
        parts[f"level{lv}"] = ((s // (2 * m) == t // (2 * m)) & ((t // m) % 2 == 1) & ((s // m) % 2 == 0)) * 1.0
    parts["restart"] = np.tile((np.arange(T)[None, :] % CH != 0) * 1.0, (P, 1))
    parts["ones"] = np.ones((P, P))
    at = 0
    for name, a in parts.items():
        CONST[name] = (at, a.shape[1])
        at += a.shape[1]
    return np.ascontiguousarray(np.concatenate(list(parts.values()), 1).astype(np.float32))


CONSTANTS = constants()


def distances():
    q, k = np.arange(2)[None, :, None] * P + np.arange(P)[:, None, None], np.arange(T)[None, None, :]
    return np.where(k // CH <= q // CH, -np.abs(q - k) * 1.0, -1e30).astype(np.float32)

VECTORS = {"mu_r": 16, "mu_k": 16, "mu_v": 16, "mu_g": 16, "mu_w": 16, "mu_a": 16, "w0": 16, "a0": 16, "k_k": 16,
           "k_a": 16, "r_k": 16, "gn_g": 16, "gn_b": 16, "subln": 2, "g_pre_mix": 16, "g_pre_mlp": 16,
           "pool_scale": 8, "b_dw": 8, "conv_g": 8, "conv_b": 8, "w_dw": 8 * TAPS}
VEC = {}
_at = 0
for _name, _n in VECTORS.items():
    VEC[_name] = (_at, _n)
    _at += _n
NVEC = _at


class Signal:

    def __init__(self, sem):
        self.sem, self.base, self.off = sem, 0, 0

    @property
    def n(self):
        return self.base + self.off


class Steps:

    def __init__(self, eng, sem):
        self.eng, self.own, self.past = eng, Signal(sem), []

    def do(self, ins, sig=None):
        sig = sig or self.own
        ins.then_inc(sig.sem, 1)
        sig.off += 1
        self.past.append((sig.sem, sig.n))

    def prev(self, back=1):
        self.eng.wait_ge(*self.past[-back])

    @contextmanager
    def loop(self, trips, each):
        start = {s: s.n for s in each}
        self.past = [(self.own.sem, self.own.n)]
        with self.eng.Fori(0, trips) as i:
            for s, k in each.items():
                s.base, s.off = start[s] + i * k, 0
            self.past = [(self.own.sem, self.own.n)]
            yield i
            for s, k in each.items():
                assert s.off == k, (s.sem, s.off, k)
        for s, k in each.items():
            s.base, s.off = start[s] + trips * k, 0
        self.past = [(self.own.sem, self.own.n)]


def program(nc, ins, out, dbg=None, upto=99):
    ctx = ExitStack()
    with ctx:
        def sb(name, shape, dt=F32):
            return ctx.enter_context(nc.sbuf_tensor(name, shape, dt))

        def sem(name):
            return ctx.enter_context(nc.semaphore(name))

        wraw = sb("wraw", [P, RING, 2, GW])
        whi = sb("whi", [P, RING, 2, GW], F32R)
        wlo = sb("wlo", [P, RING, 2, GW], F32R)
        cst = sb("cst", [P, CONSTANTS.shape[1]])
        vec = sb("vec", [P, NVEC])
        M = sb("M", [P, KT, N])
        gC = sb("gC", [P, KT, T // CH])
        small = sb("small", [P, 256])
        with nc.sbuf_tensor("act_hi", [P, KT, TM], F32R) as ahi, nc.sbuf_tensor("act_lo", [P, KT, TM], F32R) as alo:
            pass
        work = sb("work", [P, 2 * KT * TM])
        with nc.sbuf_tensor("regions_r", [P, 7, 4096], F32R) as RR:
            pass
        R = sb("regions", [P, 7, 4096])
        ps = ctx.enter_context(nc.psum_tensor("ps", [P, 8, 512], F32))
        bonus_dram = nc.dram_tensor("bonus_scratch", [P, KT, T], F32)
        gate_dram = nc.dram_tensor("gate_scratch", [P, KT, T], F32)

        def cs(name):
            return cst[:, CONST[name][0]:CONST[name][0] + CONST[name][1]]

        def ve(name, j=None):
            a, n = VEC[name]
            return vec[:, a:a + n] if j is None else vec[:, a + j:a + j + 1]

        def bank(b, n=1):
            return ps[:, b, :] if n == 1 else ps[:, b:b + n, :].rearrange("p b n -> p (b n)")

        raw_loaded = [sem(f"raw_loaded{q}") for q in range(RING)]
        hi_ready, lo_ready, slab_used = sem("hi_ready"), sem("lo_ready"), sem("slab_used")
        names = """params_loaded x_loaded lora_loaded
            xa_ready xa_hi xa_tmp xs_ready lora_z lora_h lora_zz lora_s1 lora_s2 dec_done
            acc_free_act acc_free_dve act_step dve_step pool_step pe_step
            kk_copied kk_ready gi_ready ss_done sq_ready rn_ready rnx_ready rnx_bc rn_used rk_ready rk_bc vt_mm v_ready bvs_ready bv_stored0 bv_stored1 bv_loaded
            silu_ready gate_stored0 gate_stored1 gate_loaded
            am_mm am_ready tok_mm tok_ready lv_b lv_y lv_ysb lv_z lv_t prep_done bon_ready gn_var gn_std
            w_mm w_sb u_mm u_sb y_mm y_sb m_mm m_sb gn_ready yn_ready zt_mm z1_ready z_ready z_f z_hi
            row_loaded ln_ready ln_t_mm out_stored
            x_reloaded ln_std ln_var turn_src turn_mm turn_hi
            acc_act acc_dve extra_loaded meta_loaded post_loaded grp_loaded last_loaded lam_ready lam_exp lam_done sc_mm sc_read sc_ready e_ready at_ready att_mm attT_ready o_mm
            ostd_ready on_ready ot_mm ot_ready zb_ready zb_hi x2_cols ssq ssum sstd
            meta_ssq meta_src meta_mm meta_f meta_hi meta_ready cv_sig cv_a pool_d pool_mm pool_y p_hi conv_c cs_mm xc_ready sqc_ready cv_mm cvar cstd
            cn_ready conv_y c_hi m_ready m_hi f_relu f_sq f_hi f_ready y2_cols out_cols""".split()
        S = {n: sem(n) for n in names}
        block = ctx.enter_context(nc.Block())

        G0 = {}
        g_at = 0
        for name, n in (("g", 4), ("k", 4), ("r", 4), ("v", 4), ("wout", 4), ("ks", 4), ("vs", 4), ("q", 4), ("gb", 4), ("bout", 4),
                        ("cv", 4), ("pool", 2), ("gates", 8), ("pc", 4), ("wo", 4), ("up0", 8), ("down0", 8), ("up1", 8),
                        ("down1", 8)):
            G0[name] = g_at
            g_at += n
        GROUPS = g_at

        XS = {"g": 0, "k": 16, "r": 32, "v": 48, "z": 64, "ln0": 72, "z2": 76, "u1": 80, "pc": 84, "m": 88, "u2": 92}
        ACC_ACT = {"ks": 4, "vs": 8, "q": 12, "gb": 16, "cv": 20, "pool": 24, "gates": 26, "wo": 34, "up0": 38, "up1": 46}
        ACC_DVE = {"wout": 0, "bout": 4, "pc": 8, "down0": 12, "down1": 16}

        W_in = ins["a_w_in"]
        xT_ap = ins["xT"]

        xT = R[:, 0, :].rearrange("p (k t) -> p k t", k=KT)
        xx = R[:, 1, :].rearrange("p (k t) -> p k t", k=KT)
        KR = R[:, 2:4, :].rearrange("p a n -> p (a n)").rearrange("p (j a t) -> p j a t", j=KT, a=2)
        Bc = R[:, 4, :].rearrange("p (k t) -> p k t", k=KT)
        Kc = R[:, 5, :].rearrange("p (k t) -> p k t", k=KT)
        V = R[:, 6, :].rearrange("p (c j n) -> p c j n", c=4, j=KT)
        vtmp = [R[:, 1, 1024 * i:1024 * (i + 1)] for i in range(4)]
        tmpA = [R[:, 6, 1024 * i:1024 * (i + 1)] for i in range(4)]
        w1s = R[:, 5, 0:2 * KT * LORA].rearrange("p (a k n) -> p a k n", a=2, k=KT)
        w2s = R[:, 6, :].rearrange("p (a n) -> p a n", a=2)
        xa = [work[:, i * T:(i + 1) * T] for i in range(4)]
        hw = [work[:, 2048 + i * T:2048 + (i + 1) * T] for i in range(2)]

        mv = small[:, 240:244].rearrange("p (b a) -> p b a", b=2)
        H = R[:, 4, :].rearrange("p (b n) -> p b n", b=2)
        xre = R[:, 5, :].rearrange("p (b n) -> p b n", b=2)
        gT = R[:, 2, :].rearrange("p (k t) -> p k t", k=KT)
        rows = R[:, 6, :].rearrange("p (a n) -> p a n", a=2)
        bvT = R[:, 3, :].rearrange("p (k t) -> p k t", k=KT)
        zt = [R[:, 0, 512 * i:512 * (i + 1)] for i in range(4)]
        def wk(at, n):
            return work[:, at:at + n]
        AM = R[:, 0, :].rearrange("p (j a t) -> p j a t", j=KT, a=4)
        Yn = R[:, 1, :].rearrange("p (c n) -> p c n", c=4)
        Tm, TT, Yl, Bm = (wk(1024 * i, 1024) for i in range(4))
        BKt = wk(4096, 2048).rearrange("p (a n) -> p a n", a=2)
        Wt, U = wk(6144, 1024), wk(7168, 1024)

        four_k = lambda r: R[:, r, :].rearrange("p (k t) -> p k t", k=KT)
        qT, kT, gbT = four_k(0), four_k(1), four_k(3)
        vS = R[:, 2, :].rearrange("p (b n) -> p b n", b=2)
        a5 = lambda at, n: R[:, 5, at:at + n]
        sc = a5(0, 768).rearrange("p (m k) -> p m k", m=2)
        es = a5(768, 768).rearrange("p (m k) -> p m k", m=2)
        attn, attT, t1, dist, On = a5(1536, 384), a5(1920, 384), a5(2304, 384), a5(2688, 384), a5(3072, 512)
        lam = a5(3584, 512).rearrange("p (a n) -> p a n", a=4)
        osq = a5(3584, 256)
        sm = lambda at, n: small[:, 64 + at:64 + at + n]
        mx, nmx, rsum, rrec, oss, ostd, orstd = sm(0, 4), sm(4, 4), sm(8, 4), sm(12, 4), sm(16, 2), sm(18, 2), sm(20, 2)
        sub1, nlam, lsum, lexp, eps5, eps6 = sm(22, 2), sm(24, 1), sm(26, 2), sm(28, 2), sm(30, 1), sm(31, 1)
        ssr = sm(32, 8).rearrange("p (b c) -> p b c", b=2)
        rsm, rstd_, rrstd, mss, mstd, mrstd = sm(40, 2), sm(42, 2), sm(44, 2), sm(46, 1), sm(47, 1), sm(48, 1)
        junk = M[:].rearrange("p k n -> p (k n)")
        rowsB = R[:, 2, :].rearrange("p (a n) -> p a n", a=2)
        src = R[:, 5, :].rearrange("p (b n) -> p b n", b=2)
        metaS = R[0:META, 1, 0:C]
        metaU = R[:, 1, C:C + KT * META].rearrange("p (k t) -> p k t", k=KT)
        sa, sgb, mT = four_k(0), four_k(1), four_k(2)
        PAD = TAPS - 1 - META
        A2 = R[:, 2, 0:8 * (PAD + TM)].rearrange("p (j t) -> p j t", j=8)
        ctmp = R[:, 2, 8 * (PAD + TM):8 * (PAD + TM) + 4 * TM].rearrange("p (b t) -> p b t", b=4)
        cc = R[:, 3, 0:8 * T].rearrange("p (j t) -> p j t", j=8)
        csq = [R[:, 2, 2304 + 512 * i:2304 + 512 * (i + 1)].rearrange("p (j t) -> p j t", j=2) for i in range(2)]
        cmean, crstd = R[:, 2, 3328:3584], R[:, 2, 3584:3840]
        wgrp = R[:, 3, 2048:4096].rearrange("p (g n) -> p g n", g=8)
        pz = R[:, 5, 0:8 * TM].rearrange("p (j t) -> p j t", j=8)
        pt = [R[:, 5, 8 * TM + 2 * TM * i:8 * TM + 2 * TM * (i + 1)].rearrange("p (j t) -> p j t", j=2) for i in range(3)]
        mtmp = [R[:, 3, 1024 * i:1024 * (i + 1)] for i in range(2)]
        fhi = RR[:, 0:2, :].rearrange("p a (k t) -> p (a k) t", t=T)
        flo = RR[:, 2:4, :].rearrange("p a (k t) -> p (a k) t", t=T)
        frel = [R[:, 6, 2048 + 1024 * i:3072 + 1024 * i] for i in range(2)]
        fsq = junk
        yS = src

        def xtmp(k):
            return M[:].rearrange("p k n -> p (k n)")[:, (k % 4) * T:(k % 4 + 1) * T]

        def split_hi(act, G, q):
            act.wait_ge(raw_loaded[q % RING], 16 * (2 * G + 1 + q // RING))
            if not (isinstance(G, int) and G == 0 and q < RING):
                act.wait_ge(slab_used, SLABS * G + q - RING + 1)
            nc.scalar.activation(whi[:, q % RING], wraw[:, q % RING], ACT.Copy).then_inc(hi_ready, 1)

        def split_lo(dve, G, q):
            dve.wait_ge(hi_ready, SLABS * G + q + 1)
            nc.vector.tensor_tensor(wlo[:, q % RING], wraw[:, q % RING], whi[:, q % RING].bitcast(F32),
                                    ALU.subtract).then_inc(lo_ready, 1)

        def group_slabs(eng, split, G, hook=None):
            for u in range(SLABS):
                g, q = (G, RING + u) if u < RING else (G + 1, u - RING)
                if not isinstance(g, int) or g < GROUPS:
                    split(eng, g, q)
                if hook:
                    hook(u)

        @block.sync
        def _(sp):
            sp.dma_start(cst[:], ins["consts"]).then_inc(S["params_loaded"], 16)
            sp.dma_start(vec[:], ins["vectors"]).then_inc(S["params_loaded"], 16)
            sp.dma_start(xT, xT_ap[:, :, 1:T + 1]).then_inc(S["x_loaded"], 16)
            sp.dma_start(xx, xT_ap[:, :, 0:T]).then_inc(S["x_loaded"], 16)
            for i, n in enumerate(("a_w1", "a_a1")):
                sp.dma_start(w1s[:, i], ins[n][0].rearrange("(k p) n -> p k n", p=P)).then_inc(S["lora_loaded"], 16)
            for i, n in enumerate(("a_w2", "a_a2")):
                sp.dma_start(w2s[0:LORA, i, :], ins[n][0]).then_inc(S["lora_loaded"], 16)

            def load_group(G, w, col, first=False, w_rest=None):
                v = w.rearrange("(k p) n -> p k n", p=P)
                for q in range(SLABS):
                    k = 2 * q
                    if w_rest is not None and q == SLABS // 2:
                        v = w_rest.rearrange("(k p) n -> p k n", p=P)
                    if w_rest is not None and q >= SLABS // 2:
                        k = 2 * q - SLABS
                    if not (first and q < RING):
                        sp.wait_ge(lo_ready, SLABS * G + q - RING + 1)
                    sp.dma_start(wraw[:, q % RING], v[:, k:k + 2, bass.ds(col, GW)]).then_inc(raw_loaded[q % RING], 16)

            load_group(0, W_in[0, 3], 0, first=True)
            with sp.Fori(1, 4) as i:
                load_group(i, W_in[0, 3], i * GW)
            for name, w in (("k", W_in[0, 1]), ("r", W_in[0, 0]), ("v", W_in[0, 2]), ("wout", ins["a_w_out"][0])):
                with sp.Fori(0, 4) as i:
                    load_group(i + G0[name], w, i * GW)
            if upto > 2:
                w_in2 = ins["w_in_2"][0]
                for name, w, col0, n in (("ks", ins["w_k_shared"], 0, 4), ("vs", ins["w_v_shared"], 0, 4), ("q", ins["b_w_qg"][0], 0, 4),
                                         ("gb", ins["b_w_qg"][0], C, 4), ("bout", ins["b_w_out"][0], 0, 4),
                                         ("cv", w_in2, C // 2, 4), ("pool", w_in2, 0, 2), ("gates", w_in2, 3 * C // 2, 8)):
                    with sp.Fori(0, n) as i:
                        load_group(i + G0[name], w, i * GW + col0)
                with sp.Fori(0, 4) as i:
                    load_group(i + G0["pc"], ins["w_pool_out_2"][0], i * GW, w_rest=ins["w_conv_out_2"][0])
                with sp.Fori(0, 4) as i:
                    load_group(i + G0["wo"], ins["w_o_2"][0], i * GW)
                for half in range(2):
                    with sp.Fori(0, 8) as i:
                        load_group(i + G0[f"up{half}"], ins["w_up_2"][0], i * GW + half * FF // 2)
                    with sp.Fori(0, 4) as i:
                        for quarter in range(2):
                            r0 = half * FF // 2 + quarter * C
                            load_group(2 * i + G0[f"down{half}"] + quarter, ins["w_down_2"][0, r0:r0 + C, :], i * GW)
                for c in range(4):
                    cols = slice(c * GW, (c + 1) * GW)
                    sp.wait_ge(S["out_cols"], c + 1)
                    sp.dma_start(out.rearrange("o (b p) n -> p (o b) n", p=P)[:, :, cols], H[:, :, cols]).then_inc(S["out_stored"], 16)
                if dbg is None:
                    sp.wait_ge(S["out_stored"], 64)

            if dbg is not None:
                dbg(sp, S, locals(), R, ahi, alo)

        @block.gpsimd
        def _(pool):
            for s in range(4):
                pool.wait_ge(S["silu_ready"], s + 1)
                pool.dma_start(gate_dram[:, 4 * s:4 * s + 4, :], tmpA[2 * (s % 2)].rearrange("p (b t) -> p b t", b=4)).then_inc(S[f"gate_stored{s % 2}"], 16)
            for s in range(4):
                pool.wait_ge(S["bvs_ready"], s + 1)
                pool.dma_start(bonus_dram[:, 4 * s:4 * s + 4, :], vtmp[2 + s % 2].rearrange("p (b t) -> p b t", b=4)).then_inc(S[f"bv_stored{s % 2}"], 16)
            for it in range(4):
                for lv in range(6):
                    for f in range(2):
                        n_ = (it * 6 + lv) * 2 + f
                        if lv == 0:
                            pool.wait_ge(S["am_ready"], 8 * it + 4 * f + 4)
                        if n_ >= 2:
                            pool.wait_ge(S["lv_y"], n_ - 1)
                        if lv == 1:
                            pool.wait_ge(S["lv_t"], n_ - 1)
                        nc.gpsimd.tensor_tensor(
                            Bm[:, f * GW:(f + 1) * GW].rearrange("p (h t) -> p h t", h=8), AM[:, 8 * f:8 * f + 8, 0, :],
                            cs(f"level{lv}").unsqueeze(1).broadcast_to([P, 8, CH]), ALU.mult).then_inc(S["lv_b"], 1)
            pool.wait_ge(S["y_mm"], 8)
            pool.wait_ge(S["bv_stored0"], 32)
            pool.wait_ge(S["bv_stored1"], 32)
            pool.wait_ge(S["gate_stored0"], 32)
            pool.wait_ge(S["gate_stored1"], 32)
            pool.dma_start(gT, gate_dram[:, :, :]).then_inc(S["gate_loaded"], 16)
            pool.dma_start(bvT, bonus_dram[:, :, :]).then_inc(S["bv_loaded"], 16)
            pool.dma_start(xre, ins["x"][0].rearrange("(b p) n -> p b n", p=P)).then_inc(S["x_reloaded"], 16)
            for i, n in enumerate(("ln_g", "ln_b")):
                pool.dma_start(rows[:, i, :], ins[n][0:1, :].broadcast_to([P, C])).then_inc(S["row_loaded"], 16)
            if upto < 3:
                return
            pool.wait_ge(S["acc_dve"], 4)
            pool.dma_start(lam, ins["b_lambda"][0:1].rearrange("o a n -> o (a n)").broadcast_to([P, 512]).rearrange("p (a n) -> p a n", a=4)).then_inc(S["extra_loaded"], 16)
            pool.dma_start(dist[:, 0:T], ins["dist"][:, 1, :]).then_inc(S["extra_loaded"], 16)
            pool.dma_start(dist[:, T:T + P], ins["dist"][:, 0, 0:P]).then_inc(S["extra_loaded"], 16)
            pool.wait_ge(S["turn_src"], 4)
            for i, n in enumerate(("ln_g", "ln_b")):
                pool.dma_start(rows[:, i, :], ins[n][1:2, :].broadcast_to([P, C])).then_inc(S["row_loaded"], 16)
            pool.wait_ge(S["o_mm"], AH)
            pool.dma_start(rowsB[:, 0, :], ins["g_pre_mix_2"][0:1, :].broadcast_to([P, C])).then_inc(S["meta_loaded"], 16)
            pool.dma_start(rowsB[0:META, 1, :], ins["meta_2"]).then_inc(S["meta_loaded"], 16)
            pool.wait_ge(S["x2_cols"], 4)
            for i, n in enumerate(("g_post_mix_2", "g_pre_mlp_2")):
                pool.dma_start(rows[:, i, :], ins[n][0:1, :].broadcast_to([P, C])).then_inc(S["post_loaded"], 16)
            pool.wait_ge(S["xs_ready"], XS["u1"])
            pool.dma_start(wgrp, ins["w_pool_grp_2"][0].rearrange("g (i p) n -> p (g i) n", p=P)).then_inc(S["grp_loaded"], 16)
            pool.wait_ge(S["turn_src"], 12)
            pool.dma_start(rows[:, 0, :], ins["g_post_mlp_2"][0:1, :].broadcast_to([P, C])).then_inc(S["last_loaded"], 16)

        @block.tensor
        def _(pe):
            mm = nc.tensor.matmul
            steps = Steps(pe, S["pe_step"])

            def three(o, hi_s, lo_s, hi_m, lo_m, first, last, sig=None):
                mm(o, hi_s, hi_m, start=first, stop=False, skip_group_check=True)
                mm(o, hi_s, lo_m, start=False, stop=False, skip_group_check=True)
                i = mm(o, lo_s, hi_m, start=False, stop=last, skip_group_check=True)
                if sig:
                    i.then_inc(sig, 1)

            def ws_group(G, outs, n, xh, xl, x_ready=None, hook=None):
                for q in range(SLABS):
                    pe.wait_ge(lo_ready, SLABS * G + q + 1)
                    for kk in range(2):
                        if x_ready:
                            pe.wait_ge(S["xs_ready"], x_ready(2 * q + kk))
                        for b in range(4):
                            c = slice(b * P, (b + 1) * P)
                            o, opens = outs[b]
                            three(o, whi[:, q % RING, kk, c], wlo[:, q % RING, kk, c], xh[:, 2 * q + kk, 0:n],
                                  xl[:, 2 * q + kk, 0:n], first=q == 0 and kk == 0 and opens,
                                  last=q == SLABS - 1 and kk == 1,
                                  sig=slab_used if kk == 1 and b == 3 else None)
                    if hook:
                        hook(q)

            def wm_group(G, outs, xh, xl, first=True, last=True, x_ready=None, k0=0, hook=None, ready=S["xs_ready"]):
                for q in range(SLABS):
                    pe.wait_ge(lo_ready, SLABS * G + q + 1)
                    for kk in range(2):
                        k = k0 + 2 * q + kk
                        if x_ready:
                            pe.wait_ge(ready, x_ready(k))
                        for tb in range(2):
                            c = slice(tb * P, (tb + 1) * P)
                            three(outs[tb], xh[:, k, c], xl[:, k, c], whi[:, q % RING, kk], wlo[:, q % RING, kk],
                                  first=first and q == 0 and kk == 0, last=last and q == SLABS - 1 and kk == 1,
                                  sig=slab_used if kk == 1 and tb == 1 else None)
                    if hook:
                        hook(q)

            def packed(b0):
                return [(ps[:, b0 + b // 2, (b % 2) * T:(b % 2 + 1) * T], b % 2 == 0) for b in range(4)]

            def turn(i, xs0, H):
                for c in range(4):
                    pe.wait_ge(S["turn_src"], 4 * i + c + 1)
                    if c >= 2:
                        pe.wait_ge(S["xs_ready"], xs0 + c - 1)
                    for k in range(4 * c, 4 * c + 4):
                        for tb in range(2):
                            m_ = nc.tensor.transpose(ps[:, 4 + 2 * (c % 2) + (k % 4) // 2, (k % 2) * T + tb * P:][:, 0:P],
                                                     H[:, tb, k * P:(k + 1) * P], cs("ident"))
                    m_.then_inc(S["turn_mm"], 1)

            pe.wait_ge(S["lora_loaded"], 64)
            for i in range(2):
                for k in range(KT):
                    pe.wait_ge(S["xa_ready"], KT * i + k + 1)
                    m_ = mm(ps[0:LORA, 6 + i, 0:T], w1s[:, i, k, :], xa[(KT * i + k) % 4],
                            start=(k == 0), stop=(k == KT - 1))
                    m_.then_inc(S["lora_z"], 1)
            for i in range(2):
                pe.wait_ge(S["lora_h"], i + 1)
                for j2 in range(KT // 2):
                    u = 8 * i + j2
                    if u >= 4:
                        pe.wait_ge(S["lora_s1"], 2 * (u - 3))
                    for j in (2 * j2, 2 * j2 + 1):
                        m_ = mm(ps[:, u % 4, (j % 2) * T:(j % 2 + 1) * T], w2s[0:LORA, i, j * P:(j + 1) * P],
                                hw[i][0:LORA, :], start=True, stop=True)
                    m_.then_inc(S["lora_zz"], 1)
            pe.wait_ge(S["lora_s1"], 32)

            for s in range(4):
                if s >= 2:
                    pe.wait_ge(S["silu_ready"], s - 1)
                ws_group(G0["g"] + s, packed(2 * (s % 2)), T, ahi, alo, (lambda k: k + 1) if s == 0 else None)
            def ss(g):
                def hook(q):
                    if q != 1:
                        return
                    pe.wait_ge(S["sq_ready"], g + 1)
                    for b in range(4):
                        for tb in range(2):
                            m_ = mm(ps[:, 6, tb * HEADS + 8 * g + 2 * b:][:, 0:2],
                                    tmpA[1][:, b * T + tb * P:b * T + (tb + 1) * P], cs("sel2"), start=True, stop=True)
                    m_.then_inc(S["ss_done"], 1)
                return hook
            for s in range(4):
                if s < 2:
                    pe.wait_ge(S["silu_ready"], 3 + s)
                else:
                    pe.wait_ge(S["kk_ready"], s - 1)
                    pe.wait_ge(S["acc_free_dve"], s - 1)
                ws_group(G0["k"] + s, packed(2 * (s % 2)), T, ahi, alo, (lambda k: KT + k + 1) if s == 0 else None,
                         ss(s - 1) if s else None)
            def bc(g):
                def hook(q):
                    if q == 1:
                        pe.wait_ge(S["rnx_ready"], g + 1)
                        for b in range(4):
                            for tb in range(2):
                                m_ = nc.tensor.transpose(ps[:, 4 + b // 2, (b % 2) * T + tb * P:][:, 0:P],
                                                         tmpA[0][:, (tb * 4 + b) * P:(tb * 4 + b + 1) * P], cs("ident"))
                        m_.then_inc(S["rnx_bc"], 1)
                return hook
            for s in range(4):
                if s < 2:
                    pe.wait_ge(S["kk_ready"], 3 + s)
                    pe.wait_ge(S["acc_free_dve"], 3 + s)
                    hook = ss(3) if s == 0 else bc(0)
                else:
                    pe.wait_ge(S["acc_free_dve"], 4 + s - 1)
                    hook = bc(s - 1)
                ws_group(G0["r"] + s, packed(2 * (s % 2)), T, ahi, alo, (lambda k: 2 * KT + k + 1) if s == 0 else None, hook)
            def vt(g):
                def hook(q):
                    if q == 1:
                        pe.wait_ge(S["acc_act"], g + 1)
                        if g:
                            pe.wait_ge(S["v_ready"], g)
                        for b in range(4):
                            for c in range(4):
                                for hs in (0, N):
                                    o = ps[hs:hs + N, 4 + b // 2, ((b % 2) * 4 + c) * N:((b % 2) * 4 + c + 1) * N]
                                    m_ = mm(o, vtmp[0][hs:hs + N, b * T + c * CH:b * T + (c + 1) * CH],
                                            cs("ident64")[hs:hs + N, :], start=True, stop=True)
                        m_.then_inc(S["vt_mm"], 1)
                    if q == 3:
                        pe.wait_ge(S["rk_ready"], g + 1)
                        if g:
                            pe.wait_ge(S["bvs_ready"], g)
                        for b in range(4):
                            m_ = mm(ps[:, 6 + b // 2, (b % 2) * T:(b % 2 + 1) * T], cs("heads"), vtmp[1][:, b * T:(b + 1) * T],
                                    start=True, stop=True)
                        m_.then_inc(S["rk_bc"], 1)
                return hook
            for s in range(4):
                if s < 2:
                    pe.wait_ge(S["acc_free_dve"], 4 + 3 + s)
                else:
                    pe.wait_ge(S["acc_act"], s - 1)
                ws_group(G0["v"] + s, packed(2 * (s % 2)), T, ahi, alo, (lambda k: 3 * KT + k + 1) if s == 0 else None,
                         vt(s - 1) if s else bc(3))
            vt(3)(1)
            vt(3)(3)

            pe.wait_ge(S["v_ready"], 4)
            pe.wait_ge(S["bvs_ready"], 4)
            pe.wait_ge(S["prep_done"], 1)
            for it in range(4):
                ts = slice(it * CH, (it + 1) * CH)
                for u in range(8):
                    if it:
                        pe.wait_ge(S["y_sb"], 2 * it)
                        pe.wait_ge(S["m_sb"], 2 * it)
                    for j in range(4 * (u // 2), 4 * (u // 2) + 4):
                        for hs in (0, N):
                            m_ = mm(ps[hs:hs + N, u, (j % 4) * P:(j % 4 + 1) * P].rearrange("p (a t) -> p a t", a=2),
                                    (Bc, Kc)[u % 2][hs:hs + N, j, ts], KR[hs:hs + N, j, :, ts], start=True, stop=True)
                    m_.then_inc(S["am_mm"], 1)
                for u in range(4):
                    pe.wait_ge(S["am_ready"], 8 * it + u + 1)
                    for j in range(8 * (u % 2), 8 * (u % 2) + 8):
                        for hs in (0, N):
                            m_ = mm(ps[hs:hs + N, u, (j % 8) * N:(j % 8 + 1) * N], (Bc, Kc)[u // 2][hs:hs + N, j, ts],
                                    cs("ident64")[hs:hs + N, :], start=True, stop=True)
                    m_.then_inc(S["tok_mm"], 1)

                def pairs(f, o_bank, *terms, done=True):
                    for j in range(8 * f, 8 * f + 8):
                        for hs in (0, N):
                            r_ = slice(hs, hs + N)
                            for n_, (lhs, rhs) in enumerate(terms):
                                m_ = mm(ps[r_, o_bank, (j % 8) * N:(j % 8 + 1) * N], lhs(r_, j), rhs(r_, j), start=n_ == 0,
                                        stop=n_ == len(terms) - 1)
                    return m_
                flat = lambda t_: lambda r_, j: t_[r_, j * N:(j + 1) * N]
                am = lambda a_: lambda r_, j: AM[r_, j, a_, :]
                hat = lambda a_: lambda r_, j: KR[r_, j, a_, ts]
                state = lambda r_, j: M[r_, j, :]
                value = lambda r_, j: V[r_, it, j, :]
                tok = lambda a_: lambda r_, j: BKt[r_, a_, j * N:(j + 1) * N]
                eye = lambda r_, j: cs("ident64")[r_, :]
                for lv in range(6):
                    for f in range(2):
                        n_ = (it * 6 + lv) * 2 + f
                        pe.wait_ge(S["lv_b"], n_ + 1)
                        if lv == 0:
                            pe.wait_ge(S["am_ready"], 8 * it + 8)
                            pe.wait_ge(S["tok_ready"], 4 * it + 4)
                        else:
                            pe.wait_ge(S["lv_t"], n_ - 1)
                        pairs(f, 4 + f, (flat(Bm), flat(Tm) if lv else eye)).then_inc(S["lv_y"], 1)
                    if lv == 0:
                        continue
                    for f in range(2):
                        pe.wait_ge(S["lv_ysb"], (it * 5 + lv - 1) * 2 + f + 1)
                        if lv < 5:
                            pairs(f, f, (flat(TT), flat(Yl)))
                        pairs(f, 2 + f, (flat(Yl), flat(TT))).then_inc(S["lv_z"], 1)
                pe.wait_ge(S["lv_t"], 12 * it + 12)
                if it:
                    pe.wait_ge(S["m_sb"], 2 * it)
                for f in range(2):
                    terms = ([(hat(0), state)] if it else []) + [(am(2), value)]
                    pairs(f, f, *terms).then_inc(S["w_mm"], 1)
                for f in range(2):
                    pe.wait_ge(S["w_sb"], 2 * it + f + 1)
                    pairs(f, 2 + f, (flat(TT), flat(Wt))).then_inc(S["u_mm"], 1)
                for f in range(2):
                    pe.wait_ge(S["u_sb"], 2 * it + f + 1)
                    terms = ([(hat(1), state)] if it else []) + [(am(1), flat(U)), (am(3), value)]
                    pairs(f, 4 + f, *terms).then_inc(S["y_mm"], 1)
                    if it < 3:
                        pairs(f, 6 + f, (tok(0), flat(U)), (tok(1), value)).then_inc(S["m_mm"], 1)

            pe.wait_ge(S["yn_ready"], 4)
            for j2 in range(8):
                if j2 >= 4:
                    pe.wait_ge(S["z1_ready"], j2 - 3)
                for j in (2 * j2, 2 * j2 + 1):
                    for c in range(4):
                        for hs in (0, N):
                            m_ = mm(ps[hs:hs + N, 4 + j2 % 4, (j % 2) * T + c * CH:(j % 2) * T + (c + 1) * CH],
                                    Yn[hs:hs + N, c, j * N:(j + 1) * N], cs("ident64")[hs:hs + N, :], start=True, stop=True)
                m_.then_inc(S["zt_mm"], 1)

            if upto < 2:
                return
            def wm_stage(name, x_ready):
                for s in range(4):
                    if s >= 2:
                        pe.wait_ge(S["acc_dve"], s - 1)
                    wm_group(G0[name] + s, [bank(2 * (s % 2)), bank(2 * (s % 2) + 1)], ahi, alo, x_ready=x_ready if s == 0 else None)
            wm_stage("wout", lambda k: 4 * KT + k // 2 + 1)
            turn(0, XS["ln0"], H)
            if upto < 3:
                return
            four_each = lambda name: lambda k: XS[name] + k // 4 + 1

            def ws_four(name, x_ready=None):
                with pe.Fori(0, 2) as i:
                    for s in range(2):
                        pe.wait_ge(acc_act, 2 * i + (ACC_ACT[name] + s - 1))
                        ws_group(2 * i + (G0[name] + s), packed(2 * s), T, ahi, alo, x_ready)

            acc_act, acc_dve = S["acc_act"], S["acc_dve"]
            pe.wait_ge(acc_dve, 4)
            ws_four("ks", four_each("ln0"))
            with pe.Fori(0, 2) as i:
                for s in range(2):
                    pe.wait_ge(acc_act, 2 * i + (ACC_ACT["vs"] + s - 1))
                    wm_group(2 * i + (G0["vs"] + s), [bank(2 * s), bank(2 * s + 1)], ahi, alo)
            ws_four("q")

            def att(t):
                for h in range(AH):
                    if t == PER * h + 6:
                        pe.wait_ge(S["on_ready"], h + 1)
                        for e in range(2):
                            for i in range(2):
                                m_ = nc.tensor.transpose(ps[:, 7, e * T + (1 - i) * P:][:, 0:P],
                                                         On[:, i * T + e * P:i * T + (e + 1) * P], cs("ident"))
                        m_.then_inc(S["ot_mm"], 1)
                    if t == PER * h + 4:
                        pe.wait_ge(S["attT_ready"], h + 1)
                        if h:
                            pe.wait_ge(S["ot_ready"], h)
                        for i, kb, first, last in ((0, 0, True, False), (0, 1, False, True), (1, 0, True, True)):
                            m_ = mm(ps[:, 7, i * T:(i + 1) * T], attT[:, (2 * i + kb) * P:(2 * i + kb + 1) * P],
                                    vS[:, kb, h * T:(h + 1) * T], start=first, stop=last)
                        m_.then_inc(S["o_mm"], 1)
                    if t == PER * h + 3:
                        pe.wait_ge(S["at_ready"], h + 1)
                        if h:
                            pe.wait_ge(S["attT_ready"], h)
                        for n_ in range(3):
                            m_ = nc.tensor.transpose(ps[:, 6, n_ * P:(n_ + 1) * P], attn[:, n_ * P:(n_ + 1) * P], cs("ident"))
                        m_.then_inc(S["att_mm"], 1)
                    if t == PER * h:
                        pe.wait_ge(acc_act, ACC_ACT["q"] + h // 2 + 1)
                        if h:
                            pe.wait_ge(S["sc_read"], h)
                        for m in range(2):
                            mm(ps[:, 4 + m, 0:T], qT[:, 2 * h + m, P:T], kT[:, 2 * h + m, :], start=True, stop=True)
                            m_ = mm(ps[:, 4 + m, T:T + P], qT[:, 2 * h + m, 0:P], kT[:, 2 * h + m, 0:P], start=True, stop=True)
                        m_.then_inc(S["sc_mm"], 1)
            for s in range(4):
                pe.wait_ge(acc_act, ACC_ACT["gb"] + s - 1)
                ws_group(G0["gb"] + s, packed(2 * (s % 2)), T, ahi, alo, None, lambda q, s=s: att(8 * s + q))
            for t in range(32, PER * 7 + 7):
                att(t)

            def meta(q):
                if q == 1:
                    pe.wait_ge(S["meta_src"], 1)
                    for k in range(KT):
                        m_ = nc.tensor.transpose(ps[:, 4, k * META:(k + 1) * META], metaS[:, k * P:(k + 1) * P],
                                                 cs("ident")[0:META, 0:META])
                    m_.then_inc(S["meta_mm"], 1)
            for s in range(4):
                if s < 2:
                    pe.wait_ge(acc_act, ACC_ACT["gb"] + 3 + s)
                else:
                    pe.wait_ge(acc_dve, ACC_DVE["bout"] + s - 1)
                wm_group(G0["bout"] + s, [bank(2 * (s % 2)), bank(2 * (s % 2) + 1)], ahi, alo, x_ready=four_each("z2") if s == 0 else None,
                         hook=meta if s == 2 else None)
            turn(1, XS["u1"], src)

            wide = lambda p: [(ps[:, 4 * p + b, 0:TM], True) for b in range(4)]
            pe.wait_ge(acc_dve, ACC_DVE["bout"] + 4)
            pe.wait_ge(S["meta_ready"], 1)
            for n_, (name, s) in enumerate((("cv", 0), ("cv", 1), ("cv", 2), ("cv", 3), ("pool", 0), ("pool", 1))):
                if n_ >= 2:
                    pe.wait_ge(acc_act, ACC_ACT["cv"] + n_ - 1)
                ws_group(G0[name] + s, wide(n_ % 2), TM, ahi, alo, four_each("u1") if n_ == 0 else None)

            def pool_map(q):
                if q != 1:
                    return
                pe.wait_ge(S["grp_loaded"], 16)
                pe.wait_ge(acc_act, ACC_ACT["pool"] + 2)
                pe.wait_ge(S["pool_d"], 1)
                for g in range(4):
                    for e in range(2):
                        for i in range(2):
                            m_ = mm(ps[:, 4 + g, e * T:(e + 1) * T], wgrp[:, 2 * g + i, e * P:(e + 1) * P],
                                    pz[:, 2 * g + i, META:TM], start=i == 0, stop=i == 1)
                m_.then_inc(S["pool_mm"], 1)
            for s in range(8):
                pe.wait_ge(acc_act, ACC_ACT["gates"] + s - 1)
                ws_group(G0["gates"] + s, packed(2 * (s % 2)), T, ahi, alo, None, pool_map if s == 2 else None)

            def conv_norm(q):
                if q == 0:
                    pe.wait_ge(S["conv_c"], 8)
                    pe.wait_ge(S["pool_y"], 4)
                    for j in range(8):
                        m_ = mm(ps[:, 6, 0:T], cs("ones"), cc[:, j, :], start=j == 0, stop=j == 7)
                    m_.then_inc(S["cs_mm"], 1)
                if q == 1:
                    for u in range(4):
                        pe.wait_ge(S["sqc_ready"], u + 1)
                        for j in range(2):
                            m_ = mm(ps[:, 7, 0:T], cs("ones"), csq[u % 2][:, j, :], start=u + j == 0, stop=u == 3 and j == 1)
                        m_.then_inc(S["cv_mm"], 1)
            for s in range(4):
                if s == 0:
                    pe.wait_ge(acc_act, ACC_ACT["gates"] + 8)
                elif s > 1:
                    pe.wait_ge(acc_dve, ACC_DVE["pc"] + s - 1)
                else:
                    pe.wait_ge(S["xs_ready"], XS["pc"] + 4)
                b0 = 4 * (s % 2)
                for part in range(2):
                    for q in range(4 * part, 4 * part + 4):
                        pe.wait_ge(lo_ready, SLABS * (G0["pc"] + s) + q + 1)
                        if s == 0:
                            pe.wait_ge(S["xs_ready"], XS["pc"] + q // 2 + 1)
                        for kk in range(2):
                            for b in range(4):
                                c = slice(b * P, (b + 1) * P)
                                o = ps[:, b0 + 2 * part + b // 2, (b % 2) * T:(b % 2 + 1) * T]
                                three(o, whi[:, q % RING, kk, c], wlo[:, q % RING, kk, c], ahi[:, 2 * q + kk, 0:T], alo[:, 2 * q + kk, 0:T],
                                      first=q == 4 * part and kk == 0 and b % 2 == 0, last=q == 4 * part + 3 and kk == 1,
                                      sig=slab_used if kk == 1 and b == 3 else None)
                        if s == 0:
                            conv_norm(q)
            for s in range(4):
                if s < 2:
                    pe.wait_ge(acc_dve, ACC_DVE["pc"] + 3)
                else:
                    pe.wait_ge(acc_act, ACC_ACT["wo"] + s - 1)
                wm_group(G0["wo"] + s, [bank(2 * (s % 2)), bank(2 * (s % 2) + 1)], ahi, alo, x_ready=four_each("m") if s == 0 else None)
            turn(2, XS["u2"], src)

            for half in range(2):
                up, down = f"up{half}", f"down{half}"
                if half:
                    pe.wait_ge(acc_dve, ACC_DVE["down1"])
                with pe.Fori(0, 4) as i:
                    for s in range(2):
                        pe.wait_ge(acc_act, 2 * i + (ACC_ACT[up] + s - 1))
                        ws_group(2 * i + (G0[up] + s), packed(2 * s), T, ahi, alo, four_each("u2"))
                pe.wait_ge(acc_act, ACC_ACT[up] + 8)
                with pe.Fori(0, 2) as i:
                    for s in range(2):
                        pe.wait_ge(acc_dve, 2 * i + (ACC_DVE[down] + s - 1))
                        for part in range(2):
                            wm_group(4 * i + (G0[down] + 2 * s + part), [bank(2 * s), bank(2 * s + 1)], fhi, flo, first=part == 0, last=part == 1,
                                     x_ready=lambda k: 8 * half + k // 4 + 1, k0=KT * part, ready=S["f_ready"])

        @block.scalar
        def _(act):
            a = nc.scalar.activation
            st = Steps(act, S["act_step"])
            sig = {k: Signal(v) for k, v in S.items()}

            act.wait_ge(S["params_loaded"], 32)
            act.wait_ge(S["lora_z"], KT)
            st.do(a(hw[0][0:LORA, :], ps[0:LORA, 6, 0:T], ACT.Tanh), sig["lora_h"])
            act.wait_ge(S["lora_z"], 2 * KT)
            st.do(a(hw[1][0:LORA, :], ps[0:LORA, 7, 0:T], ACT.Copy), sig["lora_h"])
            for i in range(2):
                for j in range(KT):
                    act.wait_ge(S["lora_zz"], 8 * i + j // 2 + 1)
                    o = KR[:, j, 0, :] if i == 0 else Bc[:, j, :]
                    st.do(a(o, ps[:, (8 * i + j // 2) % 4, (j % 2) * T:(j % 2 + 1) * T], ACT.Sigmoid,
                            bias=ve("w0" if i == 0 else "a0", j)), sig["lora_s1"])
            act.wait_ge(S["dec_done"], 2)
            st.do(a(gC[:], KR[:, :, 1, CH - 1::CH], ACT.Exp, scale=-DECAY))

            def build_hook(stage):
                def hook(u):
                    for k in (2 * u, 2 * u + 1):
                        act.wait_ge(S["xa_tmp"], KT * stage + k + 1)
                        st.do(a(ahi[:, k, 0:T], xtmp(k), ACT.Copy), sig["xa_hi"])
                return hook

            build_first = build_hook(0)
            for u in range(SLABS):
                if u < RING:
                    split_hi(act, 0, u)
                build_first(u)
            for s in range(4):
                G = G0["g"] + s
                group_slabs(act, split_hi, G, build_hook(1) if s == 3 else None)
                act.wait_ge(slab_used, SLABS * (G + 1))
                if s >= 2:
                    act.wait_ge(S[f"gate_stored{s % 2}"], 16)
                st.do(a(tmpA[2 * (s % 2)], bank(2 * (s % 2), 2), ACT.Silu), sig["silu_ready"])
            for s in range(4):
                G = G0["k"] + s
                group_slabs(act, split_hi, G, build_hook(2) if s == 3 else None)
                act.wait_ge(slab_used, SLABS * (G + 1))
                if s == 0:
                    act.wait_ge(S["gate_stored0"], 32)
                    act.wait_ge(S["gate_stored1"], 32)
                else:
                    act.wait_ge(S["acc_free_dve"], s)
                    act.wait_ge(S["ss_done"], s)
                kp = ps[:, 2 * (s % 2):2 * (s % 2) + 2, :].rearrange("p b (c t) -> p (b c) t", c=2)
                for b in range(4):
                    st.do(a(tmpA[0][:, b * T:(b + 1) * T], kp[:, b, :], ACT.Copy, scale=ve("k_k", 4 * s + b)),
                          sig["kk_copied"] if b == 3 else None)
                st.do(a(tmpA[2].rearrange("p (b t) -> p b t", b=4), KR[:, 4 * s:4 * s + 4, 1, :], ACT.Exp, scale=DECAY))
                st.do(a(KR[:, 4 * s:4 * s + 4, 0, :], KR[:, 4 * s:4 * s + 4, 0, :], ACT.Exp, scale=-DECAY), sig["kk_ready"])
                st.prev(3)
                st.do(a(tmpA[1], tmpA[0], ACT.Square), sig["sq_ready"])
            for s in range(4):
                G = G0["r"] + s
                group_slabs(act, split_hi, G, build_hook(3) if s == 3 else None)
                if s == 0:
                    act.wait_ge(S["ss_done"], 4)
                    st.do(a(small[:, 0:64], ps[:, 6, 0:64], ACT.Sqrt), sig["rn_ready"])
                act.wait_ge(S["dec_done"], 2)
                st.do(a(KR[:, 4 * s:4 * s + 4, 1, :], KR[:, 4 * s:4 * s + 4, 1, :], ACT.Exp, scale=-DECAY), sig["gi_ready"])
            for s in range(4):
                G = G0["v"] + s
                group_slabs(act, split_hi, G)
                act.wait_ge(slab_used, SLABS * (G + 1))
                if s == 0:
                    act.wait_ge(S["prep_done"], 1)
                else:
                    act.wait_ge(S["bvs_ready"], s)
                b0 = 2 * (s % 2)
                st.do(a(vtmp[0], bank(b0, 2), ACT.Copy), sig["acc_act"])
                act.wait_ge(S["vt_mm"], s + 1)
                st.do(a(V[:, :, 4 * s:4 * s + 4, :], ps[:, 4:6, :].rearrange("p b (j c n) -> p c (b j) n", j=2, c=4), ACT.Copy),
                      sig["v_ready"])
            for it in range(4):
                for u in range(4):
                    act.wait_ge(S["tok_mm"], 4 * it + u + 1)
                    if it:
                        act.wait_ge(S["m_mm"], 2 * it)
                    st.do(a(BKt[:, u // 2, (u % 2) * GW:(u % 2 + 1) * GW], bank(u), ACT.Copy), sig["tok_ready"])
                def gn_sqrt(i):
                    act.wait_ge(S["gn_var"], i + 1)
                    st.do(a(small[:, 176:192], small[:, 160:176], ACT.Sqrt), sig["gn_std"])
                for lv in range(1, 6):
                    for f in range(2):
                        act.wait_ge(S["lv_y"], (it * 6 + lv) * 2 + f + 1)
                        act.wait_ge(S["lv_t"], (it * 6 + lv) * 2 + f - 1)
                        st.do(a(Yl[:, f * GW:(f + 1) * GW], bank(4 + f), ACT.Copy), sig["lv_ysb"])
                    if lv == 2 and it:
                        gn_sqrt(it - 1)
                for f in range(2):
                    act.wait_ge(S["w_mm"], 2 * it + f + 1)
                    st.do(a(Wt[:, f * GW:(f + 1) * GW], bank(f), ACT.Copy), sig["w_sb"])
                for f in range(2):
                    act.wait_ge(S["u_mm"], 2 * it + f + 1)
                    if it:
                        act.wait_ge(S["m_mm"], 2 * it)
                        act.wait_ge(S["gn_var"], it)
                    st.do(a(U[:, f * GW:(f + 1) * GW], bank(2 + f), ACT.Copy, scale=-1.0), sig["u_sb"])
                for f in range(2):
                    act.wait_ge(S["y_mm"], 2 * it + f + 1)
                    if it == 0 and f == 0:
                        act.wait_ge(S["bv_stored0"], 32)
                        act.wait_ge(S["bv_stored1"], 32)
                    st.do(a(Yn[:, it, f * GW:(f + 1) * GW], bank(4 + f), ACT.Copy), sig["y_sb"])
            gn_sqrt(3)
            def z_hi(j2):
                act.wait_ge(S["z_f"], j2 + 1)
                st.do(a(ahi[:, 2 * j2:2 * j2 + 2, 0:T], zt[2 + j2 % 2].rearrange("p (b t) -> p b t", b=2), ACT.Copy), sig["z_hi"])
            for j2 in range(8):
                act.wait_ge(S["zt_mm"], j2 + 1)
                if j2 >= 2:
                    act.wait_ge(S["z_f"], j2 - 1)
                for b in range(2):
                    st.do(a(zt[j2 % 2][:, b * T:(b + 1) * T], ps[:, 4 + j2 % 4, b * T:(b + 1) * T], ACT.Identity,
                            bias=ve("gn_b", 2 * j2 + b), scale=ve("gn_g", 2 * j2 + b)), sig["z1_ready"] if b else None)
                if j2:
                    z_hi(j2 - 1)
            z_hi(7)
            if upto < 2:
                return
            def ln_act(i):
                act.wait_ge(S["ln_var"], i + 1)
                st.do(a(small[:, 244:246], mv[:, :, 1], ACT.Sqrt), sig["ln_std"])
                for c in range(4):
                    act.wait_ge(S["turn_mm"], 4 * i + c + 1)
                    st.do(a(ahi[:, 4 * c:4 * c + 4, 0:T], ps[:, 4 + 2 * (c % 2):6 + 2 * (c % 2), :].rearrange("p b (k t) -> p (b k) t", k=2),
                            ACT.Copy), sig["turn_hi"])
            for s in range(4):
                group_slabs(act, split_hi, G0["wout"] + s)
            ln_act(0)
            if upto < 3:
                return

            def evac_stage(name, n, evac, hook=None):
                for s in range(n):
                    G = G0[name] + s
                    group_slabs(act, split_hi, G, (lambda u, s=s: hook(8 * s + u)) if hook else None)
                    act.wait_ge(slab_used, SLABS * (G + 1))
                    evac(s)
            two = lambda s: ps[:, 2 * (s % 2):2 * (s % 2) + 2, :]
            tiles = lambda s: ps[:, 2 * (s % 2):2 * (s % 2) + 2, :].rearrange("p b (c t) -> p (b c) t", c=2)
            evac_stage("ks", 4, lambda s: st.do(a(kT[:, 4 * s:4 * s + 4, :], tiles(s), ACT.Copy), sig["acc_act"]))
            evac_stage("vs", 4, lambda s: st.do(a(vS[:, :, s * GW:(s + 1) * GW], two(s), ACT.Copy), sig["acc_act"]))
            evac_stage("q", 4, lambda s: st.do(a(qT[:, 4 * s:4 * s + 4, :], tiles(s), ACT.Copy), sig["acc_act"]))
            act.wait_ge(S["lam_ready"], 1)
            st.do(a(lexp, lsum, ACT.Exp), sig["lam_exp"])

            scale = DH ** -0.5
            def att(t):
                for h in range(AH):
                    if t == PER * h + 6:
                        act.wait_ge(S["ot_mm"], h + 1)
                        for e in range(2):
                            st.do(a(qT[:, 2 * h + e, :], ps[:, 7, e * T:(e + 1) * T], ACT.Copy, scale=sub1[:, e:e + 1]),
                                  sig["ot_ready"] if e else None)
                    if t == PER * h + 4:
                        act.wait_ge(S["o_mm"], h + 1)
                        act.wait_ge(S["lam_done"], 1)
                        for i in range(2):
                            if h or i:
                                st.prev()
                            st.do(a(osq, ps[:, 7, i * T:(i + 1) * T], ACT.Square, accum_out=oss[:, i:i + 1]))
                        st.prev()
                        if h:
                            act.wait_ge(S["on_ready"], h)
                        st.do(a(ostd, oss, ACT.Sqrt, bias=eps5, scale=1.0 / (2 * DH)), sig["ostd_ready"])
                    if t == PER * h + 3:
                        act.wait_ge(S["att_mm"], h + 1)
                        if h:
                            act.wait_ge(S["o_mm"], h)
                        st.do(a(attT, ps[:, 6, 0:384], ACT.Copy), sig["attT_ready"])
                    if t == PER * h + 1:
                        act.wait_ge(S["sc_ready"], h + 1)
                        if h:
                            act.wait_ge(S["at_ready"], h)
                        for i, cols in ((0, slice(0, T)), (1, slice(T, T + P))):
                            for m in range(2):
                                n_ = 2 * i + m
                                st.do(a(es[:, m, cols], sc[:, m, cols], ACT.Exp, bias=nmx[:, n_:n_ + 1], scale=scale,
                                        accum_out=rsum[:, n_:n_ + 1]), sig["e_ready"] if n_ == 3 else None)
            evac_stage("gb", 4, lambda s: st.do(a(gbT[:, 4 * s:4 * s + 4, :], tiles(s), ACT.Silu), sig["acc_act"]), att)
            for t in range(32, PER * 7 + 7):
                att(t)

            def four_hi(src_, k0, c, ready, n, done):
                act.wait_ge(ready, n)
                st.do(a(ahi[:, k0 + 4 * c:k0 + 4 * c + 4, 0:T], src_, ACT.Copy), done)
            for c in range(4):
                four_hi(qT[:, 4 * c:4 * c + 4, :], 0, c, S["zb_ready"], c + 1, sig["zb_hi"])

            def meta_norm():
                act.wait_ge(S["meta_loaded"], 32)
                st.do(a(metaS, rowsB[0:META, 1, :], ACT.Square, accum_out=mss[0:META]))
                st.prev()
                st.do(a(mstd[0:META], mss[0:META], ACT.Sqrt, bias=eps6[0:META], scale=1.0 / C), sig["meta_ssq"])
            def meta_turned():
                act.wait_ge(S["meta_f"], 1)
                st.do(a(ahi[:, :, T:TM], metaU, ACT.Copy), sig["meta_hi"])
            for s in range(4):
                group_slabs(act, split_hi, G0["bout"] + s)
                if s == 0:
                    meta_norm()
                if s == 2:
                    meta_turned()

            def ln_sqrt(i):
                act.wait_ge(S["ln_var"], i + 1)
                st.do(a(small[:, 244:246], mv[:, :, 1], ACT.Sqrt), sig["ln_std"])

            def squares(n, cols_ready, base):
                for c in range(4):
                    act.wait_ge(cols_ready, base + c + 1)
                    for tb in range(2):
                        if c or tb:
                            st.prev()
                        st.do(a(junk[:, 0:GW], src_of(n)[:, tb, c * GW:(c + 1) * GW], ACT.Square, accum_out=ssr[:, tb, c:c + 1]),
                              sig["ssq"] if c == 3 and tb else None)

            def src_of(n):
                return yS if n == 3 else H

            def rms_sqrt(n):
                act.wait_ge(S["ssum"], n + 1)
                st.do(a(rstd_, rsm, ACT.Sqrt, bias=eps6, scale=1.0 / C), sig["sstd"])

            def turned_hi(i):
                for c in range(4):
                    act.wait_ge(S["turn_mm"], 4 * i + c + 1)
                    st.do(a(ahi[:, 4 * c:4 * c + 4, 0:T], ps[:, 4 + 2 * (c % 2):6 + 2 * (c % 2), :].rearrange("p b (k t) -> p (b k) t", k=2),
                            ACT.Copy), sig["turn_hi"])
            ln_sqrt(1)
            squares(0, S["x2_cols"], 0)
            rms_sqrt(0)
            turned_hi(1)

            def wide_evac(dst, p, fn, last):
                st.do(a(dst[:, :, META:TM], ps[:, 4 * p:4 * p + 4, 0:T], fn))
                st.do(a(dst[:, :, 0:META], ps[:, 4 * p:4 * p + 4, T:TM], fn), last)
            def cv_evac(s):
                if s < 2:
                    wide_evac(A2[:, 4 * s:4 * s + 4, PAD:], s % 2, ACT.Copy, sig["acc_act"])
                else:
                    if s == 3:
                        act.wait_ge(S["cv_a"], 1)
                    wide_evac(ctmp, s % 2, ACT.Sigmoid, sig["acc_act"])
            evac_stage("cv", 4, cv_evac)
            evac_stage("pool", 2, lambda s: wide_evac(pz[:, 4 * s:4 * s + 4, :], s % 2, ACT.Copy, sig["acc_act"]))

            def gates_evac(s):
                dst = (sa, sgb)[s // 4]
                st.do(a(dst[:, 4 * (s % 4):4 * (s % 4) + 4, :], tiles(s), ACT.Sigmoid), sig["acc_act"])
                if s == 3:
                    act.wait_ge(S["pool_mm"], 1)
                    for j in range(8):
                        st.do(a(pz[:, j, META:TM], ps[:, 4 + j // 2, (j % 2) * T:(j % 2 + 1) * T], ACT.Copy, scale=ve("pool_scale", j)),
                              sig["pool_y"] if j % 2 else None)
            evac_stage("gates", 8, gates_evac)
            for c in range(2):
                four_hi(pz[:, 4 * c:4 * c + 4, META:TM], 0, c, S["pool_y"], 4, sig["p_hi"])
            act.wait_ge(S["cs_mm"], 1)
            st.do(a(cmean, ps[:, 6, 0:T], ACT.Copy, scale=1.0 / 1024), sig["cvar"])
            for u in range(4):
                act.wait_ge(S["xc_ready"], u // 2 + 1)
                if u >= 2:
                    act.wait_ge(S["cv_mm"], u - 1)
                st.do(a(csq[u % 2], cc[:, 2 * u:2 * u + 2, :], ACT.Square), sig["sqc_ready"])
            act.wait_ge(S["cv_mm"], 4)
            st.do(a(crstd, ps[:, 7, 0:T], ACT.Sqrt, bias=eps5, scale=1.0 / 1024), sig["cstd"])
            for c in range(2):
                act.wait_ge(S["cn_ready"], c + 1)
                for j in range(4 * c, 4 * c + 4):
                    st.do(a(cc[:, j, :], cc[:, j, :], ACT.Silu, bias=ve("conv_b", j), scale=ve("conv_g", j)), sig["conv_y"] if j % 4 == 3 else None)
                st.prev()
                st.do(a(ahi[:, 8 + 4 * c:12 + 4 * c, 0:T], cc[:, 4 * c:4 * c + 4, :], ACT.Copy), sig["c_hi"])
            for s in range(4):
                group_slabs(act, split_hi, G0["pc"] + s)
            for c in range(4):
                four_hi(mT[:, 4 * c:4 * c + 4, :], 0, c, S["m_ready"], c + 1, sig["m_hi"])
            def wo_evac(s):
                cols = slice(s * GW, (s + 1) * GW)
                for tb in range(2):
                    if s or tb:
                        st.prev()
                    st.do(a(junk[:, 0:GW], bank(2 * (s % 2) + tb), ACT.Square, accum_out=ssr[:, tb, s:s + 1]))
                st.do(a(yS[:, :, cols], two(s), ACT.Copy), sig["acc_act"])
            evac_stage("wo", 4, wo_evac)
            rms_sqrt(1)
            squares(2, S["y2_cols"], 0)
            rms_sqrt(2)
            turned_hi(2)

            def up_evac(half, s):
                if half or s >= 2:
                    act.wait_ge(S["f_sq"], 8 * half + s - 1)
                st.do(a(frel[s % 2], bank(2 * (s % 2), 2), ACT.Relu), sig["acc_act"])
                st.prev()
                st.do(a(fhi[:, 4 * s:4 * s + 4, :], frel[s % 2].rearrange("p (b t) -> p b t", b=4), ACT.Square), sig["f_hi"])
            for half in range(2):
                evac_stage(f"up{half}", 8, lambda s: up_evac(half, s))
                for s in range(8):
                    group_slabs(act, split_hi, G0[f"down{half}"] + s)
            squares(3, S["acc_dve"], ACC_DVE["down1"])
            rms_sqrt(3)

        @block.vector
        def _(dve):
            tt, ts_, stt = nc.vector.tensor_tensor, nc.vector.tensor_scalar, nc.vector.scalar_tensor_tensor
            st = Steps(dve, S["dve_step"])
            sig = {k: Signal(v) for k, v in S.items()}
            dve.wait_ge(S["params_loaded"], 32)
            dve.wait_ge(S["x_loaded"], 32)
            st.do(tt(xx, xx, xT, ALU.subtract))
            ka1 = small[:, 128:144]
            st.do(ts_(ka1, ve("k_a"), -1.0, 1.0, ALU.mult, ALU.add))
            st.prev(2)
            for i, mu in enumerate(("mu_w", "mu_a")):
                for k in range(KT):
                    n_ = KT * i + k
                    if n_ >= 4:
                        dve.wait_ge(S["lora_z"], n_ - 3)
                    st.do(stt(xa[n_ % 4], xx[:, k, :], ve(mu, k), xT[:, k, :], ALU.mult, ALU.add), sig["xa_ready"])
            for j in range(KT):
                dve.wait_ge(S["lora_s1"], j + 1)
                st.do(nc.vector.tensor_tensor_scan(KR[:, j, 1, :], cs("restart"), KR[:, j, 0, :], 0.0, ALU.mult, ALU.add),
                      sig["dec_done"] if j == KT - 1 else None)
            st.prev()
            st.do(tt(KR[:, :, 0, :], KR[:, :, 1, :], KR[:, :, 0, :], ALU.subtract), sig["dec_done"])

            def build_hook(stage, mu, G):
                def hook(u):
                    for k in (2 * u, 2 * u + 1):
                        n_ = KT * stage + k
                        if n_ >= 4:
                            dve.wait_ge(S["xs_ready"], n_ - 3)
                        st.do(stt(xtmp(k), xx[:, k, :], ve(mu, k), xT[:, k, :], ALU.mult, ALU.add), sig["xa_tmp"])
                    for k in (2 * u, 2 * u + 1):
                        dve.wait_ge(S["xa_hi"], KT * stage + k + 1)
                        st.do(tt(alo[:, k, 0:T], xtmp(k), ahi[:, k, 0:T].bitcast(F32), ALU.subtract), sig["xs_ready"])
                return hook

            dve.wait_ge(S["lora_zz"], 16)
            first = build_hook(0, "mu_g", None)
            for u in range(SLABS):
                if u < RING:
                    split_lo(dve, 0, u)
                first(u)
            for s in range(4):
                group_slabs(dve, split_lo, G0["g"] + s, build_hook(1, "mu_k", 0) if s == 3 else None)
            KP = tmpA[3]
            for s in range(4):
                G = G0["k"] + s
                group_slabs(dve, split_lo, G, build_hook(2, "mu_r", 0) if s == 3 else None)
                dve.wait_ge(slab_used, SLABS * (G + 1))
                if s == 0:
                    dve.wait_ge(S["gate_stored0"], 32)
                    dve.wait_ge(S["gate_stored1"], 32)
                j4 = slice(4 * s, 4 * s + 4)
                four = lambda t_: t_.rearrange("p (b t) -> p b t", b=4)
                kp = bank(2 * (s % 2), 2)
                for b in range(4):
                    st.do(ts_(KP[:, b * T:(b + 1) * T], Bc[:, 4 * s + b, :], ve("k_a", 4 * s + b), ka1[:, 4 * s + b:4 * s + b + 1],
                              ALU.mult, ALU.add))
                st.prev()
                dve.wait_ge(S["kk_copied"], s + 1)
                st.do(tt(KP, KP, kp, ALU.mult))
                dve.wait_ge(S["kk_ready"], s + 1)
                st.do(tt(KR[:, j4, 0, :], KR[:, j4, 0, :], four(tmpA[0]), ALU.mult))
                st.do(tt(Bc[:, j4, :], Bc[:, j4, :], four(tmpA[0]), ALU.mult))
                st.prev(3)
                st.do(tt(Kc[:, j4, :], four(KP), four(tmpA[2]), ALU.mult))
                st.prev(2)
                st.do(tt(Bc[:, j4, :], Bc[:, j4, :], four(tmpA[2]), ALU.mult), sig["acc_free_dve"])
            rn = small[:, 0:64].rearrange("p (b h) -> p b h", b=2)
            for s in range(4):
                G = G0["r"] + s
                group_slabs(dve, split_lo, G, build_hook(3, "mu_v", 0) if s == 3 else None)
                if s == 0:
                    dve.wait_ge(S["rn_ready"], 1)
                    st.do(ts_(small[:, 0:64], small[:, 0:64], 1e-12, None, ALU.max))
                    st.prev()
                    st.do(nc.vector.reciprocal(small[:, 0:64], small[:, 0:64]))
                    st.prev()
                else:
                    dve.wait_ge(S["rnx_bc"], s)
                st.do(nc.vector.tensor_copy(tmpA[0].rearrange("p (b h n) -> p b h n", b=2, h=8),
                                            rn[:, :, 8 * s:8 * s + 8].unsqueeze(3).broadcast_to([P, 2, 8, N])), sig["rnx_ready"])
                j4 = slice(4 * s, 4 * s + 4)
                four = lambda t_: t_.rearrange("p (b t) -> p b t", b=4)
                dve.wait_ge(slab_used, SLABS * (G + 1))
                dve.wait_ge(S["gi_ready"], s + 1)
                st.do(tt(KR[:, j4, 1, :], KR[:, j4, 1, :], ps[:, 2 * (s % 2):2 * (s % 2) + 2, :].rearrange("p b (c t) -> p (b c) t", c=2), ALU.mult),
                      sig["acc_free_dve"])
                dve.wait_ge(S["rnx_bc"], s + 1)
                bcst = ps[:, 4:6, :].rearrange("p b (c t) -> p (b c) t", c=2)
                st.do(tt(KR[:, j4, 0, :], KR[:, j4, 0, :], bcst, ALU.mult))
                st.do(tt(Bc[:, j4, :], Bc[:, j4, :], bcst, ALU.mult), sig["prep_done"] if s == 3 else None)
            for s in range(4):
                group_slabs(dve, split_lo, G0["v"] + s)
                if s:
                    dve.wait_ge(S["rk_bc"], s)
                for b in range(4):
                    st.do(stt(vtmp[1][:, b * T:(b + 1) * T], Kc[:, 4 * s + b, :], ve("r_k", 4 * s + b), KR[:, 4 * s + b, 1, :],
                              ALU.mult, ALU.mult), sig["rk_ready"] if b == 3 else None)
                dve.wait_ge(S["rk_bc"], s + 1)
                dve.wait_ge(S["acc_act"], s + 1)
                if s >= 2:
                    dve.wait_ge(S[f"bv_stored{s % 2}"], 16)
                st.do(tt(vtmp[2 + s % 2], vtmp[0], bank(6, 2), ALU.mult), sig["bvs_ready"])
            def heads(t_, h=16):
                return t_.rearrange("p (h n) -> p h n", h=h)
            gsum, gvar, gstd = small[:, 144:160], small[:, 160:176], small[:, 176:192]

            def y_of(i):
                return heads(Yn[:, i, :])

            def gn_part1(i):
                dve.wait_ge(S["y_sb"], 2 * i + 2)
                y = y_of(i)
                st.do(nc.vector.tensor_reduce(gsum, y, AX.X, ALU.add))
                st.prev()
                st.do(ts_(gsum, gsum, 1.0 / N, None, ALU.mult))
                st.prev()
                st.do(tt(y, y, gsum.unsqueeze(2).broadcast_to([P, 16, N]), ALU.subtract))
                st.prev()
                st.do(tt(heads(U), y, y, ALU.mult))
                st.prev()
                if i:
                    dve.wait_ge(S["gn_std"], i)
                st.do(nc.vector.tensor_reduce(gvar, heads(U), AX.X, ALU.add))
                st.prev()
                st.do(ts_(gvar, gvar, 1.0 / N, GN_EPS, ALU.mult, ALU.add), sig["gn_var"])

            def gn_part2(i):
                dve.wait_ge(S["gn_std"], i + 1)
                st.do(nc.vector.reciprocal(gsum, gstd))
                st.prev()
                st.do(tt(y_of(i), y_of(i), gsum.unsqueeze(2).broadcast_to([P, 16, N]), ALU.mult), sig["yn_ready"])

            for it in range(4):
                if it:
                    dve.wait_ge(S["y_mm"], 2 * it)
                for u in range(8):
                    dve.wait_ge(S["am_mm"], 8 * it + u + 1)
                    st.do(tt(AM[:, 4 * (u // 2):4 * (u // 2) + 4, 2 * (u % 2):2 * (u % 2) + 2, :].rearrange("p h a t -> p h (a t)"),
                             ps[:, u, :].rearrange("p (h n) -> p h n", h=4),
                             cs("causal").unsqueeze(1).broadcast_to([P, 4, 2 * CH]), ALU.mult), sig["am_ready"])
                i8 = cs("ident64").unsqueeze(1).broadcast_to([P, 8, CH])
                for f in range(2):
                    fs = slice(f * GW, (f + 1) * GW)
                    dve.wait_ge(S["lv_y"], it * 12 + f + 1)
                    st.do(tt(heads(Tm[:, fs], 8), i8, heads(bank(4 + f), 8), ALU.subtract))
                    st.do(tt(heads(TT[:, fs], 8), i8, heads(Bm[:, fs], 8), ALU.subtract), sig["lv_t"])
                for lv in range(1, 6):
                    for f in range(2):
                        fs = slice(f * GW, (f + 1) * GW)
                        dve.wait_ge(S["lv_z"], (it * 5 + lv - 1) * 2 + f + 1)
                        if f == 0:
                            st.prev()
                        if lv < 5:
                            st.do(tt(Tm[:, fs], Tm[:, fs], bank(f), ALU.subtract))
                        st.do(tt(TT[:, fs], TT[:, fs], bank(2 + f), ALU.subtract), sig["lv_t"])
                    if it and lv == 1:
                        gn_part1(it - 1)
                    if it and lv == 3:
                        gn_part2(it - 1)
                for f in range(2):
                    if it == 3:
                        break
                    dve.wait_ge(S["m_mm"], 2 * it + f + 1)
                    new, add = M[:, 8 * f:8 * f + 8, :], heads(bank(6 + f), 8)
                    if it:
                        st.do(tt(new, new, add, ALU.add))
                        st.prev()
                        add = new
                    st.do(tt(new, add, gC[:, 8 * f:8 * f + 8, it].unsqueeze(2).broadcast_to([P, 8, N]), ALU.mult), sig["m_sb"])
            gn_part1(3)
            gn_part2(3)
            dve.wait_ge(S["gate_loaded"], 16)
            dve.wait_ge(S["bv_loaded"], 16)
            def z_lo(j2):
                dve.wait_ge(S["z_hi"], j2 + 1)
                st.do(tt(alo[:, 2 * j2:2 * j2 + 2, 0:T], zt[2 + j2 % 2].rearrange("p (b t) -> p b t", b=2),
                         ahi[:, 2 * j2:2 * j2 + 2, 0:T].bitcast(F32), ALU.subtract), sig["xs_ready"])
            for j2 in range(8):
                dve.wait_ge(S["z1_ready"], j2 + 1)
                st.do(tt(zt[j2 % 2], zt[j2 % 2], bvT[:, 2 * j2:2 * j2 + 2, :].rearrange("p k t -> p (k t)"), ALU.add), sig["z_ready"])
                st.prev()
                st.do(tt(zt[2 + j2 % 2], zt[j2 % 2], gT[:, 2 * j2:2 * j2 + 2, :].rearrange("p k t -> p (k t)"), ALU.mult), sig["z_f"])
                if j2:
                    z_lo(j2 - 1)
            z_lo(7)
            if upto < 2:
                return
            stats = small[:, 192:240].rearrange("p (b s a) -> p b s a", b=2, s=4)
            rstd = small[:, 246:248]

            def ln_evac(name, i, other, extra=None):
                for s in range(4):
                    group_slabs(dve, split_lo, G0[name] + s)
                    if extra:
                        extra(s)
                    dve.wait_ge(slab_used, SLABS * (G0[name] + s + 1))
                    cols = slice(s * GW, (s + 1) * GW)
                    st.do(stt(H[:, :, cols], other[:, :, cols], ALPHA, ps[:, 2 * (s % 2):2 * (s % 2) + 2, :], ALU.mult, ALU.add),
                          sig["acc_dve"])
                    st.prev()
                    for tb in range(2):
                        st.do(nc.vector.bn_stats(stats[:, tb, s, :], H[:, tb, cols]))

            def turned_lo(i, c):
                dve.wait_ge(S["turn_hi"], 4 * i + c + 1)
                st.do(tt(alo[:, 4 * c:4 * c + 4, 0:T], ps[:, 4 + 2 * (c % 2):6 + 2 * (c % 2), :].rearrange("p b (k t) -> p (b k) t", k=2),
                         ahi[:, 4 * c:4 * c + 4, 0:T].bitcast(F32), ALU.subtract), sig["xs_ready"])

            def ln_dve(i):
                st.prev()
                for tb in range(2):
                    st.do(nc.vector.bn_aggr(mv[:, tb, :], stats[:, tb, :, :].rearrange("p s a -> p (s a)")))
                st.prev()
                st.do(ts_(mv[:, :, 1], mv[:, :, 1], LN_EPS, None, ALU.add), sig["ln_var"])
                dve.wait_ge(S["ln_std"], i + 1)
                st.do(nc.vector.reciprocal(rstd, small[:, 244:246]))
                dve.wait_ge(S["row_loaded"], 32 * (i + 1))
                st.prev()
                for c in range(4):
                    cols = slice(c * GW, (c + 1) * GW)
                    for tb in range(2):
                        st.do(ts_(H[:, tb, cols], H[:, tb, cols], mv[:, tb, 0:1], rstd[:, tb:tb + 1], ALU.subtract, ALU.mult))
                    st.prev()
                    for a_ in range(2):
                        st.do(tt(H[:, :, cols], H[:, :, cols], rows[:, a_, cols].unsqueeze(1).broadcast_to([P, 2, GW]),
                                 ALU.mult if a_ == 0 else ALU.add), None if a_ == 0 else sig["turn_src" if i == 0 else "x2_cols"])
                        if a_ == 0:
                            st.prev()
                    if c and i == 0:
                        turned_lo(0, c - 1)
                if i == 0:
                    turned_lo(0, 3)
            dve.wait_ge(S["x_reloaded"], 16)
            ln_evac("wout", 0, xre)
            ln_dve(0)
            if upto < 3:
                return
            slabs = lambda name, n: [group_slabs(dve, split_lo, G0[name] + s) for s in range(n)]
            slabs("ks", 4)
            st.do(nc.vector.memset(eps5, 1e-5))
            st.do(nc.vector.memset(eps6, RMS_EPS))
            st.do(ts_(sub1, ve("subln"), 1.0 - LAM_INIT, None, ALU.mult))
            slabs("vs", 4)
            dve.wait_ge(S["extra_loaded"], 48)
            for i in range(2):
                st.do(tt(lam[:, 2 * i, :], lam[:, 2 * i, :], lam[:, 2 * i + 1, :], ALU.mult))
            st.prev()
            for i in range(2):
                st.do(nc.vector.tensor_reduce(lsum[:, i:i + 1], lam[:, 2 * i, :], AX.X, ALU.add), sig["lam_ready"] if i else None)
            slabs("q", 4)
            dve.wait_ge(S["lam_exp"], 1)
            st.do(tt(nlam, lexp[:, 1:2], lexp[:, 0:1], ALU.subtract))
            st.prev()
            st.do(ts_(nlam, nlam, -LAM_INIT, None, ALU.add), sig["lam_done"])

            scale = DH ** -0.5
            def att(t):
                if t in (11, 19, 27):
                    zmul((t - 11) // 8)
                for h in range(AH):
                    if t == PER * h + 5:
                        dve.wait_ge(S["ostd_ready"], h + 1)
                        st.do(nc.vector.reciprocal(orstd, ostd))
                        if h:
                            dve.wait_ge(S["ot_mm"], h)
                        st.prev()
                        for i in range(2):
                            st.do(ts_(On[:, i * T:(i + 1) * T], ps[:, 7, i * T:(i + 1) * T], orstd[:, i:i + 1], None, ALU.mult),
                                  sig["on_ready"] if i else None)
                    if t == PER * h + 2:
                        dve.wait_ge(S["e_ready"], h + 1)
                        st.do(nc.vector.reciprocal(rrec, rsum))
                        st.prev()
                        st.do(ts_(rrec[:, 1:4:2], rrec[:, 1:4:2], nlam, None, ALU.mult))
                        st.prev()
                        both = ((0, slice(0, T)), (1, slice(T, T + P)))
                        for i, cols in both:
                            st.do(ts_(t1[:, cols], es[:, 1, cols], rrec[:, 2 * i + 1:2 * i + 2], None, ALU.mult))
                        if h:
                            dve.wait_ge(S["att_mm"], h)
                        st.prev()
                        for i, cols in both:
                            st.do(stt(attn[:, cols], es[:, 0, cols], rrec[:, 2 * i:2 * i + 1], t1[:, cols], ALU.mult, ALU.add),
                                  sig["at_ready"] if i else None)
                    if t == PER * h:
                        dve.wait_ge(S["sc_mm"], h + 1)
                        if h:
                            dve.wait_ge(S["e_ready"], h)
                        st.do(stt(sc, dist.unsqueeze(1).broadcast_to([P, 2, 384]), 2.0 ** -(h + 1) / scale, ps[:, 4:6, 0:384],
                                  ALU.mult, ALU.add), sig["sc_read"])
                        st.prev()
                        st.do(nc.vector.tensor_reduce(mx[:, 0:2], sc[:, :, 0:T], AX.X, ALU.max))
                        st.do(nc.vector.tensor_reduce(mx[:, 2:4], sc[:, :, T:T + P], AX.X, ALU.max))
                        st.prev()
                        st.do(ts_(nmx, mx, -scale, None, ALU.mult), sig["sc_ready"])

            def zmul(s):
                dve.wait_ge(S["acc_act"], ACC_ACT["gb"] + s + 1)
                dve.wait_ge(S["ot_ready"], 2 * s + 2)
                j4 = slice(4 * s, 4 * s + 4)
                st.do(tt(qT[:, j4, :], qT[:, j4, :], gbT[:, j4, :], ALU.mult), sig["zb_ready"])
            for s in range(4):
                group_slabs(dve, split_lo, G0["gb"] + s, lambda u, s=s: att(8 * s + u))
            for t in range(32, PER * 7 + 7):
                att(t)
            zmul(3)

            def four_lo(src_, k0, c, ready, n):
                dve.wait_ge(ready, n)
                ks_ = slice(k0 + 4 * c, k0 + 4 * c + 4)
                st.do(tt(alo[:, ks_, 0:T], src_, ahi[:, ks_, 0:T].bitcast(F32), ALU.subtract), sig["xs_ready"])
            for c in range(4):
                four_lo(qT[:, 4 * c:4 * c + 4, :], 0, c, S["zb_hi"], c + 1)

            def meta(s):
                if s == 1:
                    dve.wait_ge(S["meta_ssq"], 1)
                    st.do(nc.vector.reciprocal(mrstd[0:META], mstd[0:META]))
                    st.prev()
                    st.do(stt(metaS, rowsB[0:META, 1, :], mrstd[0:META], rowsB[0:META, 0, :], ALU.mult, ALU.mult), sig["meta_src"])
                if s == 2:
                    dve.wait_ge(S["meta_mm"], 1)
                    st.do(nc.vector.tensor_copy(metaU, ps[:, 4, 0:KT * META].rearrange("p (k t) -> p k t", k=KT)), sig["meta_f"])
                if s == 3:
                    dve.wait_ge(S["meta_hi"], 1)
                    st.do(tt(alo[:, :, T:TM], metaU, ahi[:, :, T:TM].bitcast(F32), ALU.subtract), sig["meta_ready"])
            ln_evac("bout", 1, H, meta)
            ln_dve(1)

            def rms(n):
                dve.wait_ge(S["ssq"] if n != 1 else S["acc_act"], (1, ACC_ACT["up0"], 2, 3)[n])
                st.do(nc.vector.tensor_reduce(rsm, ssr, AX.X, ALU.add), sig["ssum"])
                dve.wait_ge(S["sstd"], n + 1)
                st.do(nc.vector.reciprocal(rrstd, rstd_))
                st.prev()

            def normed_turned(i, gain):
                for c in range(4):
                    cols = slice(c * GW, (c + 1) * GW)
                    for tb in range(2):
                        st.do(stt(src[:, tb, cols], H[:, tb, cols], rrstd[:, tb:tb + 1], gain[:, cols], ALU.mult, ALU.mult),
                              sig["turn_src"] if tb else None)
                    if c:
                        turned_lo(i, c - 1)
                turned_lo(i, 3)
            rms(0)
            normed_turned(1, rowsB[:, 0, :])

            slabs("cv", 3)
            st.do(nc.vector.memset(A2[:, :, 0:PAD], 0.0))
            def cv_gate(s):
                dve.wait_ge(S["acc_act"], ACC_ACT["cv"] + 3 + s)
                x_ = A2[:, 4 * s:4 * s + 4, PAD:]
                st.do(tt(x_, x_, ctmp, ALU.mult), sig["cv_a"])
            cv_gate(0)

            conv_at = [0]
            def conv_steps(n, limit):
                for _ in range(n):
                    if conv_at[0] >= limit:
                        return
                    pair, tap = divmod(conv_at[0], TAPS)
                    for j in (2 * pair, 2 * pair + 1):
                        w_ = ve("w_dw")[:, j * TAPS + tap:j * TAPS + tap + 1]
                        x_ = A2[:, j, tap:tap + T]
                        if conv_at[0] or j % 2:
                            st.prev(1 if tap == 0 and j % 2 == 0 else 2)
                        if tap == 0:
                            st.do(ts_(cc[:, j, :], x_, w_, ve("b_dw", j), ALU.mult, ALU.add))
                        else:
                            st.do(stt(cc[:, j, :], x_, w_, cc[:, j, :], ALU.mult, ALU.add), sig["conv_c"] if tap == TAPS - 1 else None)
                    conv_at[0] += 1
            st.prev()
            group_slabs(dve, split_lo, G0["cv"] + 3, lambda u: conv_steps(2, 62))
            cv_gate(1)
            st.prev()
            for s in range(2):
                group_slabs(dve, split_lo, G0["pool"] + s, lambda u: conv_steps(2, 124))

            def pools():
                dve.wait_ge(S["acc_act"], ACC_ACT["pool"] + 2)
                for g, w in enumerate(WINDOWS):
                    z, prev_, span, k = pz[:, 2 * g:2 * g + 2, :], None, 1, 0
                    cur = z
                    while span < w:
                        nxt = pt[k % 2]
                        st.do(tt(nxt[:, :, 2 * span - 1:], cur[:, :, 2 * span - 1:], cur[:, :, span - 1:TM - span], ALU.add))
                        st.prev()
                        cur, span, k = nxt, 2 * span, k + 1
                    st.do(stt(z[:, :, META:], cur[:, :, META:], 1.0 / w, z[:, :, META:], ALU.mult, ALU.subtract),
                          sig["pool_d"] if g == 3 else None)
                    st.prev()
            for s in range(8):
                if s == 1:
                    pools()
                group_slabs(dve, split_lo, G0["gates"] + s, (lambda u: conv_steps(2, 124)) if s != 0 else None)
            conv_steps(124, 124)
            for c in range(2):
                four_lo(pz[:, 4 * c:4 * c + 4, META:TM], 0, c, S["p_hi"], c + 1)
            dve.wait_ge(S["cvar"], 1)
            for c in range(2):
                st.do(tt(cc[:, 4 * c:4 * c + 4, :], cc[:, 4 * c:4 * c + 4, :], cmean.unsqueeze(1).broadcast_to([P, 4, T]), ALU.subtract),
                      sig["xc_ready"])
            dve.wait_ge(S["cstd"], 1)
            st.do(nc.vector.reciprocal(crstd, crstd))
            st.prev()
            for c in range(2):
                st.do(tt(cc[:, 4 * c:4 * c + 4, :], cc[:, 4 * c:4 * c + 4, :], crstd.unsqueeze(1).broadcast_to([P, 4, T]), ALU.mult),
                      sig["cn_ready"])
            for c in range(2):
                four_lo(cc[:, 4 * c:4 * c + 4, :], 8, c, S["c_hi"], c + 1)
            flat4 = lambda t_: t_.rearrange("p b t -> p (b t)")
            for s in range(4):
                group_slabs(dve, split_lo, G0["pc"] + s)
                dve.wait_ge(slab_used, SLABS * (G0["pc"] + s + 1))
                j4, b0 = slice(4 * s, 4 * s + 4), 4 * (s % 2)
                if s:
                    st.prev()
                st.do(tt(mtmp[0], flat4(sa[:, j4, :]), bank(b0, 2), ALU.mult))
                st.do(tt(mtmp[1], flat4(sgb[:, j4, :]), bank(b0 + 2, 2), ALU.mult), sig["acc_dve"])
                st.prev()
                st.do(tt(flat4(mT[:, j4, :]), mtmp[0], mtmp[1], ALU.add), sig["m_ready"])
            for c in range(4):
                four_lo(mT[:, 4 * c:4 * c + 4, :], 0, c, S["m_hi"], c + 1)
            slabs("wo", 4)

            def post(n, gain, done):
                for c in range(4):
                    cols = slice(c * GW, (c + 1) * GW)
                    for tb in range(2):
                        st.do(stt(yS[:, tb, cols], yS[:, tb, cols], rrstd[:, tb:tb + 1], gain[:, cols], ALU.mult, ALU.mult))
                    st.prev()
                    st.do(tt(H[:, :, cols], H[:, :, cols], yS[:, :, cols], ALU.add), done)
            rms(1)
            dve.wait_ge(S["post_loaded"], 32)
            post(1, rows[:, 0, :], sig["y2_cols"])
            rms(2)
            normed_turned(2, rows[:, 1, :])

            def f_lo(half, s):
                n_ = 8 * half + s
                dve.wait_ge(S["acc_act"], ACC_ACT[f"up{half}"] + s + 1)
                st.prev()
                st.do(tt(fsq, frel[s % 2], frel[s % 2], ALU.mult), sig["f_sq"])
                dve.wait_ge(S["f_hi"], n_ + 1)
                st.prev()
                st.do(tt(flo[:, 4 * s:4 * s + 4, :], fsq.rearrange("p (b t) -> p b t", b=4), fhi[:, 4 * s:4 * s + 4, :].bitcast(F32),
                         ALU.subtract), sig["f_ready"])
            for half in range(2):
                for s in range(8):
                    group_slabs(dve, split_lo, G0[f"up{half}"] + s)
                    f_lo(half, s)
                for s in range(4):
                    for part in range(2):
                        G = G0[f"down{half}"] + 2 * s + part
                        group_slabs(dve, split_lo, G)
                    dve.wait_ge(slab_used, SLABS * (G + 1))
                    y_ = yS[:, :, s * GW:(s + 1) * GW]
                    if half:
                        st.do(tt(y_, y_, ps[:, 2 * (s % 2):2 * (s % 2) + 2, :], ALU.add), sig["acc_dve"])
                    else:
                        st.do(nc.vector.tensor_copy(y_, ps[:, 2 * (s % 2):2 * (s % 2) + 2, :]), sig["acc_dve"])
            rms(3)
            dve.wait_ge(S["last_loaded"], 16)
            post(3, rows[:, 0, :], sig["out_cols"])


WEIGHTS = ["a_w_in", "a_w1", "a_a1", "a_w2", "a_a2", "a_w_out", "w_k_shared", "w_v_shared", "b_w_qg", "b_w_out", "b_lambda", "ln_g",
           "ln_b", "meta_2", "g_pre_mix_2", "w_in_2", "w_pool_grp_2", "w_pool_out_2", "w_conv_out_2", "w_o_2", "g_post_mix_2",
           "g_pre_mlp_2", "w_up_2", "w_down_2", "g_post_mlp_2"]


def layouts(inputs):
    def tiles(a):
        return np.asarray(a).reshape(-1, P).T
    x = np.asarray(inputs["x"])
    xT = np.zeros((P, KT, T + 1), x.dtype)
    xT[:, :, 1:] = x[0].T.reshape(KT, P, T).transpose(1, 0, 2)
    g = {k: np.asarray(v)[0] for k, v in inputs.items() if np.asarray(v).ndim > 1 and k != "meta_2"}
    v = {"mu_r": g["a_mu_proj"][0], "mu_k": g["a_mu_proj"][1], "mu_v": g["a_mu_proj"][2], "mu_g": g["a_mu_proj"][3],
         "mu_w": g["a_mu_lora"][0], "mu_a": g["a_mu_lora"][1], "w0": g["a_w0"], "a0": g["a_a0"], "k_k": g["a_k_k"],
         "k_a": g["a_k_a"], "r_k": g["a_r_k"], "gn_g": g["a_gn_g"], "gn_b": g["a_gn_b"], "subln": g["b_subln_g"],
         "g_pre_mix": g["g_pre_mix_2"], "g_pre_mlp": g["g_pre_mlp_2"], "pool_scale": g["pool_scale_2"], "b_dw": g["b_dw_2"],
         "conv_g": g["conv_ln_g_2"], "conv_b": g["conv_ln_b_2"]}
    packed = [tiles(v[n]) for n in VECTORS if n != "w_dw"]
    packed.append(g["w_dw_2"].reshape(TAPS, 8, P).transpose(2, 1, 0).reshape(P, 8 * TAPS))
    arrays = {"consts": CONSTANTS, "vectors": np.ascontiguousarray(np.concatenate(packed, 1)), "dist": distances(), "xT": xT, "x": x}
    return arrays


def kernel(**inputs):
    import concourse.bacc as _bacc
    from concourse.bass_utils import run_bass_kernel_spmd as _run

    nc = _bacc.Bacc("TRN2", target_bir_lowering=False, num_devices=1)
    arrays = {f"in_{n}": a for n, a in layouts(inputs).items()}
    for n in WEIGHTS:
        arrays[f"in_{n}"] = np.ascontiguousarray(inputs[n])
    ins = {n[3:]: nc.dram_tensor(n, a.shape, mybir.dt.from_np(a.dtype), kind="ExternalInput").ap() for n, a in arrays.items()}
    out = nc.dram_tensor("out", (1, T, C), F32, kind="ExternalOutput").ap()
    program(nc, ins, out)
    return _run(nc, [arrays], core_ids=[0]).results[0]["out"]
```

```python
from contextlib import ExitStack

import numpy as np

import concourse.bass as bass
from concourse import mybir

F32 = mybir.dt.float32
F32R = mybir.dt.float32r
ALU = mybir.AluOpType
ACT = mybir.ActivationFunctionType
AX = mybir.AxisListType

P = 128
T = 256
C = 2048
KT = C // P
HEADS, N = 32, 64
CH = 64
LORA = 96
META = 16
TM = T + META
FF = 4 * C
RING = 4
SLABS = 8
GW = 512
DECAY = float(np.exp(-0.5))
ALPHA = (2.0 * 2) ** 0.25
GN_EPS, LN_EPS, SUBLN_EPS, RMS_EPS = 64e-5, 1e-5, 1e-5, 1e-6
DH = 128
AH = 8
LAM_INIT = 0.8 - 0.6 * float(np.exp(-0.3))
TAPS = 31
FIRST_HEAD, PER = 9, 6
WINDOWS = (2, 4, 8, 16)

CONST = {}


def constants():
    p = np.arange(P)
    s, t = (p % CH)[:, None], np.arange(CH)[None, :]
    parts = {"ident": np.eye(P), "ident64": (s == t) * 1.0}
    parts["heads"] = (p[:, None] // N == p[None, :] // N) * 1.0
    parts["sel2"] = (p[:, None] // N == np.arange(2)[None, :]) * 1.0
    parts["causal"] = np.concatenate([(s < t), (s <= t)], 1) * 1.0
    for lv in range(6):
        m = 1 << lv
        parts[f"level{lv}"] = ((s // (2 * m) == t // (2 * m)) & ((t // m) % 2 == 1) & ((s // m) % 2 == 0)) * 1.0
    parts["restart"] = np.tile((np.arange(T)[None, :] % CH != 0) * 1.0, (P, 1))
    parts["ones"] = np.ones((P, P))
    at = 0
    for name, a in parts.items():
        CONST[name] = (at, a.shape[1])
        at += a.shape[1]
    return np.ascontiguousarray(np.concatenate(list(parts.values()), 1).astype(np.float32))


CONSTANTS = constants()


def distances():
    q, k = np.arange(2)[None, :, None] * P + np.arange(P)[:, None, None], np.arange(T)[None, None, :]
    return np.where(k // CH <= q // CH, -np.abs(q - k) * 1.0, -1e30).astype(np.float32)

VECTORS = {"mu_r": 16, "mu_k": 16, "mu_v": 16, "mu_g": 16, "mu_w": 16, "mu_a": 16, "w0": 16, "a0": 16, "k_k": 16,
           "k_a": 16, "r_k": 16, "gn_g": 16, "gn_b": 16, "subln": 2, "g_pre_mix": 16, "g_pre_mlp": 16,
           "pool_scale": 8, "b_dw": 8, "conv_g": 8, "conv_b": 8, "w_dw": 8 * TAPS}
VEC = {}
_at = 0
for _name, _n in VECTORS.items():
    VEC[_name] = (_at, _n)
    _at += _n
NVEC = _at


class Signal:

    def __init__(self, sem):
        self.sem, self.n = sem, 0


class Steps:

    def __init__(self, eng, sem):
        self.eng, self.own, self.past = eng, Signal(sem), []

    def do(self, ins, sig=None):
        sig = sig or self.own
        ins.then_inc(sig.sem, 1)
        sig.n += 1
        self.past.append((sig.sem, sig.n))

    def prev(self, back=1):
        self.eng.wait_ge(*self.past[-back])


def program(nc, ins, out):
    ctx = ExitStack()
    with ctx:
        def sb(name, shape, dt=F32):
            return ctx.enter_context(nc.sbuf_tensor(name, shape, dt))

        def sem(name):
            return ctx.enter_context(nc.semaphore(name))

        wraw = sb("wraw", [P, RING, 2, GW])
        whi = sb("whi", [P, RING, 2, GW], F32R)
        wlo = sb("wlo", [P, RING, 2, GW], F32R)
        cst = sb("cst", [P, CONSTANTS.shape[1]])
        vec = sb("vec", [P, NVEC])
        M = sb("M", [P, KT, N])
        gC = sb("gC", [P, KT, T // CH])
        small = sb("small", [P, 256])
        with nc.sbuf_tensor("act_hi", [P, KT, TM], F32R) as ahi, nc.sbuf_tensor("act_lo", [P, KT, TM], F32R) as alo:
            pass
        work = sb("work", [P, 2 * KT * TM])
        with nc.sbuf_tensor("regions_r", [P, 7, 4096], F32R) as RR:
            pass
        R = sb("regions", [P, 7, 4096])
        ps = ctx.enter_context(nc.psum_tensor("ps", [P, 8, 512], F32))
        bonus_dram = nc.dram_tensor("bonus_scratch", [P, KT, T], F32)
        gmix_dram = nc.dram_tensor("gate_input_scratch", [P, KT, T], F32)
        gate_dram = nc.dram_tensor("gate_scratch", [P, KT, T], F32)

        def cs(name):
            return cst[:, CONST[name][0]:CONST[name][0] + CONST[name][1]]

        def ve(name, j=None):
            a, n = VEC[name]
            return vec[:, a:a + n] if j is None else vec[:, a + j:a + j + 1]

        def bank(b, n=1):
            return ps[:, b, :] if n == 1 else ps[:, b:b + n, :].rearrange("p b n -> p (b n)")

        raw_loaded = [sem(f"raw_loaded{q}") for q in range(RING)]
        hi_ready, lo_ready, slab_used = sem("hi_ready"), sem("lo_ready"), sem("slab_used")
        names = """params_loaded x_loaded0 x_loaded1 x_loaded2 x_loaded3 w1_loaded a1_loaded lora_loaded xx_ready xa_mul
            xa_ready xa_hi xa_tmp xs_ready lora_z lora_h lora_zz lora_s1 dec_done acc_free_dve act_step dve_step
            kk_copied kk_ready gi_ready ss_done sq_ready rn_ready rnx_ready rnx_bc rk_ready rk_bc vt_mm
            v_ready bvs_ready bv_stored0 bv_stored1 bv_loaded silu_ready gate_stored gate_loaded gx_tmp gx_stored0
            gx_stored1 gx_loaded0 gx_loaded1 ab_mm ab_ready am_mm am_ready tok_mm tok_ready lv_b lv_y lv_ysb lv_z
            lv_t prep_done gn_var gn_std w_mm w_sb u_mm u_sb y_mm y_sb m_mm m_sb yn_ready zt_mm z1_ready z_ready z_f
            z_hi row_loaded out_stored x_reloaded ln_scale ln_normed ln_std ln_var turn_src turn_mm turn_hi acc_act
            acc_dve extra_loaded meta_loaded post_loaded grp_loaded last_loaded lam_ready lam_exp lam_done sc_mm
            sc_read sc_ready e_ready at_ready att_mm attT_ready o_mm ostd_ready on_ready ot_mm ot_ready zb_ready
            zb_hi x2_cols ssq ssum sstd meta_ssq meta_src meta_mm meta_f meta_hi meta_ready cv_a pool_d pool_mm
            pool_y p_hi conv_c cs_mm xc_ready sqc_ready cv_mm cvar cstd cn_ready conv_y c_hi m_ready m_hi f_sq f_hi
            f_ready y2_cols out_cols""".split()
        S = {n: sem(n) for n in names}
        block = ctx.enter_context(nc.Block())

        G0 = {}
        g_at = 0
        for name, n in (("k", 4), ("r", 4), ("v", 4), ("g", 4), ("wout", 4), ("ks", 4), ("vs", 4), ("q", 4), ("gb", 4), ("bout", 4),
                        ("cv", 4), ("pool", 2), ("gates", 8), ("pc", 4), ("wo", 4), ("up0", 8), ("down0", 8), ("up1", 8),
                        ("down1", 8)):
            G0[name] = g_at
            g_at += n
        GROUPS = g_at

        XS = {"k": 0, "r": 8, "v": 16, "g": 24, "z": 32, "ln0": 40, "z2": 44, "u1": 48, "pc": 52, "m": 56, "u2": 60}
        ACC_ACT = {"ks": 4, "vs": 8, "q": 12, "gb": 16, "cv": 20, "pool": 24, "gates": 26, "wo": 34, "up0": 38, "up1": 46}
        ACC_DVE = {"wout": 0, "bout": 4, "pc": 8, "down0": 12, "down1": 16}

        W_in = ins["a_w_in"]
        xT_ap = ins["xT"]

        xT = R[:, 0, :].rearrange("p (k t) -> p k t", k=KT)
        xx = R[:, 1, :].rearrange("p (k t) -> p k t", k=KT)
        KR = R[:, 2:4, :].rearrange("p a n -> p (a n)").rearrange("p (j a t) -> p j a t", j=KT, a=2)
        Bc = R[:, 4, :].rearrange("p (k t) -> p k t", k=KT)
        Kc = R[:, 5, :].rearrange("p (k t) -> p k t", k=KT)
        V = R[:, 6, :].rearrange("p (c j n) -> p c j n", c=4, j=KT)
        vtmp = [R[:, 1, 1024 * i:1024 * (i + 1)] for i in range(4)]
        tmpA = [R[:, 6, 1024 * i:1024 * (i + 1)] for i in range(4)]
        w1s = R[:, 5, 0:2 * KT * LORA].rearrange("p (a k n) -> p a k n", a=2, k=KT)
        w2s = R[:, 6, :].rearrange("p (a n) -> p a n", a=2)
        xa = [R[:, 5, 3072 + i * T:3072 + (i + 1) * T] for i in range(4)]
        hw = [KR[:, KT - 1 - i, 1, :] for i in range(2)]

        rstd, nbias = small[:, 246:248], small[:, 248:250]
        mv = small[:, 240:244].rearrange("p (b a) -> p b a", b=2)
        H = R[:, 4, :].rearrange("p (b n) -> p b n", b=2)
        xre = R[:, 5, :].rearrange("p (b n) -> p b n", b=2)
        gT = R[:, 2, :].rearrange("p (k t) -> p k t", k=KT)
        rows = R[:, 6, :].rearrange("p (a n) -> p a n", a=2)
        bvT = R[:, 3, :].rearrange("p (k t) -> p k t", k=KT)
        zt = [R[:, 0, 512 * i:512 * (i + 1)] for i in range(4)]
        def wk(at, n):
            return work[:, at:at + n]
        TTs = R[:, 0, :].rearrange("p (c n) -> p c n", c=4)
        AB, Bm, Tm, Yl = (R[:, 1, 1024 * i:1024 * (i + 1)] for i in range(4))
        AM = wk(0, 3072).rearrange("p (j a t) -> p j a t", j=KT, a=3)
        BKt = wk(3072, 2048).rearrange("p (a n) -> p a n", a=2)
        Wt, U, gsq = wk(5120, 1024), wk(6144, 1024), wk(7168, 1024)
        Yn = R[:, 1, :].rearrange("p (c n) -> p c n", c=4)
        gate = M[:].rearrange("p k n -> p (k n)")

        level_steps = [("ab", 0, 0, 0), ("ab", 0, 1, 0)]
        for c in range(4):
            level_steps += [("y", c, 0, 0), ("y", c, 1, 0)]
            for lv in range(1, 6):
                level_steps += [("y", c, 0, lv), ("y", c, 1, lv)]
                for f in range(2):
                    level_steps += [("z", c, f, lv)] * (lv < 5) + [("zt", c, f, lv)] + [("ab", c + 1, f, 0)] * (lv == 5 and c < 3)
        steps_at, at_ = [], 0
        for h in range(2 * 4 * SLABS):
            n_ = 0 if h < 7 else 2
            steps_at.append(level_steps[at_:at_ + n_])
            at_ += n_
        steps_at.append(level_steps[at_:])

        def beside(h, do):
            for e in steps_at[h + 1] + (steps_at[h + 2] if h + 2 < len(steps_at) - 1 else []):
                do(*e)

        four_k = lambda r: R[:, r, :].rearrange("p (k t) -> p k t", k=KT)
        qT, kT, gbT = four_k(0), four_k(1), four_k(3)
        vS = R[:, 2, :].rearrange("p (b n) -> p b n", b=2)
        a5 = lambda at, n: R[:, 5, at:at + n]
        sc = a5(0, 768).rearrange("p (m k) -> p m k", m=2)
        es = a5(768, 768).rearrange("p (m k) -> p m k", m=2)
        attn, attT, t1, dist, On = a5(1536, 384), a5(1920, 384), a5(2304, 384), a5(2688, 384), a5(3072, 512)
        lam = a5(3584, 512).rearrange("p (a n) -> p a n", a=4)
        osq = a5(3584, 256)
        sm = lambda at, n: small[:, 64 + at:64 + at + n]
        mx, nmx, rsum, rrec, oss, ostd, orstd = sm(0, 4), sm(4, 4), sm(8, 4), sm(12, 4), sm(16, 2), sm(18, 2), sm(20, 2)
        sub1, nlam, lsum, lexp, eps5, eps6 = sm(22, 2), sm(24, 1), sm(26, 2), sm(28, 2), sm(30, 1), sm(31, 1)
        ssr = sm(32, 8).rearrange("p (b c) -> p b c", b=2)
        rsm, rstd_, rrstd, mss, mstd, mrstd = sm(40, 2), sm(42, 2), sm(44, 2), sm(46, 1), sm(47, 1), sm(48, 1)
        junk = M[:].rearrange("p k n -> p (k n)")
        rowsB = R[:, 2, :].rearrange("p (a n) -> p a n", a=2)
        src = R[:, 5, :].rearrange("p (b n) -> p b n", b=2)
        metaS = R[0:META, 1, 0:C]
        metaU = R[:, 1, C:C + KT * META].rearrange("p (k t) -> p k t", k=KT)
        sa, sgb, mT = four_k(0), four_k(1), four_k(2)
        PAD = TAPS - 1 - META
        A2 = R[:, 2, 0:8 * (PAD + TM)].rearrange("p (j t) -> p j t", j=8)
        ctmp = R[:, 2, 8 * (PAD + TM):8 * (PAD + TM) + 4 * TM].rearrange("p (b t) -> p b t", b=4)
        cc = R[:, 3, 0:8 * T].rearrange("p (j t) -> p j t", j=8)
        csq = [R[:, 2, 2304 + 512 * i:2304 + 512 * (i + 1)].rearrange("p (j t) -> p j t", j=2) for i in range(2)]
        cmean, crstd = R[:, 2, 3328:3584], R[:, 2, 3584:3840]
        wgrp = R[:, 3, 2048:4096].rearrange("p (g n) -> p g n", g=8)
        pz = R[:, 5, 0:8 * TM].rearrange("p (j t) -> p j t", j=8)
        pt = [R[:, 5, 8 * TM + 2 * TM * i:8 * TM + 2 * TM * (i + 1)].rearrange("p (j t) -> p j t", j=2) for i in range(3)]
        mtmp = [R[:, 3, 1024 * i:1024 * (i + 1)] for i in range(2)]
        fhi = RR[:, 0:2, :].rearrange("p a (k t) -> p (a k) t", t=T)
        flo = RR[:, 2:4, :].rearrange("p a (k t) -> p (a k) t", t=T)
        frel = [R[:, 6, 2048 + 1024 * i:3072 + 1024 * i] for i in range(2)]
        fsq = junk
        yS = src

        def xtmp(u):
            return M[:].rearrange("p k n -> p (k n)")[:, (u % 2) * 2 * T:(u % 2 + 1) * 2 * T].rearrange("p (k t) -> p k t", k=2)

        def split_hi(act, G, q):
            act.wait_ge(raw_loaded[q % RING], 16 * (2 * G + 1 + q // RING))
            if not (isinstance(G, int) and G == 0 and q < RING):
                act.wait_ge(slab_used, SLABS * G + q - RING + 1)
            nc.scalar.activation(whi[:, q % RING], wraw[:, q % RING], ACT.Copy).then_inc(hi_ready, 1)

        def split_lo(dve, G, q):
            dve.wait_ge(hi_ready, SLABS * G + q + 1)
            nc.vector.tensor_tensor(wlo[:, q % RING], wraw[:, q % RING], whi[:, q % RING].bitcast(F32),
                                    ALU.subtract).then_inc(lo_ready, 1)

        def group_slabs(eng, split, G, hook=None, slabs=SLABS):
            for u in range(slabs):
                g, q = (G, RING + u) if u < RING else (G + 1, u - RING)
                if not isinstance(g, int) or g < GROUPS:
                    split(eng, g, q)
                if hook:
                    hook(u)

        @block.sync
        def _(sp):
            sp.dma_start(cst[:], ins["consts"]).then_inc(S["params_loaded"], 16)
            sp.dma_start(vec[:], ins["vectors"]).then_inc(S["params_loaded"], 16)
            sp.dma_start(w1s[:, 0], ins["a_w1"][0].rearrange("(k p) n -> p k n", p=P)).then_inc(S["w1_loaded"], 16)
            for i in range(4):
                k4 = slice(4 * i, 4 * i + 4)
                sp.dma_start(xT[:, k4, :], xT_ap[:, k4, 1:T + 1]).then_inc(S[f"x_loaded{i}"], 16)
                sp.dma_start(xx[:, k4, :], xT_ap[:, k4, 0:T]).then_inc(S[f"x_loaded{i}"], 16)
            sp.dma_start(w1s[:, 1], ins["a_a1"][0].rearrange("(k p) n -> p k n", p=P)).then_inc(S["a1_loaded"], 16)
            for i, n in enumerate(("a_w2", "a_a2")):
                sp.dma_start(w2s[0:LORA, i, :], ins[n][0]).then_inc(S["lora_loaded"], 16)

            def load_group(G, w, col, first=False, w_rest=None):
                v = w.rearrange("(k p) n -> p k n", p=P)
                for q in range(SLABS):
                    k = 2 * q
                    if w_rest is not None and q == SLABS // 2:
                        v = w_rest.rearrange("(k p) n -> p k n", p=P)
                    if w_rest is not None and q >= SLABS // 2:
                        k = 2 * q - SLABS
                    if not (first and q < RING):
                        sp.wait_ge(lo_ready, SLABS * G + q - RING + 1)
                    sp.dma_start(wraw[:, q % RING], v[:, k:k + 2, bass.ds(col, GW)]).then_inc(raw_loaded[q % RING], 16)

            load_group(0, W_in[0, 1], 0, first=True)
            with sp.Fori(1, 4) as i:
                load_group(i, W_in[0, 1], i * GW)
            for name, w in (("r", W_in[0, 0]), ("v", W_in[0, 2]), ("g", W_in[0, 3]), ("wout", ins["a_w_out"][0])):
                with sp.Fori(0, 4) as i:
                    load_group(i + G0[name], w, i * GW)
            w_in2 = ins["w_in_2"][0]
            for name, w, col0, n in (("ks", ins["w_k_shared"], 0, 4), ("vs", ins["w_v_shared"], 0, 4), ("q", ins["b_w_qg"][0], 0, 4),
                                     ("gb", ins["b_w_qg"][0], C, 4), ("bout", ins["b_w_out"][0], 0, 4),
                                     ("cv", w_in2, C // 2, 4), ("pool", w_in2, 0, 2), ("gates", w_in2, 3 * C // 2, 8)):
                with sp.Fori(0, n) as i:
                    load_group(i + G0[name], w, i * GW + col0)
            with sp.Fori(0, 4) as i:
                load_group(i + G0["pc"], ins["w_pool_out_2"][0], i * GW, w_rest=ins["w_conv_out_2"][0])
            with sp.Fori(0, 4) as i:
                load_group(i + G0["wo"], ins["w_o_2"][0], i * GW)
            for half in range(2):
                with sp.Fori(0, 8) as i:
                    load_group(i + G0[f"up{half}"], ins["w_up_2"][0], i * GW + half * FF // 2)
                with sp.Fori(0, 4) as i:
                    for quarter in range(2):
                        r0 = half * FF // 2 + quarter * C
                        load_group(2 * i + G0[f"down{half}"] + quarter, ins["w_down_2"][0, r0:r0 + C, :], i * GW)
            for c in range(4):
                cols = slice(c * GW, (c + 1) * GW)
                sp.wait_ge(S["out_cols"], c + 1)
                sp.dma_start(out.rearrange("o (b p) n -> p (o b) n", p=P)[:, :, cols], H[:, :, cols]).then_inc(S["out_stored"], 16)
            sp.wait_ge(S["out_stored"], 64)

        @block.gpsimd
        def _(pool):
            ptt = nc.gpsimd.tensor_tensor

            def mix(n_, u, mu, free, done):
                if n_ >= 2:
                    pool.wait_ge(S["xs_ready"], free)
                if n_ < SLABS:
                    pool.wait_ge(S["xx_ready"], u // 2 + 1)
                k2 = slice(2 * u, 2 * u + 2)
                ptt(xtmp(u), xx[:, k2, :], ve(mu)[:, k2].unsqueeze(2).broadcast_to([P, 2, T]), ALU.mult).then_inc(S["xa_mul"], 1)
                pool.wait_ge(S["xa_mul"], n_ + 1)
                ptt(xtmp(u), xtmp(u), xT[:, k2, :], ALU.add).then_inc(done, 1)

            for stage, mu in ((0, "mu_k"), (1, "mu_r")):
                for u in range(SLABS):
                    mix(SLABS * stage + u, u, mu, SLABS * stage + u - 1, S["xa_tmp"])
            for u in range(SLABS):
                if u >= 2:
                    pool.wait_ge(S[f"gx_stored{u % 2}"], 16 * (u // 2))
                mix(2 * SLABS + u, u, "mu_g", 2 * SLABS, S["gx_tmp"])
                pool.wait_ge(S["gx_tmp"], u + 1)
                pool.dma_start(gmix_dram[:, 2 * u:2 * u + 2, :], xtmp(u)).then_inc(S[f"gx_stored{u % 2}"], 16)
            pool.wait_ge(S["gx_stored0"], 64)
            pool.wait_ge(S["gx_stored1"], 64)
            for u in range(SLABS):
                mix(3 * SLABS + u, u, "mu_v", 2 * SLABS + u - 1 if u >= 2 else 2 * SLABS, S["xa_tmp"])
            for u in range(SLABS):
                pool.wait_ge(S["xs_ready"], XS["g"] + u - 1)
                pool.dma_start(xtmp(u), gmix_dram[:, 2 * u:2 * u + 2, :]).then_inc(S[f"gx_loaded{u % 2}"], 16)
            for c in range(4):
                for lv in range(6):
                    for f in range(2):
                        n_ = (c * 6 + lv) * 2 + f
                        if lv == 0:
                            pool.wait_ge(S["ab_ready"], 2 * c + f + 1)
                        if n_ >= 2:
                            pool.wait_ge(S["lv_y"], n_ - 1)
                        if lv == 1:
                            pool.wait_ge(S["lv_t"], n_ - 1)
                        fs = slice(f * GW, (f + 1) * GW)
                        ptt(Bm[:, fs].rearrange("p (h t) -> p h t", h=8), AB[:, fs].rearrange("p (h t) -> p h t", h=8),
                            cs(f"level{lv}").unsqueeze(1).broadcast_to([P, 8, CH]), ALU.mult).then_inc(S["lv_b"], 1)
            pool.wait_ge(S["y_mm"], 8)
            pool.wait_ge(S["bv_stored0"], 32)
            pool.wait_ge(S["bv_stored1"], 32)
            pool.wait_ge(S["gate_stored"], 64)
            pool.dma_start(gT, gate_dram[:, :, :]).then_inc(S["gate_loaded"], 16)
            pool.dma_start(bvT, bonus_dram[:, :, :]).then_inc(S["bv_loaded"], 16)
            pool.dma_start(xre, ins["x"][0].rearrange("(b p) n -> p b n", p=P)).then_inc(S["x_reloaded"], 16)
            for i, n in enumerate(("ln_g", "ln_b")):
                pool.dma_start(rows[:, i, :], ins[n][0:1, :].broadcast_to([P, C])).then_inc(S["row_loaded"], 16)
            pool.wait_ge(S["acc_dve"], 4)
            pool.dma_start(lam, ins["b_lambda"][0:1].rearrange("o a n -> o (a n)").broadcast_to([P, 512]).rearrange("p (a n) -> p a n", a=4)).then_inc(S["extra_loaded"], 16)
            pool.dma_start(dist[:, 0:T], ins["dist"][:, 1, :]).then_inc(S["extra_loaded"], 16)
            pool.dma_start(dist[:, T:T + P], ins["dist"][:, 0, 0:P]).then_inc(S["extra_loaded"], 16)
            pool.wait_ge(S["turn_src"], 4)
            for i, n in enumerate(("ln_g", "ln_b")):
                pool.dma_start(rows[:, i, :], ins[n][1:2, :].broadcast_to([P, C])).then_inc(S["row_loaded"], 16)
            pool.wait_ge(S["o_mm"], AH)
            pool.dma_start(rowsB[:, 0, :], ins["g_pre_mix_2"][0:1, :].broadcast_to([P, C])).then_inc(S["meta_loaded"], 16)
            pool.dma_start(rowsB[0:META, 1, :], ins["meta_2"]).then_inc(S["meta_loaded"], 16)
            pool.wait_ge(S["x2_cols"], 4)
            for i, n in enumerate(("g_post_mix_2", "g_pre_mlp_2")):
                pool.dma_start(rows[:, i, :], ins[n][0:1, :].broadcast_to([P, C])).then_inc(S["post_loaded"], 16)
            pool.wait_ge(S["xs_ready"], XS["u1"])
            pool.dma_start(wgrp, ins["w_pool_grp_2"][0].rearrange("g (i p) n -> p (g i) n", p=P)).then_inc(S["grp_loaded"], 16)
            pool.wait_ge(S["turn_src"], 12)
            pool.dma_start(rows[:, 0, :], ins["g_post_mlp_2"][0:1, :].broadcast_to([P, C])).then_inc(S["last_loaded"], 16)

        @block.tensor
        def _(pe):
            mm = nc.tensor.matmul
            def three(o, hi_s, lo_s, hi_m, lo_m, first, last, sig=None):
                mm(o, hi_s, hi_m, start=first, stop=False, skip_group_check=True)
                mm(o, hi_s, lo_m, start=False, stop=False, skip_group_check=True)
                i = mm(o, lo_s, hi_m, start=False, stop=last, skip_group_check=True)
                if sig:
                    i.then_inc(sig, 1)

            def ws_group(G, outs, n, xh, xl, x_ready=None, hook=None, half_hook=None):
                for q in range(SLABS):
                    pe.wait_ge(lo_ready, SLABS * G + q + 1)
                    for kk in range(2):
                        if x_ready:
                            pe.wait_ge(S["xs_ready"], x_ready(2 * q + kk))
                        for b in range(4):
                            c = slice(b * P, (b + 1) * P)
                            o, opens = outs[b]
                            three(o, whi[:, q % RING, kk, c], wlo[:, q % RING, kk, c], xh[:, 2 * q + kk, 0:n],
                                  xl[:, 2 * q + kk, 0:n], first=q == 0 and kk == 0 and opens,
                                  last=q == SLABS - 1 and kk == 1,
                                  sig=slab_used if kk == 1 and b == 3 else None)
                        if half_hook:
                            half_hook(2 * q + kk)
                    if hook:
                        hook(q)

            def wm_group(G, outs, xh, xl, first=True, last=True, x_ready=None, k0=0, hook=None, ready=S["xs_ready"]):
                for q in range(SLABS):
                    pe.wait_ge(lo_ready, SLABS * G + q + 1)
                    for kk in range(2):
                        k = k0 + 2 * q + kk
                        if x_ready:
                            pe.wait_ge(ready, x_ready(k))
                        for tb in range(2):
                            c = slice(tb * P, (tb + 1) * P)
                            three(outs[tb], xh[:, k, c], xl[:, k, c], whi[:, q % RING, kk], wlo[:, q % RING, kk],
                                  first=first and q == 0 and kk == 0, last=last and q == SLABS - 1 and kk == 1,
                                  sig=slab_used if kk == 1 and tb == 1 else None)
                    if hook:
                        hook(q)

            def packed(b0):
                return [(ps[:, b0 + b // 2, (b % 2) * T:(b % 2 + 1) * T], b % 2 == 0) for b in range(4)]

            def turn(i, xs0, H):
                for c in range(4):
                    pe.wait_ge(S["turn_src"], 4 * i + c + 1)
                    if c >= 2:
                        pe.wait_ge(S["xs_ready"], xs0 + c - 1)
                    for k in range(4 * c, 4 * c + 4):
                        for tb in range(2):
                            m_ = nc.tensor.transpose(ps[:, 4 + 2 * (c % 2) + (k % 4) // 2, (k % 2) * T + tb * P:][:, 0:P],
                                                     H[:, tb, k * P:(k + 1) * P], cs("ident"))
                    m_.then_inc(S["turn_mm"], 1)

            for i in range(2):
                pe.wait_ge(S[("w1_loaded", "a1_loaded")[i]], 16)
                for k in range(KT):
                    pe.wait_ge(S["xa_ready"], KT * i + k + 1)
                    m_ = mm(ps[0:LORA, 6 + i, 0:T], w1s[:, i, k, :], xa[(KT * i + k) % 4],
                            start=(k == 0), stop=(k == KT - 1))
                    m_.then_inc(S["lora_z"], 1)
            pe.wait_ge(S["lora_loaded"], 32)
            for i in range(2):
                pe.wait_ge(S["lora_h"], i + 1)
                for j2 in range(KT // 2):
                    u = 8 * i + j2
                    if u >= 4:
                        pe.wait_ge(S["lora_s1"], 2 * (u - 3))
                    for j in (2 * j2, 2 * j2 + 1):
                        m_ = mm(ps[:, u % 4, (j % 2) * T:(j % 2 + 1) * T], w2s[0:LORA, i, j * P:(j + 1) * P],
                                hw[i][0:LORA, :], start=True, stop=True)
                    m_.then_inc(S["lora_zz"], 1)
            pe.wait_ge(S["lora_s1"], 32)

            def ss(g):
                def hook(q):
                    if q != 1:
                        return
                    pe.wait_ge(S["sq_ready"], g + 1)
                    for b in range(4):
                        for tb in range(2):
                            m_ = mm(ps[:, 6, tb * HEADS + 8 * g + 2 * b:][:, 0:2],
                                    tmpA[1][:, b * T + tb * P:b * T + (tb + 1) * P], cs("sel2"), start=True, stop=True)
                    m_.then_inc(S["ss_done"], 1)
                return hook
            for s in range(4):
                if s >= 2:
                    pe.wait_ge(S["kk_ready"], s - 1)
                    pe.wait_ge(S["acc_free_dve"], s - 1)
                ws_group(G0["k"] + s, packed(2 * (s % 2)), T, ahi, alo, (lambda k: k // 2 + 1) if s == 0 else None,
                         ss(s - 1) if s else None)
            def bc(g):
                def hook(q):
                    if q == 1:
                        pe.wait_ge(S["rnx_ready"], g + 1)
                        for b in range(4):
                            for tb in range(2):
                                m_ = nc.tensor.transpose(ps[:, 4 + b // 2, (b % 2) * T + tb * P:][:, 0:P],
                                                         tmpA[0][:, (tb * 4 + b) * P:(tb * 4 + b + 1) * P], cs("ident"))
                        m_.then_inc(S["rnx_bc"], 1)
                return hook
            for s in range(4):
                if s < 2:
                    pe.wait_ge(S["kk_ready"], 3 + s)
                    pe.wait_ge(S["acc_free_dve"], 3 + s)
                    hook = ss(3) if s == 0 else bc(0)
                else:
                    pe.wait_ge(S["acc_free_dve"], 4 + s - 1)
                    hook = bc(s - 1)
                ws_group(G0["r"] + s, packed(2 * (s % 2)), T, ahi, alo, (lambda k: XS["r"] + k // 2 + 1) if s == 0 else None, hook)
            def vt(g):
                def hook(q):
                    if q == 1:
                        pe.wait_ge(S["acc_act"], g + 1)
                        if g:
                            pe.wait_ge(S["v_ready"], g)
                        for b in range(4):
                            for c in range(4):
                                for hs in (0, N):
                                    o = ps[hs:hs + N, 4 + b // 2, ((b % 2) * 4 + c) * N:((b % 2) * 4 + c + 1) * N]
                                    m_ = mm(o, vtmp[0][hs:hs + N, b * T + c * CH:b * T + (c + 1) * CH],
                                            cs("ident64")[hs:hs + N, :], start=True, stop=True)
                        m_.then_inc(S["vt_mm"], 1)
                    if q == 3:
                        pe.wait_ge(S["rk_ready"], g + 1)
                        if g:
                            pe.wait_ge(S["bvs_ready"], g)
                        for b in range(4):
                            m_ = mm(ps[:, 6 + b // 2, (b % 2) * T:(b % 2 + 1) * T], cs("heads"), vtmp[1][:, b * T:(b + 1) * T],
                                    start=True, stop=True)
                        m_.then_inc(S["rk_bc"], 1)
                return hook
            for s in range(4):
                if s < 2:
                    pe.wait_ge(S["acc_free_dve"], 4 + 3 + s)
                else:
                    pe.wait_ge(S["acc_act"], s - 1)
                ws_group(G0["v"] + s, packed(2 * (s % 2)), T, ahi, alo, (lambda k: XS["v"] + k // 2 + 1) if s == 0 else None,
                         vt(s - 1) if s else bc(3))

            def pairs(f, o_bank, *terms):
                for j in range(8 * f, 8 * f + 8):
                    for hs in (0, N):
                        r_ = slice(hs, hs + N)
                        for n_, (lhs, rhs) in enumerate(terms):
                            m_ = mm(ps[r_, o_bank, (j % 8) * N:(j % 8 + 1) * N], lhs(r_, j), rhs(r_, j), start=n_ == 0,
                                    stop=n_ == len(terms) - 1)
                return m_
            flat = lambda t_: lambda r_, j: t_[r_, j * N:(j + 1) * N]
            eye = lambda r_, j: cs("ident64")[r_, :]

            def level(kind, c, f, lv):
                n_, m_ = (c * 6 + lv) * 2 + f, (c * 5 + lv - 1) * 2 + f
                ts = slice(c * CH, (c + 1) * CH)
                if kind == "ab":
                    if c:
                        pe.wait_ge(S["lv_ysb"], 10 * c - 1 + f)
                    else:
                        pe.wait_ge(S["v_ready"], 4)
                        pe.wait_ge(S["prep_done"], 1)
                    pairs(f, 4 + f, (lambda r_, j: Bc[r_, j, ts], lambda r_, j: KR[r_, j, 0, ts])).then_inc(S["ab_mm"], 1)
                if kind == "y":
                    pe.wait_ge(S["lv_b"], n_ + 1)
                    if lv:
                        pe.wait_ge(S["lv_t"], n_ - 1)
                    pairs(f, 4 + f, (flat(Bm), flat(Tm) if lv else eye)).then_inc(S["lv_y"], 1)
                if kind in ("z", "zt"):
                    pe.wait_ge(S["lv_ysb"], m_ + 1)
                    pe.wait_ge(S["lv_t"], n_)
                if kind == "z":
                    pairs(f, 6, (flat(TTs[:, c]), flat(Yl)))
                if kind == "zt":
                    pairs(f, 7, (flat(Yl), flat(TTs[:, c]))).then_inc(S["lv_z"], 1)

            for s in range(4):
                if s < 2:
                    pe.wait_ge(S["acc_act"], 3 + s)
                else:
                    pe.wait_ge(S["silu_ready"], s - 1)
                ws_group(G0["g"] + s, packed(2 * (s % 2)), T, ahi, alo, (lambda k: XS["g"] + k // 2 + 1) if s == 0 else None,
                         vt(3) if s == 0 else None, lambda h, s=s: [level(*e) for e in steps_at[16 * s + h]])
            for e in steps_at[-1]:
                level(*e)

            pe.wait_ge(S["bvs_ready"], 4)
            pe.wait_ge(S["silu_ready"], 4)
            pe.wait_ge(S["lv_t"], 48)
            for it in range(4):
                ts = slice(it * CH, (it + 1) * CH)
                for u, (kind, n_, b) in enumerate((("K", 0, 2), ("K", 1, 3), ("B", 0, 0), ("B", 1, 1), ("K", 2, 2), ("K", 3, 3))):
                    if u >= 4:
                        pe.wait_ge(S["am_ready"], 6 * it + u - 3)
                    if kind == "K":
                        for j in range(4 * n_, 4 * n_ + 4):
                            for hs in (0, N):
                                m_ = mm(ps[hs:hs + N, b, (j % 4) * P:(j % 4 + 1) * P].rearrange("p (a t) -> p a t", a=2),
                                        Kc[hs:hs + N, j, ts], KR[hs:hs + N, j, :, ts], start=True, stop=True)
                    else:
                        m_ = pairs(n_, b, (lambda r_, j: Bc[r_, j, ts], lambda r_, j: KR[r_, j, 1, ts]))
                    m_.then_inc(S["am_mm"], 1)
                for u in range(4 if it < 3 else 0):
                    pe.wait_ge(S["am_ready"], 6 * it + u + 3)
                    src_ = (Bc, Kc)[u // 2]
                    pairs(u % 2, u, (lambda r_, j: src_[r_, j, ts], eye)).then_inc(S["tok_mm"], 1)

                am = lambda a_: lambda r_, j: AM[r_, j, a_, :]
                hat = lambda a_: lambda r_, j: KR[r_, j, a_, ts]
                state = lambda r_, j: M[r_, j, :]
                value = lambda r_, j: V[r_, it, j, :]
                tok = lambda a_: lambda r_, j: BKt[r_, a_, j * N:(j + 1) * N]
                if it:
                    pe.wait_ge(S["m_sb"], 2 * it)
                for f in range(2):
                    if it < 3:
                        pe.wait_ge(S["tok_ready"], 4 * it + f + 1)
                    else:
                        pe.wait_ge(S["am_ready"], 6 * it + 6)
                    terms = ([(hat(0), state)] if it else []) + [(am(1), value)]
                    pairs(f, f, *terms).then_inc(S["w_mm"], 1)
                if it < 3:
                    pe.wait_ge(S["tok_ready"], 4 * it + 4)
                for f in range(2):
                    pe.wait_ge(S["w_sb"], 2 * it + f + 1)
                    pairs(f, 2 + f, (flat(TTs[:, it]), flat(Wt))).then_inc(S["u_mm"], 1)
                for f in range(2):
                    pe.wait_ge(S["u_sb"], 2 * it + f + 1)
                    if it:
                        pe.wait_ge(S["y_sb"], 2 * it - 1 + f)
                    terms = ([(hat(1), state)] if it else []) + [(am(0), flat(U)), (am(2), value)]
                    pairs(f, 4 + f, *terms).then_inc(S["y_mm"], 1)
                    if it < 3:
                        pairs(f, 6 + f, (tok(0), flat(U)), (tok(1), value)).then_inc(S["m_mm"], 1)

            for j2 in range(8):
                pe.wait_ge(S["yn_ready"], 4 + j2 // 4)
                if j2 >= 4:
                    pe.wait_ge(S["z1_ready"], j2 - 3)
                for j in (2 * j2, 2 * j2 + 1):
                    for c in range(4):
                        for hs in (0, N):
                            m_ = mm(ps[hs:hs + N, 4 + j2 % 4, (j % 2) * T + c * CH:(j % 2) * T + (c + 1) * CH],
                                    Yn[hs:hs + N, c, j * N:(j + 1) * N], cs("ident64")[hs:hs + N, :], start=True, stop=True)
                m_.then_inc(S["zt_mm"], 1)

            def wm_stage(name, x_ready):
                for s in range(4):
                    if s >= 2:
                        pe.wait_ge(S["acc_dve"], s - 1)
                    wm_group(G0[name] + s, [bank(2 * (s % 2)), bank(2 * (s % 2) + 1)], ahi, alo, x_ready=x_ready if s == 0 else None)
            wm_stage("wout", lambda k: XS["z"] + k // 2 + 1)
            turn(0, XS["ln0"], H)
            four_each = lambda name: lambda k: XS[name] + k // 4 + 1

            def ws_four(name, x_ready=None):
                with pe.Fori(0, 2) as i:
                    for s in range(2):
                        pe.wait_ge(acc_act, 2 * i + (ACC_ACT[name] + s - 1))
                        ws_group(2 * i + (G0[name] + s), packed(2 * s), T, ahi, alo, x_ready)

            acc_act, acc_dve = S["acc_act"], S["acc_dve"]
            pe.wait_ge(acc_dve, 4)
            ws_four("ks", four_each("ln0"))
            with pe.Fori(0, 2) as i:
                for s in range(2):
                    pe.wait_ge(acc_act, 2 * i + (ACC_ACT["vs"] + s - 1))
                    wm_group(2 * i + (G0["vs"] + s), [bank(2 * s), bank(2 * s + 1)], ahi, alo)
            def att(t):
                for h in range(AH):
                    if t == FIRST_HEAD + PER * h + 10:
                        pe.wait_ge(S["on_ready"], h + 1)
                        for e in range(2):
                            for i in range(2):
                                m_ = nc.tensor.transpose(ps[:, 7, e * T + (1 - i) * P:][:, 0:P],
                                                         On[:, i * T + e * P:i * T + (e + 1) * P], cs("ident"))
                        m_.then_inc(S["ot_mm"], 1)
                    if t == FIRST_HEAD + PER * h + 7:
                        pe.wait_ge(S["attT_ready"], h + 1)
                        if h:
                            pe.wait_ge(S["ot_ready"], h)
                        for i, kb, first, last in ((0, 0, True, False), (0, 1, False, True), (1, 0, True, True)):
                            m_ = mm(ps[:, 7, i * T:(i + 1) * T], attT[:, (2 * i + kb) * P:(2 * i + kb + 1) * P],
                                    vS[:, kb, h * T:(h + 1) * T], start=first, stop=last)
                        m_.then_inc(S["o_mm"], 1)
                    if t == FIRST_HEAD + PER * h + 5:
                        pe.wait_ge(S["at_ready"], h + 1)
                        if h:
                            pe.wait_ge(S["attT_ready"], h)
                        for n_ in range(3):
                            m_ = nc.tensor.transpose(ps[:, 6, n_ * P:(n_ + 1) * P], attn[:, n_ * P:(n_ + 1) * P], cs("ident"))
                        m_.then_inc(S["att_mm"], 1)
                    if t == FIRST_HEAD + PER * h:
                        pe.wait_ge(acc_act, ACC_ACT["q"] + h // 2 + 1)
                        if h:
                            pe.wait_ge(S["sc_read"], h)
                        for m in range(2):
                            mm(ps[:, 4 + m, 0:T], qT[:, 2 * h + m, P:T], kT[:, 2 * h + m, :], start=True, stop=True)
                            m_ = mm(ps[:, 4 + m, T:T + P], qT[:, 2 * h + m, 0:P], kT[:, 2 * h + m, 0:P], start=True, stop=True)
                        m_.then_inc(S["sc_mm"], 1)
            for s in range(8):
                pe.wait_ge(acc_act, ACC_ACT["q"] + s - 1)
                ws_group(G0["q"] + s, packed(2 * (s % 2)), T, ahi, alo, None, lambda q, s=s: att(8 * s + q))

            def meta(q):
                if q == 1:
                    pe.wait_ge(S["meta_src"], 1)
                    for k in range(KT):
                        m_ = nc.tensor.transpose(ps[:, 4, k * META:(k + 1) * META], metaS[:, k * P:(k + 1) * P],
                                                 cs("ident")[0:META, 0:META])
                    m_.then_inc(S["meta_mm"], 1)
            for s in range(4):
                if s < 2:
                    pe.wait_ge(acc_act, ACC_ACT["gb"] + 3 + s)
                else:
                    pe.wait_ge(acc_dve, ACC_DVE["bout"] + s - 1)
                wm_group(G0["bout"] + s, [bank(2 * (s % 2)), bank(2 * (s % 2) + 1)], ahi, alo, x_ready=four_each("z2") if s == 0 else None,
                         hook=meta if s == 2 else None)
            turn(1, XS["u1"], src)

            wide = lambda p: [(ps[:, 4 * p + b, 0:TM], True) for b in range(4)]
            pe.wait_ge(acc_dve, ACC_DVE["bout"] + 4)
            pe.wait_ge(S["meta_ready"], 1)
            for n_, (name, s) in enumerate((("cv", 0), ("cv", 1), ("cv", 2), ("cv", 3), ("pool", 0), ("pool", 1))):
                if n_ >= 2:
                    pe.wait_ge(acc_act, ACC_ACT["cv"] + n_ - 1)
                ws_group(G0[name] + s, wide(n_ % 2), TM, ahi, alo, four_each("u1") if n_ == 0 else None)

            def pool_map(q):
                if q != 1:
                    return
                pe.wait_ge(S["grp_loaded"], 16)
                pe.wait_ge(acc_act, ACC_ACT["pool"] + 2)
                pe.wait_ge(S["pool_d"], 1)
                for g in range(4):
                    for e in range(2):
                        for i in range(2):
                            m_ = mm(ps[:, 4 + g, e * T:(e + 1) * T], wgrp[:, 2 * g + i, e * P:(e + 1) * P],
                                    pz[:, 2 * g + i, META:TM], start=i == 0, stop=i == 1)
                m_.then_inc(S["pool_mm"], 1)
            def conv_norm(t):
                if t == 3:
                    pe.wait_ge(S["conv_c"], 8)
                    pe.wait_ge(S["pool_y"], 4)
                    for j in range(8):
                        m_ = mm(ps[:, 6, 0:T], cs("ones"), cc[:, j, :], start=j == 0, stop=j == 7)
                    m_.then_inc(S["cs_mm"], 1)
                if t in (7, 8, 9, 10):
                    u = t - 7
                    pe.wait_ge(S["sqc_ready"], u + 1)
                    for j in range(2):
                        m_ = mm(ps[:, 7, 0:T], cs("ones"), csq[u % 2][:, j, :], start=u + j == 0, stop=u == 3 and j == 1)
                    m_.then_inc(S["cv_mm"], 1)
            for s in range(8):
                pe.wait_ge(acc_act, ACC_ACT["gates"] + s - 1)
                ws_group(G0["gates"] + s, packed(2 * (s % 2)), T, ahi, alo, None,
                         pool_map if s == 2 else (lambda q, s=s: conv_norm(8 * (s - 6) + q)) if s >= 6 else None)

            for s in range(4):
                if s == 0:
                    pe.wait_ge(acc_act, ACC_ACT["gates"] + 7)
                    pe.wait_ge(S["cstd"], 1)
                elif s > 1:
                    pe.wait_ge(acc_dve, ACC_DVE["pc"] + s - 1)
                b0 = 4 * (s % 2)
                for part in range(2):
                    if s == 0 and part:
                        pe.wait_ge(acc_act, ACC_ACT["gates"] + 8)
                    for q in range(4 * part, 4 * part + 4):
                        pe.wait_ge(lo_ready, SLABS * (G0["pc"] + s) + q + 1)
                        if s == 0:
                            pe.wait_ge(S["xs_ready"], XS["pc"] + q // 2 + 1)
                        for kk in range(2):
                            for b in range(4):
                                c = slice(b * P, (b + 1) * P)
                                o = ps[:, b0 + 2 * part + b // 2, (b % 2) * T:(b % 2 + 1) * T]
                                three(o, whi[:, q % RING, kk, c], wlo[:, q % RING, kk, c], ahi[:, 2 * q + kk, 0:T], alo[:, 2 * q + kk, 0:T],
                                      first=q == 4 * part and kk == 0 and b % 2 == 0, last=q == 4 * part + 3 and kk == 1,
                                      sig=slab_used if kk == 1 and b == 3 else None)
            for s in range(4):
                if s < 2:
                    pe.wait_ge(acc_dve, ACC_DVE["pc"] + 3)
                else:
                    pe.wait_ge(acc_act, ACC_ACT["wo"] + s - 1)
                wm_group(G0["wo"] + s, [bank(2 * (s % 2)), bank(2 * (s % 2) + 1)], ahi, alo, x_ready=four_each("m") if s == 0 else None)
            turn(2, XS["u2"], src)

            for half in range(2):
                up, down = f"up{half}", f"down{half}"
                if half:
                    pe.wait_ge(acc_dve, ACC_DVE["down1"] - 1)
                with pe.Fori(0, 4) as i:
                    for s in range(2):
                        if half and s:
                            pe.wait_ge(acc_dve, ACC_DVE["down1"])
                        pe.wait_ge(acc_act, 2 * i + (ACC_ACT[up] + s - 1))
                        ws_group(2 * i + (G0[up] + s), packed(2 * s), T, ahi, alo, four_each("u2"))
                pe.wait_ge(acc_act, ACC_ACT[up] + 7)
                with pe.Fori(0, 2) as i:
                    for s in range(2):
                        if s:
                            pe.wait_ge(acc_act, ACC_ACT[up] + 8)
                        pe.wait_ge(acc_dve, 2 * i + (ACC_DVE[down] + s - 1))
                        for part in range(2):
                            wm_group(4 * i + (G0[down] + 2 * s + part), [bank(2 * s), bank(2 * s + 1)], fhi, flo, first=part == 0, last=part == 1,
                                     x_ready=lambda k: 8 * half + k // 4 + 1, k0=KT * part, ready=S["f_ready"])

        @block.scalar
        def _(act):
            a = nc.scalar.activation
            st = Steps(act, S["act_step"])
            sig = {k: Signal(v) for k, v in S.items()}

            act.wait_ge(S["params_loaded"], 32)
            act.wait_ge(S["lora_z"], KT)
            st.do(a(hw[0][0:LORA, :], ps[0:LORA, 6, 0:T], ACT.Tanh), sig["lora_h"])
            act.wait_ge(S["lora_z"], 2 * KT)
            st.do(a(hw[1][0:LORA, :], ps[0:LORA, 7, 0:T], ACT.Copy), sig["lora_h"])
            def build_hook(stage):
                def hook(u):
                    if stage < 3:
                        act.wait_ge(S["xa_tmp"], SLABS * stage + u + 1)
                    else:
                        act.wait_ge(S[f"gx_loaded{u % 2}"], 16 * (u // 2 + 1))
                    st.do(a(ahi[:, 2 * u:2 * u + 2, 0:T], xtmp(u), ACT.Copy), sig["xa_hi"])
                return hook

            build_first = build_hook(0)
            for u in range(SLABS):
                for n_ in range(4 * u, 4 * u + 4):
                    i, j = divmod(n_, KT)
                    act.wait_ge(S["lora_zz"], 8 * i + j // 2 + 1)
                    o = KR[:, j, 0, :] if i == 0 else Bc[:, j, :]
                    st.do(a(o, ps[:, (8 * i + j // 2) % 4, (j % 2) * T:(j % 2 + 1) * T], ACT.Sigmoid,
                            bias=ve("w0" if i == 0 else "a0", j)), sig["lora_s1"])
                if u < RING:
                    split_hi(act, 0, u)
                build_first(u)
            for s in range(4):
                G = G0["k"] + s
                group_slabs(act, split_hi, G, build_hook(1) if s == 3 else None)
                act.wait_ge(slab_used, SLABS * (G + 1))
                if s:
                    act.wait_ge(S["acc_free_dve"], s)
                    act.wait_ge(S["ss_done"], s)
                else:
                    act.wait_ge(S["dec_done"], 2)
                    st.do(a(gC[:], KR[:, :, 1, CH - 1::CH], ACT.Exp, scale=-DECAY))
                kp = ps[:, 2 * (s % 2):2 * (s % 2) + 2, :].rearrange("p b (c t) -> p (b c) t", c=2)
                for b in range(4):
                    st.do(a(tmpA[0][:, b * T:(b + 1) * T], kp[:, b, :], ACT.Copy, scale=ve("k_k", 4 * s + b)),
                          sig["kk_copied"] if b == 3 else None)
                st.do(a(tmpA[2].rearrange("p (b t) -> p b t", b=4), KR[:, 4 * s:4 * s + 4, 1, :], ACT.Exp, scale=DECAY))
                st.do(a(KR[:, 4 * s:4 * s + 4, 0, :], KR[:, 4 * s:4 * s + 4, 0, :], ACT.Exp, scale=-DECAY), sig["kk_ready"])
                st.prev(3)
                st.do(a(tmpA[1], tmpA[0], ACT.Square), sig["sq_ready"])
            for s in range(4):
                G = G0["r"] + s
                group_slabs(act, split_hi, G, build_hook(2) if s == 3 else None)
                if s == 0:
                    act.wait_ge(S["ss_done"], 4)
                    st.do(a(small[:, 0:64], ps[:, 6, 0:64], ACT.Sqrt), sig["rn_ready"])
                act.wait_ge(S["dec_done"], 2)
                st.do(a(KR[:, 4 * s:4 * s + 4, 1, :], KR[:, 4 * s:4 * s + 4, 1, :], ACT.Exp, scale=-DECAY), sig["gi_ready"])
            def bonus_store(s):
                act.wait_ge(S["bvs_ready"], s + 1)
                act.dma_start(bonus_dram[:, 4 * s:4 * s + 4, :], vtmp[2 + s % 2].rearrange("p (b t) -> p b t", b=4)).then_inc(S[f"bv_stored{s % 2}"], 16)
            for s in range(4):
                G = G0["v"] + s
                group_slabs(act, split_hi, G, build_hook(3) if s == 3 else None)
                act.wait_ge(slab_used, SLABS * (G + 1))
                if s == 0:
                    act.wait_ge(S["prep_done"], 1)
                else:
                    bonus_store(s - 1)
                b0 = 2 * (s % 2)
                if s == 0:
                    act.wait_ge(S["gx_stored0"], 64)
                st.do(a(vtmp[0], bank(b0, 2), ACT.Copy), sig["acc_act"])
                act.wait_ge(S["vt_mm"], s + 1)
                st.do(a(V[:, :, 4 * s:4 * s + 4, :], ps[:, 4:6, :].rearrange("p b (j c n) -> p c (b j) n", j=2, c=4), ACT.Copy),
                      sig["v_ready"])
            def level(kind, c, f, lv):
                if kind == "y" and lv:
                    n_ = (c * 6 + lv) * 2 + f
                    if n_ < 4:
                        act.wait_ge(S["bv_stored1"], 32)
                    act.wait_ge(S["lv_y"], n_ + 1)
                    act.wait_ge(S["lv_t"], n_ - 1)
                    st.do(a(Yl[:, f * GW:(f + 1) * GW], bank(4 + f), ACT.Copy), sig["lv_ysb"])
            for s in range(4):
                G = G0["g"] + s
                group_slabs(act, split_hi, G, lambda u, s=s: (bonus_store(3) if (s, u) == (0, 3) else None, beside(16 * s + 2 * u, level)))
                act.wait_ge(slab_used, SLABS * (G + 1))
                if s == 0:
                    act.wait_ge(S["xs_ready"], XS["z"])
                else:
                    act.wait_ge(S["gate_stored"], 16 * s)
                st.do(a(gate, bank(2 * (s % 2), 2), ACT.Silu), sig["silu_ready"])
                act.wait_ge(S["silu_ready"], s + 1)
                act.dma_start(gate_dram[:, 4 * s:4 * s + 4, :], gate.rearrange("p (b t) -> p b t", b=4)).then_inc(S["gate_stored"], 16)
            for e in steps_at[-1]:
                level(*e)
            def gn_sqrt(i, h0=0, h1=16):
                act.wait_ge(S["gn_var"], i + 1)
                if i == 4:
                    act.wait_ge(S["yn_ready"], 4)
                st.do(a(small[:, 176 + h0:176 + h1], small[:, 160 + h0:160 + h1], ACT.Sqrt), sig["gn_std"])
            for it in range(4):
                for u in range(4 if it < 3 else 0):
                    act.wait_ge(S["tok_mm"], 4 * it + u + 1)
                    if it:
                        act.wait_ge(S["m_mm"], 2 * it)
                    st.do(a(BKt[:, u // 2, (u % 2) * GW:(u % 2 + 1) * GW], bank(u), ACT.Copy), sig["tok_ready"])
                for f in range(2):
                    act.wait_ge(S["w_mm"], 2 * it + f + 1)
                    st.do(a(Wt[:, f * GW:(f + 1) * GW], bank(f), ACT.Copy), sig["w_sb"])
                if it:
                    gn_sqrt(it - 1)
                for f in range(2):
                    act.wait_ge(S["u_mm"], 2 * it + f + 1)
                    st.do(a(U[:, f * GW:(f + 1) * GW], bank(2 + f), ACT.Copy, scale=-1.0), sig["u_sb"])
                for f in range(2):
                    act.wait_ge(S["y_mm"], 2 * it + f + 1)
                    st.do(a(Yn[:, it, f * GW:(f + 1) * GW], bank(4 + f), ACT.Copy), sig["y_sb"])
            gn_sqrt(3, 0, 8)
            gn_sqrt(4, 8, 16)
            def z_hi(j2):
                act.wait_ge(S["z_f"], j2 + 1)
                st.do(a(ahi[:, 2 * j2:2 * j2 + 2, 0:T], zt[2 + j2 % 2].rearrange("p (b t) -> p b t", b=2), ACT.Copy), sig["z_hi"])
            for j2 in range(8):
                act.wait_ge(S["zt_mm"], j2 + 1)
                if j2 >= 2:
                    act.wait_ge(S["z_f"], j2 - 1)
                for b in range(2):
                    st.do(a(zt[j2 % 2][:, b * T:(b + 1) * T], ps[:, 4 + j2 % 4, b * T:(b + 1) * T], ACT.Identity,
                            bias=ve("gn_b", 2 * j2 + b), scale=ve("gn_g", 2 * j2 + b)), sig["z1_ready"] if b else None)
                if j2:
                    z_hi(j2 - 1)
            z_hi(7)
            def ln_norm(i, c):
                cols = slice(c * GW, (c + 1) * GW)
                for tb in range(2):
                    st.do(a(H[:, tb, cols], H[:, tb, cols], ACT.Identity, bias=nbias[:, tb:tb + 1], scale=rstd[:, tb:tb + 1]),
                          sig["ln_normed"] if tb else None)

            def ln_sqrt(i):
                act.wait_ge(S["ln_var"], i + 1)
                st.do(a(small[:, 244:246], mv[:, :, 1], ACT.Sqrt), sig["ln_std"])
                act.wait_ge(S["ln_scale"], i + 1)
                ln_norm(i, 0)
                ln_norm(i, 1)

            def turned_hi(i, c):
                act.wait_ge(S["turn_mm"], 4 * i + c + 1)
                st.do(a(ahi[:, 4 * c:4 * c + 4, 0:T], ps[:, 4 + 2 * (c % 2):6 + 2 * (c % 2), :].rearrange("p b (k t) -> p (b k) t", k=2),
                        ACT.Copy), sig["turn_hi"])
            for s in range(4):
                group_slabs(act, split_hi, G0["wout"] + s, slabs=SLABS if s < 3 else SLABS - 1)
            ln_sqrt(0)
            for c in range(4):
                if c < 2:
                    ln_norm(0, c + 2)
                if c == 0:
                    split_hi(act, G0["ks"], RING - 1)
                turned_hi(0, c)

            def evac_stage(name, n, evac, hook=None):
                for s in range(n):
                    G = G0[name] + s
                    group_slabs(act, split_hi, G, (lambda u, s=s: hook(8 * s + u)) if hook else None)
                    act.wait_ge(slab_used, SLABS * (G + 1))
                    evac(s)
            two = lambda s: ps[:, 2 * (s % 2):2 * (s % 2) + 2, :]
            tiles = lambda s: ps[:, 2 * (s % 2):2 * (s % 2) + 2, :].rearrange("p b (c t) -> p (b c) t", c=2)
            evac_stage("ks", 4, lambda s: st.do(a(kT[:, 4 * s:4 * s + 4, :], tiles(s), ACT.Copy), sig["acc_act"]))
            evac_stage("vs", 4, lambda s: st.do(a(vS[:, :, s * GW:(s + 1) * GW], two(s), ACT.Copy), sig["acc_act"]))
            act.wait_ge(S["lam_ready"], 1)
            st.do(a(lexp, lsum, ACT.Exp), sig["lam_exp"])

            scale = DH ** -0.5
            def att(t):
                for h in range(AH):
                    if t == FIRST_HEAD + PER * h + 10:
                        act.wait_ge(S["ot_mm"], h + 1)
                        for e in range(2):
                            st.do(a(qT[:, 2 * h + e, :], ps[:, 7, e * T:(e + 1) * T], ACT.Copy, scale=sub1[:, e:e + 1]),
                                  sig["ot_ready"] if e else None)
                    if t == FIRST_HEAD + PER * h + 7:
                        act.wait_ge(S["o_mm"], h + 1)
                        act.wait_ge(S["lam_done"], 1)
                        for i in range(2):
                            if h or i:
                                st.prev()
                            st.do(a(osq, ps[:, 7, i * T:(i + 1) * T], ACT.Square, accum_out=oss[:, i:i + 1]))
                        st.prev()
                        if h:
                            act.wait_ge(S["on_ready"], h)
                        st.do(a(ostd, oss, ACT.Sqrt, bias=eps5, scale=1.0 / (2 * DH)), sig["ostd_ready"])
                    if t == FIRST_HEAD + PER * h + 5:
                        act.wait_ge(S["att_mm"], h + 1)
                        if h:
                            act.wait_ge(S["o_mm"], h)
                        st.do(a(attT, ps[:, 6, 0:384], ACT.Copy), sig["attT_ready"])
                    if t == FIRST_HEAD + PER * h + 1:
                        act.wait_ge(S["sc_ready"], h + 1)
                        if h:
                            act.wait_ge(S["at_ready"], h)
                        for i, cols in ((0, slice(0, T)), (1, slice(T, T + P))):
                            for m in range(2):
                                n_ = 2 * i + m
                                st.do(a(es[:, m, cols], sc[:, m, cols], ACT.Exp, bias=nmx[:, n_:n_ + 1], scale=scale,
                                        accum_out=rsum[:, n_:n_ + 1]), sig["e_ready"] if n_ == 3 else None)
            evac_stage("q", 4, lambda s: st.do(a(qT[:, 4 * s:4 * s + 4, :], tiles(s), ACT.Copy), sig["acc_act"]), att)
            def four_hi(src_, k0, c, ready, n, done):
                act.wait_ge(ready, n)
                st.do(a(ahi[:, k0 + 4 * c:k0 + 4 * c + 4, 0:T], src_, ACT.Copy), done)
            def gb_evac(s):
                if s == 3:
                    for c in range(2):
                        four_hi(qT[:, 4 * c:4 * c + 4, :], 0, c, S["zb_ready"], c + 1, sig["zb_hi"])
                st.do(a(gbT[:, 4 * s:4 * s + 4, :], tiles(s), ACT.Silu), sig["acc_act"])
            evac_stage("gb", 4, gb_evac, lambda t: att(32 + t))
            for c in (2, 3):
                four_hi(qT[:, 4 * c:4 * c + 4, :], 0, c, S["zb_ready"], c + 1, sig["zb_hi"])


            def meta_norm():
                act.wait_ge(S["meta_loaded"], 32)
                st.do(a(metaS, rowsB[0:META, 1, :], ACT.Square, accum_out=mss[0:META]))
                st.prev()
                st.do(a(mstd[0:META], mss[0:META], ACT.Sqrt, bias=eps6[0:META], scale=1.0 / C), sig["meta_ssq"])
            def meta_turned():
                act.wait_ge(S["meta_f"], 1)
                st.do(a(ahi[:, :, T:TM], metaU, ACT.Copy), sig["meta_hi"])
            for s in range(4):
                group_slabs(act, split_hi, G0["bout"] + s, slabs=SLABS if s < 3 else SLABS - 1)
                if s == 0:
                    meta_norm()
                if s == 2:
                    meta_turned()

            def squares(n, cols_ready, base, then=None):
                for c in range(4):
                    act.wait_ge(cols_ready, base + c + 1)
                    for tb in range(2):
                        st.prev()
                        st.do(a(junk[:, 0:GW], src_of(n)[:, tb, c * GW:(c + 1) * GW], ACT.Square, accum_out=ssr[:, tb, c:c + 1]),
                              sig["ssq"] if c == 3 and tb else None)
                    if then:
                        then(c)

            def src_of(n):
                return yS if n == 3 else H

            def rms_sqrt(n):
                act.wait_ge(S["ssum"], n + 1)
                st.do(a(rstd_, rsm, ACT.Sqrt, bias=eps6, scale=1.0 / C), sig["sstd"])

            ln_sqrt(1)
            squares(0, S["x2_cols"], 0, lambda c: ln_norm(1, c + 2) if c < 2 else None)
            rms_sqrt(0)
            split_hi(act, G0["cv"], RING - 1)
            for c in range(4):
                turned_hi(1, c)

            def wide_evac(dst, p, fn, last):
                st.do(a(dst[:, :, META:TM], ps[:, 4 * p:4 * p + 4, 0:T], fn))
                st.do(a(dst[:, :, 0:META], ps[:, 4 * p:4 * p + 4, T:TM], fn), last)
            def cv_evac(s):
                if s < 2:
                    wide_evac(A2[:, 4 * s:4 * s + 4, PAD:], s % 2, ACT.Copy, sig["acc_act"])
                else:
                    if s == 3:
                        act.wait_ge(S["cv_a"], 1)
                    wide_evac(ctmp, s % 2, ACT.Sigmoid, sig["acc_act"])
            evac_stage("cv", 4, cv_evac)
            evac_stage("pool", 2, lambda s: wide_evac(pz[:, 4 * s:4 * s + 4, :], s % 2, ACT.Copy, sig["acc_act"]))

            def gates_evac(s):
                if s == 7:
                    four_hi(pz[:, 0:4, META:TM], 0, 0, S["pool_y"], 4, sig["p_hi"])
                dst = (sa, sgb)[s // 4]
                st.do(a(dst[:, 4 * (s % 4):4 * (s % 4) + 4, :], tiles(s), ACT.Sigmoid), sig["acc_act"])
                if s == 3:
                    act.wait_ge(S["pool_mm"], 1)
                    for j in range(8):
                        st.do(a(pz[:, j, META:TM], ps[:, 4 + j // 2, (j % 2) * T:(j % 2 + 1) * T], ACT.Copy, scale=ve("pool_scale", j)),
                              sig["pool_y"] if j % 2 else None)
            def conv_norm(t):
                t -= 48
                if t == 4:
                    act.wait_ge(S["cs_mm"], 1)
                    st.do(a(cmean, ps[:, 6, 0:T], ACT.Copy, scale=1.0 / 1024), sig["cvar"])
                if t in (6, 7, 8, 9):
                    u = t - 6
                    act.wait_ge(S["xc_ready"], u // 2 + 1)
                    if u >= 2:
                        act.wait_ge(S["cv_mm"], u - 1)
                    st.do(a(csq[u % 2], cc[:, 2 * u:2 * u + 2, :], ACT.Square), sig["sqc_ready"])
                if t == 10:
                    act.wait_ge(S["cv_mm"], 4)
                    st.do(a(crstd, ps[:, 7, 0:T], ACT.Sqrt, bias=eps5, scale=1.0 / 1024), sig["cstd"])
                if t in (13, 14):
                    c = t - 13
                    act.wait_ge(S["cn_ready"], c + 1)
                    for j in range(4 * c, 4 * c + 4):
                        st.do(a(cc[:, j, :], cc[:, j, :], ACT.Silu, bias=ve("conv_b", j), scale=ve("conv_g", j)), sig["conv_y"] if j % 4 == 3 else None)

            evac_stage("gates", 8, gates_evac, conv_norm)
            four_hi(pz[:, 4:8, META:TM], 0, 1, S["pool_y"], 4, sig["p_hi"])
            for c in range(2):
                four_hi(cc[:, 4 * c:4 * c + 4, :], 8, c, S["conv_y"], c + 1, sig["c_hi"])
            for s in range(4):
                group_slabs(act, split_hi, G0["pc"] + s)
            for c in range(4):
                four_hi(mT[:, 4 * c:4 * c + 4, :], 0, c, S["m_ready"], c + 1, sig["m_hi"])
            def wo_evac(s):
                cols = slice(s * GW, (s + 1) * GW)
                for tb in range(2):
                    if s or tb:
                        st.prev()
                    st.do(a(junk[:, 0:GW], bank(2 * (s % 2) + tb), ACT.Square, accum_out=ssr[:, tb, s:s + 1]))
                st.do(a(yS[:, :, cols], two(s), ACT.Copy), sig["acc_act"])
            evac_stage("wo", 4, wo_evac)
            rms_sqrt(1)
            squares(2, S["y2_cols"], 0)
            rms_sqrt(2)
            for c in range(4):
                turned_hi(2, c)

            def up_evac(half, s):
                if half or s >= 2:
                    act.wait_ge(S["f_sq"], 8 * half + s - 1)
                st.do(a(frel[s % 2], bank(2 * (s % 2), 2), ACT.Relu), sig["acc_act"])
                st.prev()
                st.do(a(fhi[:, 4 * s:4 * s + 4, :], frel[s % 2].rearrange("p (b t) -> p b t", b=4), ACT.Square), sig["f_hi"])
            for half in range(2):
                evac_stage(f"up{half}", 8, lambda s: up_evac(half, s))
                for s in range(8):
                    group_slabs(act, split_hi, G0[f"down{half}"] + s)
            squares(3, S["acc_dve"], ACC_DVE["down1"])
            rms_sqrt(3)

        @block.vector
        def _(dve):
            tt, ts_, stt = nc.vector.tensor_tensor, nc.vector.tensor_scalar, nc.vector.scalar_tensor_tensor
            st = Steps(dve, S["dve_step"])
            sig = {k: Signal(v) for k, v in S.items()}
            dve.wait_ge(S["params_loaded"], 32)
            ka1 = small[:, 128:144]
            st.do(ts_(ka1, ve("k_a"), -1.0, 1.0, ALU.mult, ALU.add))
            for i, mu in enumerate(("mu_w", "mu_a")):
                for k in range(KT):
                    if i == 0 and k % 4 == 0:
                        dve.wait_ge(S[f"x_loaded{k // 4}"], 32)
                        k4 = slice(k, k + 4)
                        st.do(tt(xx[:, k4, :], xx[:, k4, :], xT[:, k4, :], ALU.subtract), sig["xx_ready"])
                        st.prev()
                    n_ = KT * i + k
                    if n_ >= 4:
                        dve.wait_ge(S["lora_z"], n_ - 3)
                    st.do(stt(xa[n_ % 4], xx[:, k, :], ve(mu, k), xT[:, k, :], ALU.mult, ALU.add), sig["xa_ready"])
            def build_hook(stage):
                def hook(u):
                    k2 = slice(2 * u, 2 * u + 2)
                    dve.wait_ge(S["xa_hi"], SLABS * stage + u + 1)
                    st.do(tt(alo[:, k2, 0:T], xtmp(u), ahi[:, k2, 0:T].bitcast(F32), ALU.subtract), sig["xs_ready"])
                return hook

            first = build_hook(0)
            for u in range(SLABS):
                if u < RING:
                    split_lo(dve, 0, u)
                first(u)
            for j in range(KT):
                dve.wait_ge(S["lora_s1"], j + 1)
                if j == KT - 2:
                    dve.wait_ge(S["lora_zz"], 16)
                st.do(nc.vector.tensor_tensor_scan(KR[:, j, 1, :], cs("restart"), KR[:, j, 0, :], 0.0, ALU.mult, ALU.add),
                      sig["dec_done"] if j == KT - 1 else None)
            st.prev()
            st.do(tt(KR[:, :, 0, :], KR[:, :, 1, :], KR[:, :, 0, :], ALU.subtract), sig["dec_done"])
            KP = tmpA[3]
            for s in range(4):
                G = G0["k"] + s
                group_slabs(dve, split_lo, G, build_hook(1) if s == 3 else None)
                dve.wait_ge(slab_used, SLABS * (G + 1))
                j4 = slice(4 * s, 4 * s + 4)
                four = lambda t_: t_.rearrange("p (b t) -> p b t", b=4)
                kp = bank(2 * (s % 2), 2)
                for b in range(4):
                    st.do(ts_(KP[:, b * T:(b + 1) * T], Bc[:, 4 * s + b, :], ve("k_a", 4 * s + b), ka1[:, 4 * s + b:4 * s + b + 1],
                              ALU.mult, ALU.add))
                st.prev()
                dve.wait_ge(S["kk_copied"], s + 1)
                st.do(tt(KP, KP, kp, ALU.mult))
                dve.wait_ge(S["kk_ready"], s + 1)
                st.do(tt(KR[:, j4, 0, :], KR[:, j4, 0, :], four(tmpA[0]), ALU.mult))
                st.do(tt(Bc[:, j4, :], Bc[:, j4, :], four(tmpA[0]), ALU.mult))
                st.prev(3)
                st.do(tt(Kc[:, j4, :], four(KP), four(tmpA[2]), ALU.mult))
                st.prev(2)
                st.do(tt(Bc[:, j4, :], Bc[:, j4, :], four(tmpA[2]), ALU.mult), sig["acc_free_dve"])
            rn = small[:, 0:64].rearrange("p (b h) -> p b h", b=2)
            for s in range(4):
                G = G0["r"] + s
                group_slabs(dve, split_lo, G, build_hook(2) if s == 3 else None)
                if s == 0:
                    dve.wait_ge(S["rn_ready"], 1)
                    st.do(ts_(small[:, 0:64], small[:, 0:64], 1e-12, None, ALU.max))
                    st.prev()
                    st.do(nc.vector.reciprocal(small[:, 0:64], small[:, 0:64]))
                    st.prev()
                else:
                    dve.wait_ge(S["rnx_bc"], s)
                st.do(nc.vector.tensor_copy(tmpA[0].rearrange("p (b h n) -> p b h n", b=2, h=8),
                                            rn[:, :, 8 * s:8 * s + 8].unsqueeze(3).broadcast_to([P, 2, 8, N])), sig["rnx_ready"])
                j4 = slice(4 * s, 4 * s + 4)
                four = lambda t_: t_.rearrange("p (b t) -> p b t", b=4)
                dve.wait_ge(slab_used, SLABS * (G + 1))
                dve.wait_ge(S["gi_ready"], s + 1)
                st.do(tt(KR[:, j4, 1, :], KR[:, j4, 1, :], ps[:, 2 * (s % 2):2 * (s % 2) + 2, :].rearrange("p b (c t) -> p (b c) t", c=2), ALU.mult),
                      sig["acc_free_dve"])
                dve.wait_ge(S["rnx_bc"], s + 1)
                bcst = ps[:, 4:6, :].rearrange("p b (c t) -> p (b c) t", c=2)
                st.do(tt(KR[:, j4, 0, :], KR[:, j4, 0, :], bcst, ALU.mult))
                st.do(tt(Bc[:, j4, :], Bc[:, j4, :], bcst, ALU.mult), sig["prep_done"] if s == 3 else None)
            def bonus(s):
                dve.wait_ge(S["rk_bc"], s + 1)
                dve.wait_ge(S["acc_act"], s + 1)
                if s >= 2:
                    dve.wait_ge(S[f"bv_stored{s % 2}"], 16)
                st.do(tt(vtmp[2 + s % 2], vtmp[0], bank(6, 2), ALU.mult), sig["bvs_ready"])

            def v_hook(s):
                lows = build_hook(3)
                def hook(u):
                    if s and u == 3:
                        bonus(s - 1)
                    if s == 3:
                        lows(u)
                return hook
            for s in range(4):
                group_slabs(dve, split_lo, G0["v"] + s, v_hook(s))
                if s:
                    dve.wait_ge(S["rk_bc"], s)
                for b in range(4):
                    st.do(stt(vtmp[1][:, b * T:(b + 1) * T], Kc[:, 4 * s + b, :], ve("r_k", 4 * s + b), KR[:, 4 * s + b, 1, :],
                              ALU.mult, ALU.mult), sig["rk_ready"] if b == 3 else None)
            def heads(t_, h=16):
                return t_.rearrange("p (h n) -> p h n", h=h)
            gsums, gvars, gstd = small[:, 144:160], small[:, 160:176], small[:, 176:192]

            def y_of(i):
                return heads(Yn[:, i, :])

            def gn_part1(i, n_=0, f=None):
                dve.wait_ge(S["y_sb"], 2 * i + (2 if f is None else f + 1))
                st.prev()
                hs_ = slice(0, 16) if f is None else slice(8 * f, 8 * f + 8)
                nh = 16 if f is None else 8
                y, gsum, gvar, sq = y_of(i)[:, hs_, :], gsums[:, hs_], gvars[:, hs_], heads(gsq)[:, hs_, :]
                st.do(nc.vector.tensor_reduce(gsum, y, AX.X, ALU.add))
                st.prev()
                st.do(ts_(gsum, gsum, 1.0 / N, None, ALU.mult))
                st.prev()
                st.do(tt(y, y, gsum.unsqueeze(2).broadcast_to([P, nh, N]), ALU.subtract))
                st.prev()
                st.do(tt(sq, y, y, ALU.mult))
                st.prev()
                if i:
                    dve.wait_ge(S["gn_std"], i + n_)
                st.do(nc.vector.tensor_reduce(gvar, sq, AX.X, ALU.add))
                st.prev()
                st.do(ts_(gvar, gvar, 1.0 / N, GN_EPS, ALU.mult, ALU.add), sig["gn_var"])

            def gn_part2(i, n_=0, f=None):
                dve.wait_ge(S["gn_std"], i + n_ + 1)
                hs_ = slice(0, 16) if f is None else slice(8 * f, 8 * f + 8)
                st.prev()
                st.do(nc.vector.reciprocal(gsums[:, hs_], gstd[:, hs_]))
                st.prev()
                st.do(tt(y_of(i)[:, hs_, :], y_of(i)[:, hs_, :], gsums[:, hs_].unsqueeze(2).broadcast_to([P, 16 if f is None else 8, N]), ALU.mult),
                      sig["yn_ready"])

            i8 = cs("ident64").unsqueeze(1).broadcast_to([P, 8, CH])

            def level(kind, c, f, lv):
                n_, m_ = (c * 6 + lv) * 2 + f, (c * 5 + lv - 1) * 2 + f
                fs = slice(f * GW, (f + 1) * GW)
                if kind == "ab":
                    dve.wait_ge(S["ab_mm"], 2 * c + f + 1)
                    if c == 0:
                        st.prev()
                    st.do(tt(heads(AB[:, fs], 8), heads(bank(4 + f), 8), cs("causal")[:, 0:CH].unsqueeze(1).broadcast_to([P, 8, CH]),
                             ALU.mult), sig["ab_ready"])
                if kind == "y" and lv == 0:
                    if c == 0 and f == 0:
                        dve.wait_ge(S["bv_stored0"], 32)
                    dve.wait_ge(S["lv_y"], n_ + 1)
                    st.do(tt(heads(Tm[:, fs], 8), i8, heads(bank(4 + f), 8), ALU.subtract))
                    st.do(tt(heads(TTs[:, c, fs], 8), i8, heads(Bm[:, fs], 8), ALU.subtract), sig["lv_t"])
                if kind == "zt":
                    dve.wait_ge(S["lv_z"], m_ + 1)
                    st.prev(3 if lv < 5 else 1)
                    if lv < 5:
                        st.do(tt(Tm[:, fs], Tm[:, fs], bank(6), ALU.subtract))
                    st.do(tt(TTs[:, c, fs], TTs[:, c, fs], bank(7), ALU.subtract), sig["lv_t"])
            for s in range(4):
                group_slabs(dve, split_lo, G0["g"] + s, lambda u, s=s: (bonus(3) if (s, u) == (0, 3) else None, beside(16 * s + 2 * u, level)))
            for e in steps_at[-1]:
                level(*e)
            for it in range(4):
                for u, (kind, n_, b) in enumerate((("K", 0, 2), ("K", 1, 3), ("B", 0, 0), ("B", 1, 1), ("K", 2, 2), ("K", 3, 3))):
                    dve.wait_ge(S["am_mm"], 6 * it + u + 1)
                    if kind == "K":
                        st.do(tt(AM[:, 4 * n_:4 * n_ + 4, 1:3, :].rearrange("p h a t -> p h (a t)"), ps[:, b, :].rearrange("p (h n) -> p h n", h=4),
                                 cs("causal").unsqueeze(1).broadcast_to([P, 4, 2 * CH]), ALU.mult), sig["am_ready"])
                    else:
                        st.do(tt(AM[:, 8 * n_:8 * n_ + 8, 0, :], heads(bank(b), 8), cs("causal")[:, CH:2 * CH].unsqueeze(1).broadcast_to([P, 8, CH]),
                                 ALU.mult), sig["am_ready"])
                if it:
                    gn_part1(it - 1)
                    gn_part2(it - 1)
                if it == 0:
                    dve.wait_ge(S["gate_stored"], 64)
                for f in range(2):
                    if it == 3:
                        break
                    dve.wait_ge(S["m_mm"], 2 * it + f + 1)
                    new, add = M[:, 8 * f:8 * f + 8, :], heads(bank(6 + f), 8)
                    if it:
                        st.do(tt(new, new, add, ALU.add))
                        st.prev()
                        add = new
                    st.do(tt(new, add, gC[:, 8 * f:8 * f + 8, it].unsqueeze(2).broadcast_to([P, 8, N]), ALU.mult), sig["m_sb"])
            gn_part1(3, 0, 0)
            gn_part2(3, 0, 0)
            gn_part1(3, 1, 1)
            gn_part2(3, 1, 1)
            dve.wait_ge(S["gate_loaded"], 16)
            dve.wait_ge(S["bv_loaded"], 16)
            def z_lo(j2):
                dve.wait_ge(S["z_hi"], j2 + 1)
                st.do(tt(alo[:, 2 * j2:2 * j2 + 2, 0:T], zt[2 + j2 % 2].rearrange("p (b t) -> p b t", b=2),
                         ahi[:, 2 * j2:2 * j2 + 2, 0:T].bitcast(F32), ALU.subtract), sig["xs_ready"])
            for j2 in range(8):
                dve.wait_ge(S["z1_ready"], j2 + 1)
                st.do(tt(zt[j2 % 2], zt[j2 % 2], bvT[:, 2 * j2:2 * j2 + 2, :].rearrange("p k t -> p (k t)"), ALU.add), sig["z_ready"])
                st.prev()
                st.do(tt(zt[2 + j2 % 2], zt[j2 % 2], gT[:, 2 * j2:2 * j2 + 2, :].rearrange("p k t -> p (k t)"), ALU.mult), sig["z_f"])
                if j2:
                    z_lo(j2 - 1)
            z_lo(7)
            stats = small[:, 192:240].rearrange("p (b s a) -> p b s a", b=2, s=4)

            def ln_evac(name, i, other, extra=None):
                for s in range(4):
                    group_slabs(dve, split_lo, G0[name] + s, slabs=SLABS if s < 3 else SLABS - 1)
                    if extra:
                        extra(s)
                    dve.wait_ge(slab_used, SLABS * (G0[name] + s + 1))
                    cols = slice(s * GW, (s + 1) * GW)
                    st.do(stt(H[:, :, cols], other[:, :, cols], ALPHA, ps[:, 2 * (s % 2):2 * (s % 2) + 2, :], ALU.mult, ALU.add),
                          sig["acc_dve"])
                    st.prev()
                    for tb in range(2):
                        st.do(nc.vector.bn_stats(stats[:, tb, s, :], H[:, tb, cols]))

            def turned_lo(i, c):
                dve.wait_ge(S["turn_hi"], 4 * i + c + 1)
                st.do(tt(alo[:, 4 * c:4 * c + 4, 0:T], ps[:, 4 + 2 * (c % 2):6 + 2 * (c % 2), :].rearrange("p b (k t) -> p (b k) t", k=2),
                         ahi[:, 4 * c:4 * c + 4, 0:T].bitcast(F32), ALU.subtract), sig["xs_ready"])

            def ln_dve(i):
                st.prev()
                for tb in range(2):
                    st.do(nc.vector.bn_aggr(mv[:, tb, :], stats[:, tb, :, :].rearrange("p s a -> p (s a)")))
                st.prev()
                st.do(ts_(mv[:, :, 1], mv[:, :, 1], LN_EPS, None, ALU.add), sig["ln_var"])
                dve.wait_ge(S["ln_std"], i + 1)
                st.do(nc.vector.reciprocal(rstd, small[:, 244:246]))
                st.prev()
                st.do(stt(nbias, mv[:, :, 0], -1.0, rstd, ALU.mult, ALU.mult), sig["ln_scale"])
                dve.wait_ge(S["row_loaded"], 32 * (i + 1))
                st.prev()
                for c in range(4):
                    cols = slice(c * GW, (c + 1) * GW)
                    dve.wait_ge(S["ln_normed"], 4 * i + c + 1)
                    for a_ in range(2):
                        st.do(tt(H[:, :, cols], H[:, :, cols], rows[:, a_, cols].unsqueeze(1).broadcast_to([P, 2, GW]),
                                 ALU.mult if a_ == 0 else ALU.add), None if a_ == 0 else sig["turn_src" if i == 0 else "x2_cols"])
                        if a_ == 0:
                            st.prev()
                    if c == 2 and i == 0:
                        split_lo(dve, G0["ks"], RING - 1)
                    if c and i == 0:
                        turned_lo(0, c - 1)
                if i == 0:
                    turned_lo(0, 3)
            dve.wait_ge(S["x_reloaded"], 16)
            ln_evac("wout", 0, xre)
            ln_dve(0)
            slabs = lambda name, n: [group_slabs(dve, split_lo, G0[name] + s) for s in range(n)]
            slabs("ks", 4)
            st.do(nc.vector.memset(eps5, 1e-5))
            st.do(nc.vector.memset(eps6, RMS_EPS))
            st.do(ts_(sub1, ve("subln"), 1.0 - LAM_INIT, None, ALU.mult))
            slabs("vs", 4)
            dve.wait_ge(S["extra_loaded"], 48)
            for i in range(2):
                st.do(tt(lam[:, 2 * i, :], lam[:, 2 * i, :], lam[:, 2 * i + 1, :], ALU.mult))
            st.prev()
            for i in range(2):
                st.do(nc.vector.tensor_reduce(lsum[:, i:i + 1], lam[:, 2 * i, :], AX.X, ALU.add), sig["lam_ready"] if i else None)
            dve.wait_ge(S["lam_exp"], 1)
            st.do(tt(nlam, lexp[:, 1:2], lexp[:, 0:1], ALU.subtract))
            st.prev()
            st.do(ts_(nlam, nlam, -LAM_INIT, None, ALU.add), sig["lam_done"])

            scale = DH ** -0.5
            def att(t):
                if t in (43, 51, 59):
                    zmul((t - 43) // 8)
                for h in range(AH):
                    if t == FIRST_HEAD + PER * h + 8:
                        dve.wait_ge(S["ostd_ready"], h + 1)
                        st.do(nc.vector.reciprocal(orstd, ostd))
                        if h:
                            dve.wait_ge(S["ot_mm"], h)
                        st.prev()
                        for i in range(2):
                            st.do(ts_(On[:, i * T:(i + 1) * T], ps[:, 7, i * T:(i + 1) * T], orstd[:, i:i + 1], None, ALU.mult),
                                  sig["on_ready"] if i else None)
                    if t == FIRST_HEAD + PER * h + 2:
                        dve.wait_ge(S["e_ready"], h + 1)
                        st.do(nc.vector.reciprocal(rrec, rsum))
                        st.prev()
                        st.do(ts_(rrec[:, 1:4:2], rrec[:, 1:4:2], nlam, None, ALU.mult))
                        st.prev()
                        both = ((0, slice(0, T)), (1, slice(T, T + P)))
                        for i, cols in both:
                            st.do(ts_(t1[:, cols], es[:, 1, cols], rrec[:, 2 * i + 1:2 * i + 2], None, ALU.mult))
                        if h:
                            dve.wait_ge(S["att_mm"], h)
                        st.prev()
                        for i, cols in both:
                            st.do(stt(attn[:, cols], es[:, 0, cols], rrec[:, 2 * i:2 * i + 1], t1[:, cols], ALU.mult, ALU.add),
                                  sig["at_ready"] if i else None)
                    if t == FIRST_HEAD + PER * h:
                        dve.wait_ge(S["sc_mm"], h + 1)
                        if h:
                            dve.wait_ge(S["e_ready"], h)
                        st.do(stt(sc, dist.unsqueeze(1).broadcast_to([P, 2, 384]), 2.0 ** -(h + 1) / scale, ps[:, 4:6, 0:384],
                                  ALU.mult, ALU.add), sig["sc_read"])
                        st.prev()
                        st.do(nc.vector.tensor_reduce(mx[:, 0:2], sc[:, :, 0:T], AX.X, ALU.max))
                        st.do(nc.vector.tensor_reduce(mx[:, 2:4], sc[:, :, T:T + P], AX.X, ALU.max))
                        st.prev()
                        st.do(ts_(nmx, mx, -scale, None, ALU.mult), sig["sc_ready"])

            def zmul(s):
                dve.wait_ge(S["acc_act"], ACC_ACT["gb"] + s + 1)
                dve.wait_ge(S["ot_ready"], 2 * s + 2)
                j4 = slice(4 * s, 4 * s + 4)
                st.do(tt(qT[:, j4, :], qT[:, j4, :], gbT[:, j4, :], ALU.mult), sig["zb_ready"])
            for s in range(8):
                group_slabs(dve, split_lo, G0["q"] + s, lambda u, s=s: att(8 * s + u))

            def four_lo(src_, k0, c, ready, n):
                dve.wait_ge(ready, n)
                ks_ = slice(k0 + 4 * c, k0 + 4 * c + 4)
                st.do(tt(alo[:, ks_, 0:T], src_, ahi[:, ks_, 0:T].bitcast(F32), ALU.subtract), sig["xs_ready"])
            for c in range(4):
                if c == 2:
                    zmul(3)
                four_lo(qT[:, 4 * c:4 * c + 4, :], 0, c, S["zb_hi"], c + 1)

            def meta(s):
                if s == 1:
                    dve.wait_ge(S["meta_ssq"], 1)
                    st.do(nc.vector.reciprocal(mrstd[0:META], mstd[0:META]))
                    st.prev()
                    st.do(stt(metaS, rowsB[0:META, 1, :], mrstd[0:META], rowsB[0:META, 0, :], ALU.mult, ALU.mult), sig["meta_src"])
                if s == 2:
                    dve.wait_ge(S["meta_mm"], 1)
                    st.do(nc.vector.tensor_copy(metaU, ps[:, 4, 0:KT * META].rearrange("p (k t) -> p k t", k=KT)), sig["meta_f"])
                if s == 3:
                    dve.wait_ge(S["meta_hi"], 1)
                    st.do(tt(alo[:, :, T:TM], metaU, ahi[:, :, T:TM].bitcast(F32), ALU.subtract), sig["meta_ready"])
            ln_evac("bout", 1, H, meta)
            ln_dve(1)

            def rms(n):
                dve.wait_ge(S["ssq"] if n != 1 else S["acc_act"], (1, ACC_ACT["up0"], 2, 3)[n])
                st.do(nc.vector.tensor_reduce(rsm, ssr, AX.X, ALU.add), sig["ssum"])
                dve.wait_ge(S["sstd"], n + 1)
                st.do(nc.vector.reciprocal(rrstd, rstd_))
                st.prev()

            def normed_turned(i, gain):
                for c in range(4):
                    cols = slice(c * GW, (c + 1) * GW)
                    for tb in range(2):
                        st.do(stt(src[:, tb, cols], H[:, tb, cols], rrstd[:, tb:tb + 1], gain[:, cols], ALU.mult, ALU.mult),
                              sig["turn_src"] if tb else None)
                    if c == 2 and i == 1:
                        split_lo(dve, G0["cv"], RING - 1)
                    if c:
                        turned_lo(i, c - 1)
                turned_lo(i, 3)
            rms(0)
            normed_turned(1, rowsB[:, 0, :])

            slabs("cv", 3)
            st.do(nc.vector.memset(A2[:, :, 0:PAD], 0.0))
            def cv_gate(s):
                dve.wait_ge(S["acc_act"], ACC_ACT["cv"] + 3 + s)
                x_ = A2[:, 4 * s:4 * s + 4, PAD:]
                st.do(tt(x_, x_, ctmp, ALU.mult), sig["cv_a"])
            cv_gate(0)

            conv_at = [0]
            def conv_steps(n, limit):
                for _ in range(n):
                    if conv_at[0] >= limit:
                        return
                    pair, tap = divmod(conv_at[0], TAPS)
                    for j in (2 * pair, 2 * pair + 1):
                        w_ = ve("w_dw")[:, j * TAPS + tap:j * TAPS + tap + 1]
                        x_ = A2[:, j, tap:tap + T]
                        if conv_at[0] or j % 2:
                            st.prev(1 if tap == 0 and j % 2 == 0 else 2)
                        if tap == 0:
                            st.do(ts_(cc[:, j, :], x_, w_, ve("b_dw", j), ALU.mult, ALU.add))
                        else:
                            st.do(stt(cc[:, j, :], x_, w_, cc[:, j, :], ALU.mult, ALU.add), sig["conv_c"] if tap == TAPS - 1 else None)
                    conv_at[0] += 1
            st.prev()
            group_slabs(dve, split_lo, G0["cv"] + 3, lambda u: conv_steps(2, 62))
            cv_gate(1)
            st.prev()
            for s in range(2):
                group_slabs(dve, split_lo, G0["pool"] + s, lambda u: conv_steps(2, 124))

            def pool_steps():
                dve.wait_ge(S["acc_act"], ACC_ACT["pool"] + 2)
                for g, w in enumerate(WINDOWS):
                    z, span, k = pz[:, 2 * g:2 * g + 2, :], 1, 0
                    cur = z
                    while span < w:
                        nxt = pt[k % 2]
                        st.do(tt(nxt[:, :, 2 * span - 1:], cur[:, :, 2 * span - 1:], cur[:, :, span - 1:TM - span], ALU.add))
                        yield
                        st.prev()
                        cur, span, k = nxt, 2 * span, k + 1
                    st.do(stt(z[:, :, META:], cur[:, :, META:], 1.0 / w, z[:, :, META:], ALU.mult, ALU.subtract),
                          sig["pool_d"] if g == 3 else None)
                    yield
                    st.prev()
            pool_work = pool_steps()

            def pools(u):
                for _ in range(2):
                    next(pool_work, None)

            def conv_norm(t):
                if t == 5:
                    dve.wait_ge(S["cvar"], 1)
                    st.do(tt(cc[:, 0:4, :], cc[:, 0:4, :], cmean.unsqueeze(1).broadcast_to([P, 4, T]), ALU.subtract), sig["xc_ready"])
                if t == 6:
                    st.do(tt(cc[:, 4:8, :], cc[:, 4:8, :], cmean.unsqueeze(1).broadcast_to([P, 4, T]), ALU.subtract), sig["xc_ready"])
                if t == 11:
                    dve.wait_ge(S["cstd"], 1)
                    st.do(nc.vector.reciprocal(crstd, crstd))
                if t in (12, 13):
                    c = t - 12
                    st.prev()
                    st.do(tt(cc[:, 4 * c:4 * c + 4, :], cc[:, 4 * c:4 * c + 4, :], crstd.unsqueeze(1).broadcast_to([P, 4, T]), ALU.mult),
                          sig["cn_ready"])
            for s in range(8):
                group_slabs(dve, split_lo, G0["gates"] + s, pools if s == 0 else (lambda u: conv_steps(2, 124)) if s < 6
                            else (lambda u, s=s: conv_norm(8 * (s - 6) + u)))
                if s == 5:
                    conv_steps(124, 124)
            for c in range(2):
                four_lo(pz[:, 4 * c:4 * c + 4, META:TM], 0, c, S["p_hi"], c + 1)
            for c in range(2):
                four_lo(cc[:, 4 * c:4 * c + 4, :], 8, c, S["c_hi"], c + 1)
            flat4 = lambda t_: t_.rearrange("p b t -> p (b t)")
            for s in range(4):
                group_slabs(dve, split_lo, G0["pc"] + s)
                dve.wait_ge(slab_used, SLABS * (G0["pc"] + s + 1))
                j4, b0 = slice(4 * s, 4 * s + 4), 4 * (s % 2)
                if s == 3:
                    for c in range(2):
                        four_lo(mT[:, 4 * c:4 * c + 4, :], 0, c, S["m_hi"], c + 1)
                if s:
                    st.prev()
                st.do(tt(mtmp[0], flat4(sa[:, j4, :]), bank(b0, 2), ALU.mult))
                st.do(tt(mtmp[1], flat4(sgb[:, j4, :]), bank(b0 + 2, 2), ALU.mult), sig["acc_dve"])
                st.prev()
                st.do(tt(flat4(mT[:, j4, :]), mtmp[0], mtmp[1], ALU.add), sig["m_ready"])
            for c in (2, 3):
                four_lo(mT[:, 4 * c:4 * c + 4, :], 0, c, S["m_hi"], c + 1)
            slabs("wo", 4)

            def post(n, gain, done):
                for c in range(4):
                    cols = slice(c * GW, (c + 1) * GW)
                    for tb in range(2):
                        st.do(stt(yS[:, tb, cols], yS[:, tb, cols], rrstd[:, tb:tb + 1], gain[:, cols], ALU.mult, ALU.mult))
                    st.prev()
                    st.do(tt(H[:, :, cols], H[:, :, cols], yS[:, :, cols], ALU.add), done)
            rms(1)
            dve.wait_ge(S["post_loaded"], 32)
            post(1, rows[:, 0, :], sig["y2_cols"])
            rms(2)
            normed_turned(2, rows[:, 1, :])

            def f_lo(half, s):
                n_ = 8 * half + s
                dve.wait_ge(S["acc_act"], ACC_ACT[f"up{half}"] + s + 1)
                st.prev()
                st.do(tt(fsq, frel[s % 2], frel[s % 2], ALU.mult), sig["f_sq"])
                dve.wait_ge(S["f_hi"], n_ + 1)
                st.prev()
                st.do(tt(flo[:, 4 * s:4 * s + 4, :], fsq.rearrange("p (b t) -> p b t", b=4), fhi[:, 4 * s:4 * s + 4, :].bitcast(F32),
                         ALU.subtract), sig["f_ready"])
            for half in range(2):
                for s in range(8):
                    group_slabs(dve, split_lo, G0[f"up{half}"] + s)
                    f_lo(half, s)
                for s in range(4):
                    for part in range(2):
                        G = G0[f"down{half}"] + 2 * s + part
                        group_slabs(dve, split_lo, G)
                    dve.wait_ge(slab_used, SLABS * (G + 1))
                    y_ = yS[:, :, s * GW:(s + 1) * GW]
                    if half:
                        st.do(tt(y_, y_, ps[:, 2 * (s % 2):2 * (s % 2) + 2, :], ALU.add), sig["acc_dve"])
                    else:
                        st.do(nc.vector.tensor_copy(y_, ps[:, 2 * (s % 2):2 * (s % 2) + 2, :]), sig["acc_dve"])
            rms(3)
            dve.wait_ge(S["last_loaded"], 16)
            post(3, rows[:, 0, :], sig["out_cols"])


WEIGHTS = ["a_w_in", "a_w1", "a_a1", "a_w2", "a_a2", "a_w_out", "w_k_shared", "w_v_shared", "b_w_qg", "b_w_out", "b_lambda", "ln_g",
           "ln_b", "meta_2", "g_pre_mix_2", "w_in_2", "w_pool_grp_2", "w_pool_out_2", "w_conv_out_2", "w_o_2", "g_post_mix_2",
           "g_pre_mlp_2", "w_up_2", "w_down_2", "g_post_mlp_2"]


def layouts(inputs):
    def tiles(a):
        return np.asarray(a).reshape(-1, P).T
    x = np.asarray(inputs["x"])
    xT = np.zeros((P, KT, T + 1), x.dtype)
    xT[:, :, 1:] = x[0].T.reshape(KT, P, T).transpose(1, 0, 2)
    g = {k: np.asarray(v)[0] for k, v in inputs.items() if np.asarray(v).ndim > 1 and k != "meta_2"}
    v = {"mu_r": g["a_mu_proj"][0], "mu_k": g["a_mu_proj"][1], "mu_v": g["a_mu_proj"][2], "mu_g": g["a_mu_proj"][3],
         "mu_w": g["a_mu_lora"][0], "mu_a": g["a_mu_lora"][1], "w0": g["a_w0"], "a0": g["a_a0"], "k_k": g["a_k_k"],
         "k_a": g["a_k_a"], "r_k": g["a_r_k"], "gn_g": g["a_gn_g"], "gn_b": g["a_gn_b"], "subln": g["b_subln_g"],
         "g_pre_mix": g["g_pre_mix_2"], "g_pre_mlp": g["g_pre_mlp_2"], "pool_scale": g["pool_scale_2"], "b_dw": g["b_dw_2"],
         "conv_g": g["conv_ln_g_2"], "conv_b": g["conv_ln_b_2"]}
    packed = [tiles(v[n]) for n in VECTORS if n != "w_dw"]
    packed.append(g["w_dw_2"].reshape(TAPS, 8, P).transpose(2, 1, 0).reshape(P, 8 * TAPS))
    arrays = {"consts": CONSTANTS, "vectors": np.ascontiguousarray(np.concatenate(packed, 1)), "dist": distances(), "xT": xT, "x": x}
    return arrays


def kernel(**inputs):
    import concourse.bacc as _bacc
    from concourse.bass_utils import run_bass_kernel_spmd as _run

    nc = _bacc.Bacc("TRN2", target_bir_lowering=False, num_devices=1)
    arrays = {f"in_{n}": a for n, a in layouts(inputs).items()}
    for n in WEIGHTS:
        arrays[f"in_{n}"] = np.ascontiguousarray(inputs[n])
    ins = {n[3:]: nc.dram_tensor(n, a.shape, mybir.dt.from_np(a.dtype), kind="ExternalInput").ap() for n, a in arrays.items()}
    out = nc.dram_tensor("out", (1, T, C), F32, kind="ExternalOutput").ap()
    program(nc, ins, out)
    return _run(nc, [arrays], core_ids=[0]).results[0]["out"]
```
